# Optimizing a Trainium2 kernel written in Bass

```python
import jax, jax.numpy as jnp
from jax import lax
import numpy as np

D_MODEL = 1024
BATCH = 1
SEQ = 256
DEPTH = 2

CHUNK = 64
Q_BLOCK = 128
HEAD_DIM = 64
NORM_EPS = 1e-6
NEG_INF = -1e30
MLA_HEADS = 6
MLA_NOPE = 64
MLA_ROPE = 32
MLA_V = 64
Q_LORA = 256
KV_LORA = 128
ROPE_THETA = 10000.0
SB_HEADS = 5
FOX_HEADS = 5
N_BRANCH = 3
PEER_HEADS = 8
N_KEYS = 128
N_EXPERTS = N_KEYS * N_KEYS
D_KEY = 256
HALF_KEY = D_KEY // 2
PEER_TOPK = 16
PEER_BLOCK = 128

SB_W = SB_HEADS * HEAD_DIM
FOX_W = FOX_HEADS * HEAD_DIM
MLA_OUT = MLA_HEADS * MLA_V
MLA_QK = MLA_NOPE + MLA_ROPE
IN_SPLITS = (Q_LORA, KV_LORA, MLA_ROPE, SB_W, SB_W, SB_W, FOX_W, FOX_W, FOX_W, FOX_HEADS, N_BRANCH * D_MODEL)
D_IN = sum(IN_SPLITS)
IN_OFFSETS = tuple(int(o) for o in np.cumsum(IN_SPLITS)[:-1])

kernel_name = 'hybrid_mla_stickbreak_fox_peer'

def rmsnorm(x, g):
    xf = x.astype(jnp.float32)
    y = xf * lax.rsqrt(jnp.mean(xf * xf, axis=-1, keepdims=True) + NORM_EPS)
    return (y * g.astype(jnp.float32)).astype(x.dtype)

def rope_angles(pos):
    inv = ROPE_THETA ** (-jnp.arange(0, MLA_ROPE, 2, dtype=jnp.float32) / MLA_ROPE)
    ang = pos.astype(jnp.float32)[..., None] * inv
    return jnp.cos(ang), jnp.sin(ang)

def apply_rope(x, cos, sin):
    x1, x2 = jnp.split(x.astype(jnp.float32), 2, axis=-1)
    return jnp.concatenate([x1 * cos - x2 * sin, x1 * sin + x2 * cos], axis=-1).astype(x.dtype)

def to_blocks(a):
    b, s = a.shape[:2]
    a = a.reshape((b, s // Q_BLOCK, Q_BLOCK) + a.shape[2:])
    return jnp.moveaxis(a, 1, 0)

def from_blocks(a):
    a = jnp.moveaxis(a, 0, 1)
    return a.reshape((a.shape[0], a.shape[1] * a.shape[2]) + a.shape[3:])

def mla_branch(c_q, c_kv, k_rope_raw, pos, g_q, w_uq, g_kv, w_ukv):
    b, s, _ = c_q.shape
    q = (rmsnorm(c_q, g_q) @ w_uq).reshape(b, s, MLA_HEADS, MLA_QK)
    q_nope, q_rope = q[..., :MLA_NOPE], q[..., MLA_NOPE:]
    kv = (rmsnorm(c_kv, g_kv) @ w_ukv).reshape(b, s, MLA_HEADS, MLA_NOPE + MLA_V)
    k_nope, v = kv[..., :MLA_NOPE], kv[..., MLA_NOPE:]
    cos, sin = rope_angles(pos)
    q_rope = apply_rope(q_rope, cos[:, :, None], sin[:, :, None])
    k_rope = apply_rope(k_rope_raw, cos, sin)
    scale = MLA_QK ** -0.5
    key_chunk = jnp.arange(s) // CHUNK

    def block(args):
        qn, qr, i = args
        q_chunk = (i * Q_BLOCK + jnp.arange(Q_BLOCK)) // CHUNK
        logits = (jnp.einsum('bqhd,bkhd->bhqk', qn, k_nope)
                  + jnp.einsum('bqhr,bkr->bhqk', qr, k_rope)).astype(jnp.float32) * scale
        allowed = key_chunk[None, :] <= q_chunk[:, None]
        p = jax.nn.softmax(jnp.where(allowed, logits, NEG_INF), axis=-1)
        return jnp.einsum('bhqk,bkhd->bqhd', p.astype(v.dtype), v)

    o = lax.map(block, (to_blocks(q_nope), to_blocks(q_rope), jnp.arange(s // Q_BLOCK)))
    return from_blocks(o).reshape(b, s, MLA_OUT)

def stick_breaking_branch(q, k, v):
    b, s = q.shape[:2]
    scale = HEAD_DIM ** -0.5
    key_idx = jnp.arange(s)

    def block(args):
        qb, i = args
        q_idx = i * Q_BLOCK + jnp.arange(Q_BLOCK)
        z = jnp.einsum('bqhd,bkhd->bhqk', qb, k).astype(jnp.float32) * scale
        strict = key_idx[None, :] < q_idx[:, None]
        log_1m = jnp.where(strict, jax.nn.log_sigmoid(-z), 0.0)
        csum = jnp.cumsum(log_1m, axis=-1)
        log_a = jax.nn.log_sigmoid(z) + (csum[..., -1:] - csum)
        a = jnp.where(strict, jnp.exp(log_a), 0.0)
        return jnp.einsum('bhqk,bkhd->bqhd', a.astype(v.dtype), v)

    o = lax.map(block, (to_blocks(q), jnp.arange(s // Q_BLOCK)))
    return from_blocks(o).reshape(b, s, SB_W)

def forgetting_branch(q, k, v, f_raw, b_f):
    b, s = q.shape[:2]
    scale = HEAD_DIM ** -0.5
    key_idx = jnp.arange(s)
    log_f = jax.nn.log_sigmoid(f_raw.astype(jnp.float32) + b_f.astype(jnp.float32))
    cum_f = jnp.cumsum(log_f, axis=1)
    cum_k = jnp.transpose(cum_f, (0, 2, 1))

    def block(args):
        qb, fq, i = args
        q_idx = i * Q_BLOCK + jnp.arange(Q_BLOCK)
        logits = jnp.einsum('bqhd,bkhd->bhqk', qb, k).astype(jnp.float32) * scale
        decay = jnp.transpose(fq, (0, 2, 1))[..., :, None] - cum_k[:, :, None, :]
        causal = key_idx[None, :] <= q_idx[:, None]
        p = jax.nn.softmax(jnp.where(causal, logits + decay, NEG_INF), axis=-1)
        return jnp.einsum('bhqk,bkhd->bqhd', p.astype(v.dtype), v)

    o = lax.map(block, (to_blocks(q), to_blocks(cum_f), jnp.arange(s // Q_BLOCK)))
    return from_blocks(o).reshape(b, s, FOX_W)

def hybrid_mixer(h, pos, w_in, g_q, w_uq, g_kv, w_ukv, b_f, w_o_mla, w_o_sb, w_o_fox, b_gate, w_out):
    b, s, _ = h.shape
    z = h @ w_in
    (c_q, c_kv, k_r, q_sb, k_sb, v_sb, q_fx, k_fx, v_fx, f_raw, gate_raw) = jnp.split(z, IN_OFFSETS, axis=-1)
    sb_h = lambda a: a.reshape(b, s, SB_HEADS, HEAD_DIM)
    fx_h = lambda a: a.reshape(b, s, FOX_HEADS, HEAD_DIM)
    y_a = mla_branch(c_q, c_kv, k_r, pos, g_q, w_uq, g_kv, w_ukv) @ w_o_mla
    y_b = stick_breaking_branch(sb_h(q_sb), sb_h(k_sb), sb_h(v_sb)) @ w_o_sb
    y_c = forgetting_branch(fx_h(q_fx), fx_h(k_fx), fx_h(v_fx), f_raw, b_f) @ w_o_fox
    gates = jax.nn.sigmoid((gate_raw + b_gate).astype(jnp.float32)).astype(h.dtype)
    gates = gates.reshape(b, s, N_BRANCH, D_MODEL)
    y = gates[:, :, 0] * y_a + gates[:, :, 1] * y_b + gates[:, :, 2] * y_c
    return y @ w_out

def peer_ffn(h, w_q, sub_keys, u, v):
    b, s, d = h.shape
    t = b * s

    def block(xt):
        q = (xt @ w_q).reshape(PEER_BLOCK, PEER_HEADS, D_KEY)
        s1 = jnp.einsum('thc,nc->thn', q[..., :HALF_KEY], sub_keys[0])
        s2 = jnp.einsum('thc,nc->thn', q[..., HALF_KEY:], sub_keys[1])
        v1, i1 = lax.top_k(s1, PEER_TOPK)
        v2, i2 = lax.top_k(s2, PEER_TOPK)
        cand_s = (v1[..., :, None] + v2[..., None, :]).reshape(PEER_BLOCK, PEER_HEADS, PEER_TOPK * PEER_TOPK)
        cand_i = (i1[..., :, None] * N_KEYS + i2[..., None, :]).reshape(PEER_BLOCK, PEER_HEADS, PEER_TOPK * PEER_TOPK)
        top_s, sel = lax.top_k(cand_s, PEER_TOPK)
        e_idx = jnp.take_along_axis(cand_i, sel, axis=-1)
        g = jax.nn.softmax(top_s.astype(jnp.float32), axis=-1).astype(xt.dtype)
        u_e = jnp.take(u, e_idx, axis=0)
        v_e = jnp.take(v, e_idx, axis=0)
        act = jax.nn.gelu(jnp.einsum('thkd,td->thk', u_e, xt), approximate=False)
        return jnp.einsum('thk,thkd->td', g * act, v_e)

    out = lax.map(block, h.reshape(t // PEER_BLOCK, PEER_BLOCK, d))
    return out.reshape(b, s, d)

def setup_inputs(seed: int = 0) -> dict:
    key = jax.random.key(seed)
    ks = jax.random.split(key, 24)
    f32 = jnp.float32

    def w(k, shape, fan_in):
        return jax.random.normal(k, shape, f32) * (fan_in ** -0.5)

    def gain(k, shape):
        return 1.0 + 0.05 * jax.random.normal(k, shape, f32)

    L = DEPTH
    x = jax.random.normal(ks[0], (BATCH, SEQ, D_MODEL), f32)
    offs = jax.random.randint(ks[1], (BATCH, 1), 0, 64, dtype=jnp.int32) * CHUNK
    positions = (offs + jnp.arange(SEQ, dtype=jnp.int32)[None, :]).astype(jnp.int32)
    return {
        'x': x,
        'positions': positions,
        'norm1_g': gain(ks[2], (L, D_MODEL)),
        'w_in': w(ks[3], (L, D_MODEL, D_IN), D_MODEL),
        'mla_q_norm_g': gain(ks[4], (L, Q_LORA)),
        'w_uq': w(ks[5], (L, Q_LORA, MLA_HEADS * MLA_QK), Q_LORA),
        'mla_kv_norm_g': gain(ks[6], (L, KV_LORA)),
        'w_ukv': w(ks[7], (L, KV_LORA, MLA_HEADS * (MLA_NOPE + MLA_V)), KV_LORA),
        'fox_b_f': 3.0 + 1.0 * jax.random.normal(ks[8], (L, FOX_HEADS), f32),
        'w_o_mla': w(ks[9], (L, MLA_OUT, D_MODEL), MLA_OUT),
        'w_o_sb': w(ks[10], (L, SB_W, D_MODEL), SB_W),
        'w_o_fox': w(ks[11], (L, FOX_W, D_MODEL), FOX_W),
        'b_gate': 0.1 * jax.random.normal(ks[12], (L, N_BRANCH * D_MODEL), f32),
        'w_out': w(ks[13], (L, D_MODEL, D_MODEL), D_MODEL),
        'norm2_g': gain(ks[14], (L, D_MODEL)),
        'peer_w_q': w(ks[15], (L, D_MODEL, PEER_HEADS * D_KEY), D_MODEL),
        'peer_sub_keys': w(ks[16], (L, 2, N_KEYS, HALF_KEY), HALF_KEY),
        'peer_u': w(ks[17], (L, N_EXPERTS, D_MODEL), D_MODEL),
        'peer_v': w(ks[18], (L, N_EXPERTS, D_MODEL), PEER_HEADS),
        'final_norm_g': gain(ks[19], (D_MODEL,)),
    }

def reference(x, positions, norm1_g, w_in, mla_q_norm_g, w_uq, mla_kv_norm_g, w_ukv, fox_b_f,
              w_o_mla, w_o_sb, w_o_fox, b_gate, w_out, norm2_g, peer_w_q, peer_sub_keys,
              peer_u, peer_v, final_norm_g):
    for l in range(DEPTH):
        h = rmsnorm(x, norm1_g[l])
        x = x + hybrid_mixer(h, positions, w_in[l], mla_q_norm_g[l], w_uq[l], mla_kv_norm_g[l], w_ukv[l],
                             fox_b_f[l], w_o_mla[l], w_o_sb[l], w_o_fox[l], b_gate[l], w_out[l])
        h = rmsnorm(x, norm2_g[l])
        x = x + peer_ffn(h, peer_w_q[l], peer_sub_keys[l], peer_u[l], peer_v[l])
    return rmsnorm(x, final_norm_g)


_drawn_inputs = setup_inputs


def setup_inputs(seed=0):
    import zlib

    import numpy as np

    out = dict(_drawn_inputs(seed))
    spreads = {}
    factors = {}
    for name, (base, spread) in spreads.items():
        noise = np.random.default_rng([zlib.crc32(name.encode()), seed]).standard_normal(out[name].shape)
        drawn = base * np.exp(spread * noise) if base else spread * noise
        out[name] = __import__('jax').numpy.asarray(drawn.astype(out[name].dtype))
    for name, factor in factors.items():
        out[name] = (out[name] * factor).astype(out[name].dtype)
    return out
```

```python
from contextlib import ExitStack

import numpy as np

import concourse.bass as bass
from concourse import mybir

F32 = mybir.dt.float32
F32R = mybir.dt.float32r
I32 = mybir.dt.int32
U32 = mybir.dt.uint32
ALU = mybir.AluOpType
ACT = mybir.ActivationFunctionType
AX = mybir.AxisListType

P = 128
D = 1024
KD = D // P
SEQ = 256
NT = SEQ // P
DEPTH = 2
CHUNK = 64
HD = 64
EPS = 1e-6
NEG = -1e30
LOWEST = -3.0e38
MH, MNOPE, MROPE, MV = 6, 64, 32, 64
MQK = MNOPE + MROPE
QL, KVL = 256, 128
SH, FH = 5, 5
PH, NK, HALF, TOPK = 8, 128, 128, 16
NEXP = NK * NK
W3 = SH * HD
GATES0 = QL + KVL + MROPE + 6 * W3 + FH
NG = 3 * D // P
SCALE_A = float(MQK) ** -0.5
SCALE_H = float(HD) ** -0.5
INV_SQRT2PI = float(1.0 / (2.0 * np.pi))
PI_IN = 3.1415925
TWO_PI = (6.28125, 0.0019350051879882812, 3.019915981956753e-07)

C_ID, C_IOTA, C_START, C_DSTART, C_I16, C_FREQ, C_END = 0, 128, 256, 272, 288, 304, 320
M_MLA, M_FOX, M_STRICT, M_TRIU, M_END = 0, 256, 512, 768, 1024

B_OF = [TOPK // (a + 1) for a in range(TOPK)]
STARTS = [sum(B_OF[:a]) for a in range(TOPK)]
NCAND = sum(B_OF)
SEGMENTS = [(0, 1, 16), (1, 1, 8), (2, 1, 5), (3, 1, 4), (4, 1, 3), (5, 3, 2), (8, 8, 1)]

JOBS = (
    [("cq", "w_in", 0, QL, KD, P, True), ("ckv", "w_in", QL, 256, KD, P, True)]
    + [("qs", "w_in", 416, W3, KD, P, False), ("ks", "w_in", 416 + W3, W3, KD, P, False)]
    + [("uq", "w_uq", 0, MH * MQK, 2, P, True), ("ukv", "w_ukv", 0, MH * (MNOPE + MV), 1, P, True)]
    + [("vs", "w_in", 416 + 2 * W3, W3, KD, P, True)]
    + [("qf", "w_in", 416 + 3 * W3, W3, KD, P, False), ("kf", "w_in", 416 + 4 * W3, W3, KD, P, False)]
    + [("vf", "w_in", 416 + 5 * W3, W3 + FH + 1, KD, P, True)]
    + [("gate", "w_in", GATES0 + 256 * n, 256, KD, P, False) for n in range(12)]
    + [(f"wo{br}", s, 512 * h, 512, 3, r, False) for h in range(2)
       for br, (s, r) in enumerate((("w_o_mla", P), ("w_o_sb", 64), ("w_o_fox", 64)))]
    + [("wout", "w_out", 256 * n, 256, KD, P, True) for n in range(4)]
    + [("wq", "peer_w_q", 256 * n, 256, KD, P, False) for n in range(8)]
)
NJ = len(JOBS)
J_GATE = [j for j, x in enumerate(JOBS) if x[0] == "gate"]
J_WO = J_GATE[-1] + 1
J_WOUT = J_WO + 6
J_WQ = J_WOUT + 4
SLOT = max(x[3] * x[4] for x in JOBS)
NRAW = 3


def groups_of(j):
    name, _, _, w, _, _, tokens = JOBS[j]
    if tokens:
        n = w // 2 if w > 512 or name == "uq" else w
        return [(tt, c, n) for tt in range(NT) for c in range(0, w, n)]
    return [(None, c, min(P, w - c)) for c in range(0, w, P)]


GROUPS = [groups_of(j) for j in range(NJ)]
FIRST = [sum(len(g) for g in GROUPS[:j]) for j in range(NJ + 1)]
NBANK = 3

HEADS = (MH, SH, FH)
UNITS = [(br, qt) for br in range(3) for qt in range(NT)]


def pt_batches(u):
    br, qt = UNITS[u]
    blocks = [(h, kt) for h in range(HEADS[br]) for kt in range(qt + 1)]
    return [blocks[n:n + 4] for n in range(0, len(blocks), 4)]


PT0 = [sum(len(pt_batches(v)) for v in range(u)) for u in range(len(UNITS) + 1)]

def g1(l, k): return l * KD + k
def g2(l, k): return (DEPTH + l) * KD + k
def gb(l, n): return 2 * DEPTH * KD + l * NG + n
def gq(l, k): return 2 * DEPTH * KD + DEPTH * NG + 2 * l + k
def gkv(l): return 2 * DEPTH * KD + DEPTH * NG + 2 * DEPTH + l


NVEC = gkv(DEPTH)


NU = len(UNITS)
PER_LAYER = {
    "masks": 16, "keys": 16,
    "whi": NJ, "wlo": NJ,
    "pj": FIRST[NJ],
    "ss": 2 * NT, "ms": 2, "rt": 2, "xn": 2,
    "xT": KD, "hhi": 2 * KD, "hlo": 2 * KD,
    "cms": 2, "crt": 1, "cn": 1, "cT": 1, "chi": 3, "clo": 3,
    "rope": 1, "mT": 6, "mTc": 6,
    "score": NU, "sfree": NU, "kz": 2,
    "ab": 2, "sb_w": 2, "ex": 2,
    "pmax": 4, "pexp": 4,
    "probs": NU, "pt": PT0[NU], "ptc": PT0[NU], "pv": NU,
    "ohi": NU, "olo": NU,
    "fz": 1, "fe": 2, "lf": 1, "cum": 1, "cumc": 1,
    "sig": 3, "yacc": KD, "yhi": KD, "ylo": KD,
    "keyT": 1, "keyTc": 1, "sc": 8, "scc": NT,
    "ge": NT, "gexp": NT, "slot": NT, "slotT": NT, "slotTc": NT,
    "oh1": SEQ // 4, "oh2": SEQ // 4, "k2": SEQ // 4, "g": SEQ // 4, "gc": SEQ // 4,
    "ut": NK, "uhi": NK, "ulo": NK, "s": NK, "gelu": NK,
    "w": NK, "wsp": NK, "wl": NK, "vhi": NK, "vlo": NK, "v": NK, "xnew": 4,
}


def build(nc, t_in, out):
    ctx = ExitStack()
    base = -(-nc.sbuf_base // 64) * 64

    def at(name, shape, off, dt=F32):
        return nc.alloc_sbuf_tensor_at(name, shape, dt, offset=base + off)

    def sem(name):
        return ctx.enter_context(nc.semaphore(name))

    with ctx:
        x = at("x", [P, NT, D], 0)
        h_hi = at("h_hi", [P, KD, SEQ], 8192, F32R)
        h_lo = at("h_lo", [P, KD, SEQ], 16384, F32R)
        cst = at("cst", [P, C_END], 24576)
        vecT = at("vecT", [P, 88], 25856)
        trig = at("trig", [P, NT, 2, 16], 26208)
        st = at("st", [P, 104], 26464)
        ident = cst[:, C_ID:C_ID + P]
        iota = cst[:, C_IOTA:C_IOTA + P]
        ssq, msq, rms, rstd = (st[:, 8 * n:8 * n + 4] for n in range(4))
        mx, nmx, esum, rsum, ntot = (st[:, 32 + 6 * n:38 + 6 * n] for n in range(5))
        lf = st[:, 62:72].rearrange("p (t h) -> p t h", t=NT)
        nlf = st[:, 72:82].rearrange("p (t h) -> p t h", t=NT)
        cumq = st[:, 82:92].rearrange("p (t h) -> p t h", t=NT)
        bf = st[:, 92:92 + DEPTH * FH].rearrange("p (l h) -> p l h", l=DEPTH)
        S0 = 26880
        u_raw = [at(f"u_raw{i}", [P, D], S0 + 4096 * i) for i in range(2)]
        v_raw = [at(f"v_raw{i}", [P, D], S0 + 8192 + 4096 * i) for i in range(2)]
        u_hi = [at(f"u_hi{i}", [P, D], S0 + 16384 + 4096 * i, F32R) for i in range(2)]
        u_lo = [at(f"u_lo{i}", [P, D], S0 + 24576 + 4096 * i, F32R) for i in range(2)]
        v_hi = [at(f"v_hi{i}", [P, D], S0 + 32768 + 4096 * i, F32R) for i in range(2)]
        v_lo = [at(f"v_lo{i}", [P, D], S0 + 40960 + 4096 * i, F32R) for i in range(2)]
        wgt = at("wgt", [P, SEQ], S0 + 49152)
        w_hi = [at(f"w_hi{i}", [P, SEQ], S0 + 50176 + 1024 * i, F32R) for i in range(2)]
        w_lo = [at(f"w_lo{i}", [P, SEQ], S0 + 52224 + 1024 * i, F32R) for i in range(2)]
        G = at("G", [P, SEQ, NK], S0 + 54272)
        R0 = S0 + 16384
        sc = at("sc", [P, NT, 16 * NK], R0)
        slotT = at("slotT", [P, 3, SEQ], R0 + 16384)
        oh1 = [at(f"oh1_{i}", [P, 4, NK], R0 + 19456 + 2048 * i) for i in range(2)]
        oh2 = [at(f"oh2_{i}", [P, 4, NK], R0 + 23552 + 2048 * i) for i in range(2)]
        vtop = at("vtop", [P, 16, 16], R0 + 27648)
        itop = at("itop", [P, 16, 16], R0 + 28672, U32)
        itf = at("itf", [P, 16, 16], R0 + 29696)
        cand = at("cand", [P, PH, NCAND], R0 + 30720)
        slots = at("slots", [P, 3, P], R0 + 32320)
        selv = at("selv", [P, PH, 16], R0 + 33856)
        selp = at("selp", [P, PH, 16], R0 + 34368, U32)
        posf = at("posf", [P, P], R0 + 34880)
        sub = at("sub", [P, P], R0 + 35392)
        dtop = at("dtop", [P, PH, 16], R0 + 35904)
        key2 = [at(f"key2_{i}", [P, 4], R0 + 36480 + 32 * i) for i in range(2)]
        gsum = at("gsum", [P, 2, PH], R0 + 36416)
        M0 = S0
        A = at("A", [P, MH, SEQ], M0)
        B = at("B", [P, MH, SEQ], M0 + 6144)
        k_full = at("k_full", [P, NT, MH, MQK], M0 + 6144)
        rope_t = at("rope_t", [P, 4, MH, 16], M0)
        PT = at("PT", [P, 12, P], M0 + 12288)
        raw = [at(f"raw{i}", [P, SLOT], M0 + 18432 + 4 * SLOT * i) for i in range(NRAW)]
        WH0 = M0 + 18432 + 4 * SLOT * NRAW
        wb_hi = [at(f"wb_hi{i}", [P, SLOT], WH0 + 4 * SLOT * i, F32R) for i in range(2)]
        wb_lo = [at(f"wb_lo{i}", [P, SLOT], WH0 + 4 * SLOT * (2 + i), F32R) for i in range(2)]
        Q0 = WH0 + 16 * SLOT
        gates = at("gates", [P, NG, SEQ], Q0)
        xn = at("xn", [P, NT, D], Q0)
        keys = at("keys", [P, 2, P], Q0 + 8192)
        keysT = at("keysT", [P, 2, P], Q0 + 9216)
        C = at("C", [P, MH, SEQ], Q0 + 24576)
        q_tok = at("q_tok", [P, NT, MH * MQK], Q0 + 24576)
        yacc = at("yacc", [P, 4, SEQ], Q0 + 24576)
        ytmp = at("ytmp", [P, 2, SEQ], Q0 + 28672)
        cq = at("cq", [P, NT, QL], Q0 + 30720)
        ckv = at("ckv", [P, NT, KVL + MROPE], Q0 + 32768)
        v_s = at("v_s", [P, NT, W3], Q0 + 34048)
        v_f = at("v_f", [P, NT, W3 + FH + 1], Q0 + 36608)
        X0 = Q0 + 39232
        qT = at("qT", [P, 2, 3, SEQ], X0)
        kT = at("kT", [P, 2, 5, SEQ], X0 + 6144)
        v_m = at("v_m", [P, NT, MH * MV], X0 + 16384)
        mqk = at("mqk", [P, 2, MH, SEQ], X0 + 19456)
        y_hi = at("y_hi", [P, KD, SEQ], X0, F32R)
        y_lo = at("y_lo", [P, KD, SEQ], X0 + 8192, F32R)
        O0 = X0 + 31744
        o_hi = at("o_hi", [P, 3, 3, SEQ], O0, F32R)
        o_lo = at("o_lo", [P, 3, 3, SEQ], O0 + 9216, F32R)
        c_hi = at("c_hi", [P, 3, SEQ], O0, F32R)
        c_lo = at("c_lo", [P, 3, SEQ], O0 + 3072, F32R)
        pq = at("pq", [P, 2 * PH, SEQ], O0)
        masks = at("masks", [P, M_END], O0 + 18432)
        vecs = at("vecs", [P, P], M0)
        pos_i = at("pos_i", [P, NT], M0 + 512, I32)
        pos = at("pos", [P, NT], M0 + 544)
        ang = at("ang", [P, NT, 16], M0 + 576)
        turns_i = at("turns_i", [P, NT, 16], M0 + 704, I32)
        turns = at("turns", [P, NT, 16], M0 + 832)
        half_s = at("half_s", [P, NT, 16], M0 + 960)
        gain_f = at("gain_f", [P, D], M0 + 1088)
        y_out = at("y_out", [P, NT, D], M0 + 8192)

        ps = ctx.enter_context(nc.psum_tensor("ps", [P, 8, 512], F32))
        ps_score = ps[:, 3:6, :].rearrange("p b (h k) -> p (b h) k", k=SEQ)
        ps_norm = ps[:, 3:7, :].rearrange("p b (h k) -> p (b h) k", k=SEQ)
        ps_pt = ps[:, 6, :]
        ps_o = ps[:, 7, :].rearrange("p (h k) -> p h k", k=P)
        ps_ut = ps[:, 0:2, :].rearrange("p b n -> p (b n)")

        s_boot = sem("s_boot")
        s_bootT = sem("s_bootT")
        s_vecT = sem("s_vecT")
        s_ang = sem("s_ang")
        s_sin = sem("s_sin")
        s_trig = sem("s_trig")
        s_dve = sem("s_dve")
        s_act = sem("s_act")
        s_gain = sem("s_gain")
        s_fss = sem("s_fss")
        s_frt = sem("s_frt")
        s_fms = sem("s_fms")
        s_y = sem("s_y")
        s_out = sem("s_out")

        landed, total = [], [0] * NRAW
        for j in range(NJ):
            total[j % NRAW] += 16 * (2 if JOBS[j][5] < P else 1)
            landed.append(total[j % NRAW])
        sems = {n: sem(f"s_{n}") for n in PER_LAYER}
        for n, k in (("land", NRAW), ("free", NBANK), ("landu", 2), ("landv", 2)):
            sems[n] = [sem(f"s_{n}{i}") for i in range(k)]

        class Layer:

            def __init__(self, l):
                self.l = l

            def __getitem__(self, name):
                return sems[name]

            def had(self, name, i=0):
                if name == "land":
                    return self.l * total[i]
                if name == "free":
                    return self.l * ((FIRST[NJ] - i + NBANK - 1) // NBANK)
                return self.l * (16 * NK // 2 if name in ("landu", "landv") else PER_LAYER[name])

        L = [Layer(l) for l in range(DEPTH)]

        def chunk(buf, j):
            return buf[:, 0:JOBS[j][3] * JOBS[j][4]].rearrange("p (k n) -> p k n", k=JOBS[j][4])

        def parts(j):
            k, r = JOBS[j][4], JOBS[j][5]
            return [(P, 0, k)] if r == P else [(P, 0, k - 1), (r, k - 1, k)]

        block = ctx.enter_context(nc.Block())

        @block.sync
        def _(sp):
            sp.dma_start(x[:, :, :], t_in["x"][0].rearrange("(t p) d -> p t d", p=P)).then_inc(s_boot, 16)
            sp.dma_start(cst[:, :], t_in["consts"][:, 0:C_END]).then_inc(s_boot, 16)
            for t, r0, n in (("norm1_g", g1(0, 0), DEPTH * KD), ("norm2_g", g2(0, 0), DEPTH * KD),
                             ("b_gate", gb(0, 0), DEPTH * NG), ("mla_q_norm_g", gq(0, 0), DEPTH * 2),
                             ("mla_kv_norm_g", gkv(0), DEPTH)):
                sp.dma_start(vecs[r0:r0 + n, :], t_in[t].rearrange("l (k p) -> (l k) p", p=P)).then_inc(s_boot, 16)
            sp.dma_start(pos_i[:, :], t_in["positions"][0].rearrange("(t p) -> p t", p=P),
                         allow_slow_non_contiguous=True).then_inc(s_boot, 16)
            sp.dma_start(st[:, 92:92 + DEPTH * FH], t_in["fox_b_f"].rearrange("l h -> (l h)").partition_broadcast(P)).then_inc(s_boot, 16)

            for l in range(DEPTH):
                s = L[l]
                if l:
                    sp.wait_ge(L[l - 1]["xnew"], L[l - 1].had("xnew") + 4)
                sp.dma_start(masks[:, :], t_in["consts"][:, C_END:C_END + M_END]).then_inc(s["masks"], 16)
                for j, (name, src, c0, w, kt, last, _) in enumerate(JOBS):
                    if j >= NRAW:
                        sp.wait_ge(s["wlo"], s.had("wlo") + j - NRAW + 1)
                    if name == "wq" and JOBS[j - 1][0] == "wout":
                        sp.wait_ge(s["ylo"], s.had("ylo") + KD)
                        sp.dma_start(keys[:, :, :], t_in["peer_sub_keys"][l].rearrange("s n c -> n s c")).then_inc(s["keys"], 16)
                    for rows, k0, k1 in parts(j):
                        sp.dma_start(chunk(raw[j % NRAW], j)[0:rows, k0:k1, :],
                                     t_in[src][l, k0 * P:(k1 - 1) * P + rows, c0:c0 + w].rearrange(
                                         "(k p) n -> p k n", p=rows)).then_inc(s["land"][j % NRAW], 16)
                sp.wait_ge(s["ylo"], s.had("ylo") + KD)

                def load_block(b, i):
                    sp.dma_start(u_raw[i][:, :], t_in["peer_u"][l, bass.ds(b * P, P), :]).then_inc(s["landu"][i], 16)

                def load_v(b, i):
                    sp.dma_start(v_raw[i][:, :], t_in["peer_v"][l, bass.ds(b * P, P), :]).then_inc(s["landv"][i], 16)

                for i in range(2):
                    load_block(i, i)
                    load_v(i, i)
                with sp.Fori(1, NK // 2) as n:
                    for i in range(2):
                        sp.wait_ge(s["ut"], s.had("ut") + 2 * n + (i - 1))
                        load_block(2 * n + i, i)
                        sp.wait_ge(s["vlo"], s.had("vlo") + 2 * n + (i - 1))
                        load_v(2 * n + i, i)

            sp.wait_ge(L[-1]["v"], L[-1].had("v") + NK)
            sp.dma_start(gain_f[:, :], t_in["final_norm_g"].partition_broadcast(P)).then_inc(s_gain, 16)
            for tt in range(NT):
                sp.wait_ge(s_y, tt + 1)
                sp.dma_start(out[0, tt * P:(tt + 1) * P, :], y_out[:, tt, :]).then_inc(s_out, 16)
            sp.wait_ge(s_out, 16 * NT)

        @block.gpsimd
        def _(pool):
            for l in range(DEPTH):
                s = L[l]
                if l:
                    pool.wait_ge(L[l - 1]["xnew"], L[l - 1].had("xnew") + 4)
                pool.memset(kT[HD:P, :, 0:4:2, :], 0.0).then_inc(s["kz"], 1)
                pool.memset(kT[0:HD, :, 1:4:2, :], 0.0).then_inc(s["kz"], 1)
                for tt in range(NT):
                    pool.wait_ge(s["slotTc"], s.had("slotTc") + tt + 1)
                    first = tt * 32

                    def take_keys(g, i):
                        pool.tensor_copy(key2[i][:, :], slotT[:, 1, bass.ds(4 * g, 4)]).then_inc(s["k2"], 1)

                    def one_hot(g, i, reuse=True, more=True):
                        if reuse:
                            pool.wait_ge(s["g"], s.had("g") + g - 1)
                        pool.wait_ge(s["k2"], s.had("k2") + g + 1)
                        if more:
                            if not isinstance(g, int) or g > 0:
                                pool.wait_ge(s["oh2"], s.had("oh2") + g)
                            take_keys(g + 1, 1 - i)
                        for t in range(4):
                            ins = pool.tensor_scalar(oh2[i][:, t, :], iota, key2[i][:, t:t + 1], None, ALU.is_equal)
                        ins.then_inc(s["oh2"], 1)

                    if first:
                        pool.wait_ge(s["oh2"], s.had("oh2") + first)
                    take_keys(first, 0)
                    for i in range(2):
                        one_hot(first + i, i, reuse=tt > 0)
                    with pool.Fori(1, 15) as n:
                        for i in range(2):
                            one_hot(2 * n + (first + i), i)
                    one_hot(first + 30, 0)
                    one_hot(first + 31, 1, more=False)

        @block.scalar
        def _(act):
            count = [0]

            def link(ins):
                count[0] += 1
                ins.then_inc(s_act, 1)
                act.wait_ge(s_act, count[0])

            act.wait_ge(s_bootT, 1)
            act.activation(vecT[:, 0:NVEC], ps[:, 0, 0:NVEC], ACT.Copy).then_inc(s_vecT, 1)
            act.wait_ge(s_ang, 1)
            act.activation(trig[:, :, 1, :], ang[:, :, :], ACT.Sin).then_inc(s_sin, 1)
            act.activation(half_s[:, :, :], ang[:, :, :], ACT.Sin, scale=0.5).then_inc(s_sin, 1)

            for l in range(DEPTH):
                s = L[l]

                def split_hi(j):
                    act.wait_ge(s["land"][j % NRAW], s.had("land", j % NRAW) + landed[j])
                    if j >= 2:
                        act.wait_ge(s["pj"], s.had("pj") + FIRST[j - 1])
                    ps_ = parts(j)
                    for rows, k0, k1 in ps_:
                        ins = act.activation(chunk(wb_hi[j % 2], j)[0:rows, k0:k1, :],
                                             chunk(raw[j % NRAW], j)[0:rows, k0:k1, :], ACT.Copy)
                    ins.then_inc(s["whi"], 1)

                def evac(j, n):
                    name = JOBS[j][0]
                    g = FIRST[j] + n
                    _, c0, rows = GROUPS[j][n]
                    act.wait_ge(s["pj"], s.had("pj") + g + 1)
                    src = ps[0:rows, g % NBANK, 0:SEQ]
                    if name == "wq":
                        ins = act.activation(pq[:, 2 * (j - J_WQ) + n, :], src, ACT.Copy)
                    elif name in ("qs", "qf"):
                        ins = act.activation(qT[0:rows, int(name == "qf"), n, :], src, ACT.Copy,
                                             scale=SCALE_H if name == "qs" else 1.0)
                    else:
                        for r in range(0, rows, HD):
                            ins = act.activation(kT[r:r + HD, int(name == "kf"), 2 * n + r // HD, :],
                                                 ps[r:r + HD, g % NBANK, 0:SEQ], ACT.Copy)
                    ins.then_inc(s["free"][g % NBANK], 1)

                def evacuated(j):
                    for g in range(FIRST[j + 1] - NBANK, FIRST[j + 1]):
                        act.wait_ge(s["free"][g % NBANK], s.had("free", g % NBANK) + g // NBANK + 1)

                def norm_act(which, gain):
                    if which == 0 and l:
                        act.wait_ge(L[l - 1]["xnew"], L[l - 1].had("xnew") + 4)
                    if which == 0 and l == 0:
                        act.wait_ge(s_boot, 16 * 9)
                    if which == 1:
                        evacuated(J_WQ - 1)
                    for tt in range(NT):
                        act.activation(xn[:, tt, :], x[:, tt, :], ACT.Square,
                                       accum_out=ssq[:, tt:tt + 1]).then_inc(s["ss"], 1)
                    act.wait_ge(s["ms"], s.had("ms") + which + 1)
                    act.activation(rms[:, 0:NT], msq[:, 0:NT], ACT.Sqrt).then_inc(s["rt"], 1)
                    for k in range(KD):
                        if k % 2 == 0:
                            act.wait_ge(s["xT"], s.had("xT") + (which * KD + k) // 2 + 1)
                        act.activation(h_hi[:, k, :], ps_norm[:, k, :], ACT.Copy,
                                       scale=vecT[:, gain(l, k):gain(l, k) + 1]).then_inc(s["hhi"], 1)

                def softmax_act(u):
                    br, qt = UNITS[u]
                    H, N = HEADS[br], P * (qt + 1)
                    if br == 1:
                        act.wait_ge(s["score"], s.had("score") + u + 1)
                        act.wait_ge(s["pt"], s.had("pt") + PT0[u])
                        z = ps_score[:, 0:H, 0:N]
                        link(act.activation(A[:, 0:H, 0:N], z, ACT.Abs))
                        link(act.activation(A[:, 0:H, 0:N], A[:, 0:H, 0:N], ACT.Exp, scale=-1.0))
                        act.activation(A[:, 0:H, 0:N], A[:, 0:H, 0:N], ACT.Ln, bias=1.0).then_inc(s["ab"], 1)
                        act.wait_ge(s["sb_w"], s.had("sb_w") + qt + 1)
                        for h in range(H):
                            ins = act.activation(A[:, h, 0:N], B[:, h, 0:N], ACT.Exp, bias=ntot[:, h:h + 1])
                        ins.then_inc(s["ex"], 1)
                        return
                    act.wait_ge(s["pmax"], s.had("pmax") + (u + 1 if br == 0 else u - 1))
                    for h in range(H):
                        ins = act.activation(A[:, h, 0:N], A[:, h, 0:N], ACT.Exp, bias=nmx[:, h:h + 1],
                                             scale=SCALE_A if br == 0 else SCALE_H,
                                             accum_out=esum[:, h:h + 1])
                    ins.then_inc(s["pexp"], 1)

                def pv_act(u):
                    br, qt = UNITS[u]
                    H = HEADS[br]
                    if u:
                        act.wait_ge(s["pv"], s.had("pv") + u)
                    at_ = 0
                    for n, batch in enumerate(pt_batches(u)):
                        act.wait_ge(s["pt"], s.had("pt") + PT0[u] + n + 1)
                        m = len(batch)
                        act.activation(PT[:, at_:at_ + m, :], ps_pt[:, 0:m * P].rearrange("p (m k) -> p m k", k=P),
                                       ACT.Copy).then_inc(s["ptc"], 1)
                        at_ += m
                    act.wait_ge(s["pv"], s.had("pv") + u + 1)
                    cols = slice(qt * P, (qt + 1) * P)
                    if H % 2 == 0:
                        ins = act.activation(o_hi[:, br, :, cols], ps_o[:, 0:3, :], ACT.Copy)
                    else:
                        act.activation(o_hi[:, br, 0:2, cols], ps_o[:, 0:2, :], ACT.Copy)
                        ins = act.activation(o_hi[0:64, br, 2, cols], ps_o[0:64, 2, :], ACT.Copy)
                    ins.then_inc(s["ohi"], 1)

                norm_act(0, g1)
                for j in range(3):
                    split_hi(j)
                evacuated(1)
                for tt in range(NT):
                    act.activation(C[:, tt, :], cq[:, tt, :], ACT.Square, accum_out=ssq[:, 2 * tt:2 * tt + 1])
                    ins = act.activation(C[:, 2 + tt, 0:KVL], ckv[:, tt, 0:KVL], ACT.Square,
                                         accum_out=ssq[:, 2 * tt + 1:2 * tt + 2])
                ins.then_inc(s["cms"], 1)
                act.wait_ge(s["cms"], s.had("cms") + 2)
                act.activation(rms[:, 0:4], msq[:, 0:4], ACT.Sqrt).then_inc(s["crt"], 1)
                split_hi(3)
                for n in range(3):
                    evac(2, n)
                act.wait_ge(s["cT"], s.had("cT") + 1)
                for k in range(3):
                    c = gq(l, k) if k < 2 else gkv(l)
                    act.activation(c_hi[:, k, :], ps_norm[:, k, :], ACT.Copy, scale=vecT[:, c:c + 1]).then_inc(s["chi"], 1)
                split_hi(4)
                for n in range(3):
                    evac(3, n)
                split_hi(5)
                split_hi(6)
                split_hi(7)
                for n in range(6):
                    act.wait_ge(s["mT"], s.had("mT") + n + 1)
                    act.activation(mqk[0:MQK, n // 3, 2 * (n % 3):2 * (n % 3) + 2, :],
                                   ps_score[0:MQK, 2 * (n % 3):2 * (n % 3) + 2, :], ACT.Copy).then_inc(s["mTc"], 1)
                split_hi(8)
                for n in range(3):
                    evac(7, n)
                split_hi(9)
                for n in range(3):
                    evac(8, n)
                split_hi(10)
                act.wait_ge(s["fz"], s.had("fz") + 1)
                act.activation(lf[:, :, :], nlf[:, :, :], ACT.Exp, scale=1.0).then_inc(s["fe"], 1)
                act.wait_ge(s["fe"], s.had("fe") + 1)
                act.activation(lf[:, :, :], lf[:, :, :], ACT.Ln, bias=1.0).then_inc(s["fe"], 1)
                for u in range(len(UNITS)):
                    split_hi(10 + 2 * u + 1)
                    softmax_act(u)
                    split_hi(10 + 2 * u + 2)
                    pv_act(u)
                evacuated(J_WO - 1)
                for br in range(3):
                    act.activation(gates[:, 8 * br:8 * br + 8, :], gates[:, 8 * br:8 * br + 8, :],
                                   ACT.Sigmoid).then_inc(s["sig"], 1)
                for j in range(J_WO + 1, J_WO + 6):
                    split_hi(j)
                    if j == J_WO + 3:
                        for n in range(4):
                            act.wait_ge(s["yacc"], s.had("yacc") + n + 1)
                            act.activation(y_hi[:, n, :], yacc[:, n, :], ACT.Copy).then_inc(s["yhi"], 1)
                split_hi(J_WOUT)
                for n in range(4):
                    act.wait_ge(s["yacc"], s.had("yacc") + 4 + n + 1)
                    act.activation(y_hi[:, 4 + n, :], yacc[:, n, :], ACT.Copy).then_inc(s["yhi"], 1)
                for j in range(J_WOUT + 1, J_WQ + 1):
                    split_hi(j)
                norm_act(1, g2)
                act.wait_ge(s["keyT"], s.had("keyT") + 1)
                act.activation(keysT[:, :, :], ps_o[:, 0:2, :], ACT.Copy).then_inc(s["keyTc"], 1)
                for j in range(J_WQ, NJ):
                    if j + 1 < NJ:
                        split_hi(j + 1)
                    for n in range(2):
                        evac(j, n)
                for tt in range(NT):
                    for b in range(4):
                        act.wait_ge(s["sc"], s.had("sc") + 4 * tt + b + 1)
                        ins = act.activation(sc[:, tt, 512 * b:512 * b + 512], ps[:, 4 * tt + b, :], ACT.Copy)
                    ins.then_inc(s["scc"], 1)
                for tt in range(NT):
                    act.wait_ge(s["ge"], s.had("ge") + tt + 1)
                    act.activation(selv[:, :, :], selv[:, :, :], ACT.Exp).then_inc(s["gexp"], 1)
                    act.wait_ge(s["slotT"], s.had("slotT") + tt + 1)
                    act.activation(slotT[:, :, tt * P:tt * P + P],
                                   ps[:, 2, 0:3 * P].rearrange("p (n t) -> p n t", n=3), ACT.Copy).then_inc(s["slotTc"], 1)
                with act.Fori(0, 32) as n:
                    for i in range(2):
                        act.wait_ge(s["g"], s.had("g") + 2 * n + (i + 1))
                        act.activation(G[:, bass.ds(8 * n + 4 * i, 4), :],
                                       ps[:, i, :].rearrange("p (t k) -> p t k", t=4), ACT.Copy).then_inc(s["gc"], 1)

                def u_split(c, i):
                    act.wait_ge(s["ut"], s.had("ut") + c + 1)
                    act.activation(u_hi[i][:, :], ps_ut, ACT.Copy).then_inc(s["uhi"], 1)

                def cycle(c, i, first=False, last=False, n=None):
                    if not last:
                        if not (first and i == 0):
                            act.wait_ge(s["s"], s.had("s") + c)
                        u_split(c + 1, 1 - i)
                    act.wait_ge(s["landv"][i], s.had("landv", i) + 16 * n + 16)
                    if not first:
                        act.wait_ge(s["v"], s.had("v") + c - 1)
                    act.activation(v_hi[i][:, :], v_raw[i][:, :], ACT.Copy).then_inc(s["vhi"], 1)
                    act.wait_ge(s["s"], s.had("s") + c + 1)
                    if not (first and i == 0):
                        act.wait_ge(s["wl"], s.had("wl") + c)
                    act.activation(wgt[:, :], ps[:, 2 + i, 0:SEQ], ACT.Gelu).then_inc(s["gelu"], 1)
                    act.wait_ge(s["w"], s.had("w") + c + 1)
                    act.activation(w_hi[i][:, :], wgt[:, :], ACT.Copy).then_inc(s["wsp"], 1)

                u_split(0, 0)
                cycle(0, 0, first=True, n=0)
                cycle(1, 1, first=True, n=0)
                with act.Fori(1, NK // 2 - 1) as n:
                    for i in range(2):
                        cycle(2 * n + i, i, n=n)
                cycle(NK - 2, 0, n=NK // 2 - 1)
                cycle(NK - 1, 1, last=True, n=NK // 2 - 1)

            act.wait_ge(L[-1]["xnew"], L[-1].had("xnew") + 4)
            for tt in range(NT):
                act.activation(y_out[:, tt, :], x[:, tt, :], ACT.Square, accum_out=ssq[:, tt:tt + 1]).then_inc(s_fss, 1)
            act.wait_ge(s_fms, 1)
            act.activation(rms[:, 0:NT], msq[:, 0:NT], ACT.Sqrt).then_inc(s_frt, 1)

        @block.tensor
        def _(pe):
            pe.wait_ge(s_boot, 16 * 9)
            pe.transpose(ps[:, 0, 0:NVEC], vecs[0:NVEC, :], ident[0:NVEC, 0:NVEC]).then_inc(s_bootT, 1)
            pe.wait_ge(s_vecT, 1)

            def three(out_, a_hi, a_lo, b_hi, b_lo, start, stop):
                pe.matmul(out_, a_hi, b_hi, start=start, stop=False)
                pe.matmul(out_, a_hi, b_lo, start=False, stop=False)
                return pe.matmul(out_, a_lo, b_hi, start=False, stop=stop)

            for l in range(DEPTH):
                s = L[l]
                def project(j, a_hi, a_lo, ready=None):
                    name, _, _, w, kt, last, tokens = JOBS[j]
                    pe.wait_ge(s["wlo"], s.had("wlo") + j + 1)
                    whi, wlo = chunk(wb_hi[j % 2], j), chunk(wb_lo[j % 2], j)
                    for n, (tt, c0, m) in enumerate(GROUPS[j]):
                        g = FIRST[j] + n
                        b = g % NBANK
                        if g >= NBANK:
                            pe.wait_ge(s["free"][b], s.had("free", b) + g // NBANK)
                        if ready is not None and n == 0 and not isinstance(ready, str):
                            pe.wait_ge(*ready)
                        for k in range(kt):
                            if ready == "norm1" and n == 0:
                                pe.wait_ge(s["hlo"], s.had("hlo") + k + 1)
                            if ready == "norm2" and n == 0:
                                pe.wait_ge(s["hlo"], s.had("hlo") + KD + k + 1)
                            r = P if k < kt - 1 else last
                            edge = dict(start=k == 0, stop=k == kt - 1)
                            if tokens:
                                t = slice(tt * P, tt * P + P)
                                mm = three(ps[:, b, 0:m], a_hi[:, k, t], a_lo[:, k, t],
                                           whi[:, k, c0:c0 + m], wlo[:, k, c0:c0 + m], **edge)
                            else:
                                mm = three(ps[0:m, b, 0:SEQ], whi[0:r, k, c0:c0 + m], wlo[0:r, k, c0:c0 + m],
                                           a_hi[0:r, k, :], a_lo[0:r, k, :], **edge)
                        mm.then_inc(s["pj"], 1)

                def norm_pe(which):
                    pe.wait_ge(s["xn"], s.had("xn") + which + 1)
                    for k in range(KD):
                        for tt in range(NT):
                            mm = pe.transpose(ps_norm[:, k, tt * P:tt * P + P], xn[:, tt, k * P:k * P + P], ident)
                        if k % 2:
                            mm.then_inc(s["xT"], 1)

                def scores(u):
                    br, qt = UNITS[u]
                    N = P * (qt + 1)
                    q = slice(qt * P, qt * P + P)
                    if u:
                        pe.wait_ge(s["sfree"], s.had("sfree") + u)
                    if u == 0:
                        pe.wait_ge(s["mTc"], s.had("mTc") + 6)
                    if u == NT:
                        pe.wait_ge(s["kz"], s.had("kz") + 2)
                    for h in range(HEADS[br]):
                        o = ps_score[:, h, 0:N]
                        if br == 0:
                            mm = pe.matmul(o, mqk[0:MQK, 0, h, q], mqk[0:MQK, 1, h, 0:N], start=True, stop=True)
                            continue
                        r = P if h < 4 else HD
                        mm = pe.matmul(o, qT[0:r, br - 1, h // 2, q], kT[0:r, br - 1, h, 0:N], start=True, stop=br == 1)
                        if br == 2:
                            mm = pe.matmul(o, nlf[:, 0, h:h + 1].to_broadcast([P, P]),
                                           masks[:, M_TRIU:M_TRIU + N], start=False, stop=qt == 0)
                            if qt == 1:
                                mm = pe.matmul(ps_score[:, h, P:N], nlf[:, 1, h:h + 1].to_broadcast([P, P]),
                                               masks[:, M_TRIU:M_TRIU + P], start=False, stop=True)
                    mm.then_inc(s["score"], 1)

                def pv(u):
                    br, qt = UNITS[u]
                    H = HEADS[br]
                    pe.wait_ge(s["probs"], s.had("probs") + u + 1)
                    for n, batch in enumerate(pt_batches(u)):
                        if PT0[u] + n:
                            pe.wait_ge(s["ptc"], s.had("ptc") + PT0[u] + n)
                        for i, (h, kt) in enumerate(batch):
                            mm = pe.transpose(ps_pt[:, i * P:i * P + P], A[:, h, kt * P:kt * P + P], ident)
                        mm.then_inc(s["pt"], 1)
                    pe.wait_ge(s["ptc"], s.had("ptc") + PT0[u + 1])
                    if u:
                        pe.wait_ge(s["olo"], s.had("olo") + u)
                    v = (v_m, v_s, v_f)[br]
                    for h in range(H):
                        r = slice(64 * (h % 2), 64 * (h % 2) + 64)
                        for kt in range(qt + 1):
                            mm = pe.matmul(ps_o[r, h // 2, :], v[:, kt, h * HD:h * HD + HD],
                                           PT[:, h * (qt + 1) + kt, :], start=kt == 0, stop=kt == qt)
                    mm.then_inc(s["pv"], 1)

                norm_pe(0)
                project(0, h_hi, h_lo, "norm1")
                project(1, h_hi, h_lo)
                project(2, h_hi, h_lo)
                pe.wait_ge(s["cn"], s.had("cn") + 1)
                for k in range(3):
                    for tt in range(NT):
                        src = cq[:, tt, k * P:k * P + P] if k < 2 else ckv[:, tt, 0:KVL]
                        mm = pe.transpose(ps_norm[:, k, tt * P:tt * P + P], src, ident)
                mm.then_inc(s["cT"], 1)
                project(3, h_hi, h_lo)
                project(4, c_hi, c_lo, (s["clo"], 3))
                project(5, c_hi[:, 2:3, :], c_lo[:, 2:3, :])
                project(6, h_hi, h_lo)
                pe.wait_ge(s["rope"], s.had("rope") + 1)
                for n in range(6):
                    if n >= 3:
                        pe.wait_ge(s["mTc"], s.had("mTc") + n - 2)
                    for h in (2 * (n % 3), 2 * (n % 3) + 1):
                        for tt in range(NT):
                            src = q_tok[:, tt, h * MQK:h * MQK + MQK] if n < 3 else k_full[:, tt, h, :]
                            mm = pe.transpose(ps_score[0:MQK, h, tt * P:tt * P + P], src, ident)
                    mm.then_inc(s["mT"], 1)
                for j in range(7, 10):
                    project(j, h_hi, h_lo)
                pe.wait_ge(s["masks"], s.had("masks") + 16)
                pe.wait_ge(s["lf"], s.had("lf") + 1)
                pe.matmul(ps[:, 7, 0:FH], masks[:, M_TRIU:M_TRIU + P], lf[:, 0, :], start=True, stop=True)
                pe.matmul(ps[:, 7, 8:8 + FH], masks[:, M_TRIU + P:M_TRIU + 2 * P], lf[:, 0, :], start=True, stop=False)
                pe.matmul(ps[:, 7, 8:8 + FH], masks[:, M_TRIU:M_TRIU + P], lf[:, 1, :], start=False,
                          stop=True).then_inc(s["cum"], 1)
                pe.wait_ge(s["cumc"], s.had("cumc") + 1)
                for u in range(len(UNITS)):
                    scores(u)
                    project(10 + 2 * u, h_hi, h_lo)
                    project(11 + 2 * u, h_hi, h_lo)
                    pv(u)
                for j in range(J_WO, J_WO + 6):
                    br = (j - J_WO) % 3
                    project(j, o_hi[:, br], o_lo[:, br], (s["olo"], 6))
                for j in range(J_WOUT, J_WOUT + 4):
                    project(j, y_hi, y_lo, (s["ylo"], KD))
                norm_pe(1)
                pe.wait_ge(s["keys"], s.had("keys") + 16)
                for i in range(2):
                    mm = pe.transpose(ps_o[:, i, :], keys[:, i, :], ident)
                mm.then_inc(s["keyT"], 1)
                for j in range(J_WQ, NJ):
                    project(j, h_hi, h_lo, "norm2" if j == J_WQ else None)
                pe.wait_ge(s["keyTc"], s.had("keyTc") + 1)
                for b in range(NBANK):
                    pe.wait_ge(s["free"][b], s.had("free", b) + (FIRST[NJ] - b + NBANK - 1) // NBANK)
                for tt in range(NT):
                    for b in range(4):
                        for i in range(4):
                            n = 4 * b + i
                            mm = pe.matmul(ps[:, 4 * tt + b, i * P:i * P + P], pq[:, n, tt * P:tt * P + P],
                                           keysT[:, n % 2, :], start=True, stop=True)
                        mm.then_inc(s["sc"], 1)
                for tt in range(NT):
                    if tt == 0:
                        pe.wait_ge(s["scc"], s.had("scc") + NT)
                    else:
                        pe.wait_ge(s["slotTc"], s.had("slotTc") + tt)
                    pe.wait_ge(s["slot"], s.had("slot") + tt + 1)
                    for n in range(3):
                        mm = pe.transpose(ps[:, 2, n * P:n * P + P], slots[:, n, :], ident)
                    mm.then_inc(s["slotT"], 1)

                def weights(g, i, reuse):
                    pe.wait_ge(s["oh1"], s.had("oh1") + g + 1)
                    pe.wait_ge(s["oh2"], s.had("oh2") + g + 1)
                    if reuse:
                        pe.wait_ge(s["gc"], s.had("gc") + g - 1)
                    for t in range(4):
                        mm = pe.matmul(ps[:, i, t * P:t * P + P], oh2[i][:, t, :], oh1[i][:, t, :],
                                       start=True, stop=True)
                    mm.then_inc(s["g"], 1)

                weights(0, 0, False)
                weights(1, 1, False)
                with pe.Fori(1, 32) as n:
                    for i in range(2):
                        weights(2 * n + i, i, True)

                def transpose_block(c, i, n):
                    pe.wait_ge(s["landu"][i], s.had("landu", i) + 16 * n + 16)
                    for k in range(KD):
                        mm = pe.transpose(ps_ut[:, k * P:k * P + P], u_raw[i][:, k * P:k * P + P], ident)
                    mm.then_inc(s["ut"], 1)

                def activations(c, i, first=False):
                    pe.wait_ge(s["ulo"], s.had("ulo") + c + 1)
                    if not first:
                        pe.wait_ge(s["gelu"], s.had("gelu") + c - 1)
                    for k in range(KD):
                        e = slice(k * P, k * P + P)
                        mm = three(ps[:, 2 + i, 0:SEQ], u_hi[i][:, e], u_lo[i][:, e], h_hi[:, k, :], h_lo[:, k, :],
                                   k == 0, k == KD - 1)
                    mm.then_inc(s["s"], 1)

                def combine(c, i, start=False, stop=False):
                    pe.wait_ge(s["wl"], s.had("wl") + c + 1)
                    for tt in range(NT):
                        t = slice(tt * P, tt * P + P)
                        for hf in range(2):
                            o, d = ps[:, 4 + 2 * tt + hf, :], slice(512 * hf, 512 * hf + 512)
                            pe.matmul(o, w_hi[i][:, t], v_hi[i][:, d], start=start, stop=False)
                            pe.matmul(o, w_hi[i][:, t], v_lo[i][:, d], start=False, stop=False)
                        for hf in range(2):
                            o, d = ps[:, 4 + 2 * tt + hf, :], slice(512 * hf, 512 * hf + 512)
                            mm = pe.matmul(o, w_lo[i][:, t], v_hi[i][:, d], start=False, stop=stop)
                    mm.then_inc(s["v"], 1)

                pe.wait_ge(s["gc"], s.had("gc") + 64)
                transpose_block(0, 0, 0)
                pe.wait_ge(s["ulo"], s.had("ulo") + 1)
                transpose_block(1, 1, 0)
                activations(0, 0, first=True)
                pe.wait_ge(s["ulo"], s.had("ulo") + 2)
                transpose_block(2, 0, 1)
                activations(1, 1, first=True)
                combine(0, 0, start=True)
                with pe.Fori(1, NK // 2 - 1) as n:
                    for i in range(2):
                        c = 2 * n + i
                        pe.wait_ge(s["ulo"], s.had("ulo") + c + 1)
                        transpose_block(c + 1, 1 - i, n + i)
                        activations(c, i)
                        combine(c - 1, 1 - i)
                c = NK - 2
                pe.wait_ge(s["ulo"], s.had("ulo") + c + 1)
                transpose_block(c + 1, 1, NK // 2 - 1)
                activations(c, 0)
                combine(c - 1, 1)
                activations(c + 1, 1)
                combine(c, 0)
                combine(c + 1, 1, stop=True)

        @block.vector
        def _(dve):
            count = [0]

            def link(ins):
                count[0] += 1
                ins.then_inc(s_dve, 1)
                dve.wait_ge(s_dve, count[0])

            dve.wait_ge(s_boot, 16 * 9)
            link(dve.tensor_copy(pos[:, :], pos_i[:, :]))
            for tt in range(NT):
                ins = dve.tensor_scalar(ang[:, tt, :], cst[:, C_FREQ:C_END], pos[:, tt:tt + 1], None, ALU.mult)
            link(ins)
            link(dve.tensor_scalar(turns_i[:, :, :], ang[:, :, :], INV_SQRT2PI, None, ALU.mult))
            link(dve.tensor_copy(turns[:, :, :], turns_i[:, :, :]))
            for part in TWO_PI:
                link(dve.scalar_tensor_tensor(out=ang[:, :, :], in0=turns[:, :, :], scalar=-part, in1=ang[:, :, :],
                                              op0=ALU.mult, op1=ALU.add))
            dve.tensor_scalar(ang[:, :, :], ang[:, :, :], PI_IN, -PI_IN, ALU.min, ALU.max).then_inc(s_ang, 1)
            dve.wait_ge(s_sin, 2)
            link(dve.tensor_tensor(half_s[:, :, :], half_s[:, :, :], half_s[:, :, :], ALU.mult))
            link(dve.tensor_scalar(trig[:, :, 0, :], half_s[:, :, :], -2.0, 1.0, ALU.mult, ALU.add))

            for l in range(DEPTH):
                s = L[l]

                def split_lo(j):
                    dve.wait_ge(s["whi"], s.had("whi") + j + 1)
                    for rows, k0, k1 in parts(j):
                        ins = dve.tensor_tensor(chunk(wb_lo[j % 2], j)[0:rows, k0:k1, :],
                                                chunk(raw[j % NRAW], j)[0:rows, k0:k1, :],
                                                chunk(wb_hi[j % 2], j)[0:rows, k0:k1, :].bitcast(F32), ALU.subtract)
                    ins.then_inc(s["wlo"], 1)

                def norm_dve(which, gain):
                    dve.wait_ge(s["ss"], s.had("ss") + NT * (which + 1))
                    dve.tensor_scalar(msq[:, 0:NT], ssq[:, 0:NT], 1.0 / D, EPS, ALU.mult, ALU.add).then_inc(s["ms"], 1)
                    dve.wait_ge(s["rt"], s.had("rt") + which + 1)
                    link(dve.reciprocal(rstd[:, 0:NT], rms[:, 0:NT]))
                    for tt in range(NT):
                        ins = dve.tensor_scalar(xn[:, tt, :], x[:, tt, :], rstd[:, tt:tt + 1], None, ALU.mult)
                    ins.then_inc(s["xn"], 1)
                    for k in range(KD):
                        if k % 2 == 0:
                            dve.wait_ge(s["hhi"], s.had("hhi") + which * KD + k + 2)
                        c = gain(l, k)
                        dve.scalar_tensor_tensor(out=h_lo[:, k, :], in0=ps_norm[:, k, :], scalar=vecT[:, c:c + 1],
                                                 in1=h_hi[:, k, :].bitcast(F32), op0=ALU.mult,
                                                 op1=ALU.subtract).then_inc(s["hlo"], 1)

                def group(j, n):
                    g = FIRST[j] + n
                    dve.wait_ge(s["pj"], s.had("pj") + g + 1)
                    return g % NBANK

                def evac_tokens(j, dst):
                    for n, (tt, c0, m) in enumerate(GROUPS[j]):
                        b = group(j, n)
                        w = min(m, dst.shape[-1])
                        ins = dve.tensor_copy(dst[:, tt, c0:c0 + w], ps[:, b, 0:w])
                        ins.then_inc(s["free"][b], 1)
                    return ins

                def written(j):
                    for g in range(max(FIRST[j], FIRST[j + 1] - NBANK), FIRST[j + 1]):
                        dve.wait_ge(s["free"][g % NBANK], s.had("free", g % NBANK) + g // NBANK + 1)

                def evac_gates(j):
                    for n in range(2):
                        b = group(j, n)
                        k = 2 * (j - J_GATE[0]) + n
                        c = gb(l, k)
                        dve.tensor_scalar(gates[:, k, :], ps[:, b, 0:SEQ], vecT[:, c:c + 1], None,
                                          ALU.add).then_inc(s["free"][b], 1)

                def rotate(src, dst, tt, heads):
                    w = MROPE // 2
                    cos = trig[:, tt, 0, :].unsqueeze(1).to_broadcast([P, heads, w])
                    sin = trig[:, tt, 1, :].unsqueeze(1).to_broadcast([P, heads, w])
                    r = [rope_t[:, n, 0:heads, :] for n in range(4)]
                    dve.tensor_tensor(r[0], src[:, :, 0:w], cos, ALU.mult)
                    dve.tensor_tensor(r[1], src[:, :, w:2 * w], sin, ALU.mult)
                    dve.tensor_tensor(r[2], src[:, :, 0:w], sin, ALU.mult)
                    link(dve.tensor_tensor(r[3], src[:, :, w:2 * w], cos, ALU.mult))
                    dve.tensor_tensor(dst[:, :, 0:w], r[0], r[1], ALU.subtract)
                    link(dve.tensor_tensor(dst[:, :, w:2 * w], r[2], r[3], ALU.add))

                def softmax_dve(u, part):
                    br, qt = UNITS[u]
                    H, N = HEADS[br], P * (qt + 1)
                    m0 = P * (1 - qt)
                    Au, Bu, Cu = (t[:, 0:H, 0:N] for t in (A, B, C))
                    zu = ps_score[:, 0:H, 0:N]
                    if br == 1:
                        strict = masks[:, M_STRICT + m0:M_STRICT + 2 * P].unsqueeze(1).to_broadcast([P, H, N])
                        if part == 0:
                            dve.wait_ge(s["ab"], s.had("ab") + qt + 1)
                            link(dve.scalar_tensor_tensor(out=Bu, in0=zu, scalar=0.0, in1=Au, op0=ALU.max, op1=ALU.add))
                            link(dve.tensor_tensor(Cu, Bu, strict, ALU.mult))
                            for h in range(H):
                                dve.tensor_tensor_scan(A[:, h, 0:N], C[:, h, 0:N], C[:, h, 0:N], 0.0, ALU.add, ALU.max)
                            ins = dve.tensor_tensor(Bu, zu, Bu, ALU.subtract)
                            ins.then_inc(s["sfree"], 1)
                            dve.wait_ge(s["sfree"], s.had("sfree") + u + 1)
                            dve.tensor_tensor(Bu, Bu, Au, ALU.add)
                            dve.tensor_scalar(ntot[:, 0:H], A[:, 0:H, N - 1], -1.0, None, ALU.mult).then_inc(s["sb_w"], 1)
                        else:
                            dve.wait_ge(s["ex"], s.had("ex") + qt + 1)
                            dve.tensor_tensor(Au, Au, strict, ALU.mult).then_inc(s["probs"], 1)
                        return
                    base_ = M_MLA if br == 0 else M_FOX
                    allow = masks[:, base_ + m0:base_ + 2 * P]
                    if part == 0:
                        dve.wait_ge(s["score"], s.had("score") + u + 1)
                        if u:
                            dve.wait_ge(s["pt"], s.had("pt") + PT0[u])
                        if br == 0:
                            ins = dve.tensor_tensor(Au, zu, allow.unsqueeze(1).to_broadcast([P, H, N]), ALU.add)
                        else:
                            for h in range(H):
                                ins = dve.scalar_tensor_tensor(out=A[:, h, 0:N], in0=ps_score[:, h, 0:N],
                                                               scalar=cumq[:, qt, h:h + 1], in1=allow,
                                                               op0=ALU.add, op1=ALU.add)
                        ins.then_inc(s["sfree"], 1)
                        dve.wait_ge(s["sfree"], s.had("sfree") + u + 1)
                        link(dve.tensor_reduce(mx[:, 0:H], Au, AX.X, ALU.max))
                        dve.tensor_scalar(nmx[:, 0:H], mx[:, 0:H], -(SCALE_A if br == 0 else SCALE_H), None,
                                          ALU.mult).then_inc(s["pmax"], 1)
                    else:
                        dve.wait_ge(s["pexp"], s.had("pexp") + (u + 1 if br == 0 else u - 1))
                        link(dve.reciprocal(rsum[:, 0:H], esum[:, 0:H]))
                        dve.tensor_tensor(Au, Au, rsum[:, 0:H].unsqueeze(2).to_broadcast([P, H, N]),
                                          ALU.mult).then_inc(s["probs"], 1)

                def pv_dve(u):
                    br, qt = UNITS[u]
                    cols = slice(qt * P, (qt + 1) * P)
                    dve.wait_ge(s["ohi"], s.had("ohi") + u + 1)
                    pieces = [(P, 0, 3)] if HEADS[br] % 2 == 0 else [(P, 0, 2), (64, 2, 3)]
                    for r, a, b in pieces:
                        ins = dve.tensor_tensor(o_lo[0:r, br, a:b, cols], ps_o[0:r, a:b, :],
                                                o_hi[0:r, br, a:b, cols].bitcast(F32), ALU.subtract)
                    ins.then_inc(s["olo"], 1)

                norm_dve(0, g1)
                for j in range(2):
                    split_lo(j)
                evac_tokens(0, cq)
                evac_tokens(1, ckv)
                split_lo(2)
                dve.wait_ge(s["cms"], s.had("cms") + 1)
                dve.tensor_scalar(msq[:, 0:4:2], ssq[:, 0:4:2], 1.0 / QL, EPS, ALU.mult, ALU.add)
                dve.tensor_scalar(msq[:, 1:4:2], ssq[:, 1:4:2], 1.0 / KVL, EPS, ALU.mult, ALU.add).then_inc(s["cms"], 1)
                split_lo(3)
                dve.wait_ge(s["crt"], s.had("crt") + 1)
                link(dve.reciprocal(rstd[:, 0:4], rms[:, 0:4]))
                for tt in range(NT):
                    dve.tensor_scalar(cq[:, tt, :], cq[:, tt, :], rstd[:, 2 * tt:2 * tt + 1], None, ALU.mult)
                    ins = dve.tensor_scalar(ckv[:, tt, 0:KVL], ckv[:, tt, 0:KVL], rstd[:, 2 * tt + 1:2 * tt + 2],
                                            None, ALU.mult)
                ins.then_inc(s["cn"], 1)
                dve.wait_ge(s["chi"], s.had("chi") + 3)
                for k in range(3):
                    c = gq(l, k) if k < 2 else gkv(l)
                    dve.scalar_tensor_tensor(out=c_lo[:, k, :], in0=ps_norm[:, k, :], scalar=vecT[:, c:c + 1],
                                             in1=c_hi[:, k, :].bitcast(F32), op0=ALU.mult,
                                             op1=ALU.subtract).then_inc(s["clo"], 1)
                split_lo(4)
                split_lo(5)
                evac_tokens(4, q_tok)
                for n, (tt, c0, m) in enumerate(GROUPS[5]):
                    b = group(5, n)
                    h0 = c0 // (MNOPE + MV)
                    src = ps[:, b, 0:m].rearrange("p (h e) -> p h e", h=3)
                    dve.tensor_copy(k_full[:, tt, h0:h0 + 3, 0:MNOPE], src[:, :, 0:MNOPE])
                    ins = dve.tensor_copy(v_m[:, tt, h0 * MV:(h0 + 3) * MV].rearrange("p (h e) -> p h e", h=3),
                                          src[:, :, MNOPE:])
                    ins.then_inc(s["free"][b], 1)
                split_lo(6)
                split_lo(7)
                for tt in range(NT):
                    q3 = q_tok[:, tt, :].rearrange("p (h e) -> p h e", h=MH)[:, :, MNOPE:]
                    rotate(q3, q3, tt, MH)
                    kr = ckv[:, tt, KVL:KVL + MROPE].unsqueeze(1)
                    rotate(kr, kr, tt, 1)
                    ins = dve.tensor_copy(k_full[:, tt, :, MNOPE:], kr.to_broadcast([P, MH, MROPE]))
                ins.then_inc(s["rope"], 1)
                evac_tokens(6, v_s)
                split_lo(8)
                split_lo(9)
                evac_tokens(9, v_f)
                written(9)
                split_lo(10)
                f = v_f[:, :, W3:W3 + FH]
                link(dve.tensor_tensor(f, f, bf[:, l, :].unsqueeze(1).to_broadcast([P, NT, FH]), ALU.add))
                link(dve.tensor_scalar(nlf[:, :, :], f, -1.0, None, ALU.mult))
                dve.tensor_tensor(nlf[:, :, :], nlf[:, :, :], f, ALU.min).then_inc(s["fz"], 1)
                dve.wait_ge(s["fe"], s.had("fe") + 2)
                link(dve.scalar_tensor_tensor(out=lf[:, :, :], in0=f, scalar=0.0, in1=lf[:, :, :], op0=ALU.min,
                                              op1=ALU.subtract))
                link(dve.tensor_scalar(nlf[:, :, :], lf[:, :, :], -1.0 / SCALE_H, None, ALU.mult))
                dve.tensor_scalar(lf[:, :, :], lf[:, :, :], 1.0 / SCALE_H, None, ALU.mult).then_inc(s["lf"], 1)
                dve.wait_ge(s["cum"], s.had("cum") + 1)
                dve.tensor_copy(cumq[:, :, :], ps[:, 7, 0:16].rearrange("p (t h) -> p t h", t=NT)[:, :, 0:FH])\
                   .then_inc(s["cumc"], 1)
                dve.wait_ge(s["masks"], s.had("masks") + 16)
                for u in range(len(UNITS)):
                    split_lo(10 + 2 * u + 1)
                    softmax_dve(u, 0)
                    evac_gates(10 + 2 * u)
                    softmax_dve(u, 1)
                    evac_gates(11 + 2 * u)
                    split_lo(10 + 2 * u + 2)
                    pv_dve(u)
                for hf in range(2):
                    for br in range(3):
                        j = J_WO + 3 * hf + br
                        if j > J_WO:
                            split_lo(j)
                        dve.wait_ge(s["sig"], s.had("sig") + br + 1)
                        if hf == 1 and br == 0:
                            dve.wait_ge(s["yhi"], s.had("yhi") + 4)
                        for n in range(4):
                            b = group(j, n)
                            gt = gates[:, 8 * br + 4 * hf + n, :]
                            if br == 0:
                                dve.tensor_tensor(yacc[:, n, :], ps[:, b, 0:SEQ], gt, ALU.mult).then_inc(s["free"][b], 1)
                                continue
                            ins = dve.tensor_tensor(ytmp[:, n % 2, :], ps[:, b, 0:SEQ], gt, ALU.mult)
                            ins.then_inc(s["free"][b], 1)
                            g = FIRST[j] + n
                            dve.wait_ge(s["free"][b], s.had("free", b) + g // NBANK + 1)
                            ins = dve.tensor_tensor(yacc[:, n, :], yacc[:, n, :], ytmp[:, n % 2, :], ALU.add)
                            if br == 2:
                                ins.then_inc(s["yacc"], 1)
                    for n in range(4):
                        dve.wait_ge(s["yhi"], s.had("yhi") + 4 * hf + n + 1)
                        dve.tensor_tensor(y_lo[:, 4 * hf + n, :], yacc[:, n, :],
                                          y_hi[:, 4 * hf + n, :].bitcast(F32), ALU.subtract).then_inc(s["ylo"], 1)
                for j in range(J_WOUT, J_WOUT + 4):
                    split_lo(j)
                    c0 = 256 * (j - J_WOUT)
                    for n in range(NT):
                        b = group(j, n)
                        xs = x[:, n, c0:c0 + 256]
                        dve.tensor_tensor(xs, xs, ps[:, b, 0:256], ALU.add).then_inc(s["free"][b], 1)
                split_lo(J_WQ)
                norm_dve(1, g2)
                for j in range(J_WQ + 1, NJ):
                    split_lo(j)

                for tt in range(NT):
                    lists = [sc[:, tt, n * NK:n * NK + NK] for n in range(16)]
                    dve.wait_ge(s["scc"], s.had("scc") + tt + 1)

                    def top16(arrays, vals, idx):
                        for n, a in enumerate(arrays):
                            ins = dve.max(vals[:, n, 0:8], a)
                        link(ins)
                        for n, a in enumerate(arrays):
                            dve.max_index(idx[:, n, 0:8], vals[:, n, 0:8], a)
                        for n, a in enumerate(arrays):
                            ins = dve.match_replace(a, vals[:, n, 0:8], a, LOWEST)
                        link(ins)
                        for n, a in enumerate(arrays):
                            ins = dve.max(vals[:, n, 8:16], a)
                        link(ins)
                        for n, a in enumerate(arrays):
                            ins = dve.max_index(idx[:, n, 8:16], vals[:, n, 8:16], a)
                        link(ins)

                    top16(lists, vtop, itop)
                    link(dve.tensor_copy(itf[:, :, :], itop[:, :, :]))
                    v2 = vtop[:, :, :].rearrange("p (h s) a -> p h s a", s=2)
                    for a0, na, nb in SEGMENTS:
                        o = cand[:, :, STARTS[a0]:STARTS[a0] + na * nb]
                        if na == 1:
                            ins = dve.tensor_tensor(o, v2[:, :, 0, a0:a0 + 1].to_broadcast([P, PH, nb]),
                                                    v2[:, :, 1, 0:nb], ALU.add)
                        elif nb == 1:
                            ins = dve.tensor_tensor(o, v2[:, :, 0, a0:a0 + na],
                                                    v2[:, :, 1, 0:1].to_broadcast([P, PH, na]), ALU.add)
                        else:
                            ins = dve.tensor_tensor(
                                o.rearrange("p h (a b) -> p h a b", b=nb),
                                v2[:, :, 0, a0:a0 + na].unsqueeze(3).to_broadcast([P, PH, na, nb]),
                                v2[:, :, 1, 0:nb].unsqueeze(2).to_broadcast([P, PH, na, nb]), ALU.add)
                    link(ins)
                    top16([cand[:, h, :] for h in range(PH)], selv, selp)
                    link(dve.tensor_copy(posf[:, :], selp[:, :, :].rearrange("p h k -> p (h k)")))
                    dve.tensor_copy(gsum[:, 0, :], selv[:, :, 0])
                    link(dve.tensor_copy(gsum[:, 1, :], selv[:, :, 0]))
                    dve.tensor_tensor(selv[:, :, :], selv[:, :, :], gsum[:, 0, :].unsqueeze(2).to_broadcast([P, PH, 16]),
                                      ALU.subtract).then_inc(s["ge"], 1)
                    tmp = sc[:, tt, :].rearrange("p (n a) -> p n a", a=16)
                    tmp4 = sc[:, tt, :].rearrange("p (h n a) -> p h n a", h=PH, a=16)
                    i4 = itf[:, :, :].rearrange("p (h s) a -> p h s a", s=2)

                    def bc(c0):
                        return cst[:, c0:c0 + 16].unsqueeze(1).to_broadcast([P, P, 16])

                    def keys16(t):
                        return t.unsqueeze(2).to_broadcast([P, PH, 16, 16])

                    dve.tensor_copy(dtop[:, :, 0:1], i4[:, :, 0, 0:1])
                    link(dve.tensor_tensor(dtop[:, :, 1:16], i4[:, :, 0, 1:16], i4[:, :, 0, 0:15], ALU.subtract))
                    steps = posf[:, :].unsqueeze(2).to_broadcast([P, P, 16])
                    link(dve.tensor_tensor(tmp, steps, bc(C_START), ALU.is_ge))
                    link(dve.tensor_tensor(tmp4, tmp4, keys16(dtop[:, :, :]), ALU.mult))
                    if tt:
                        dve.wait_ge(s["slotT"], s.had("slotT") + tt)
                    link(dve.tensor_reduce(slots[:, 0, :], tmp, AX.X, ALU.add))
                    link(dve.tensor_tensor(tmp, steps, bc(C_START), ALU.is_ge))
                    link(dve.tensor_tensor(tmp, tmp, bc(C_DSTART), ALU.mult))
                    link(dve.tensor_reduce(sub[:, :], tmp, AX.X, ALU.add))
                    link(dve.tensor_tensor(posf[:, :], posf[:, :], sub[:, :], ALU.subtract))
                    link(dve.tensor_tensor(tmp, steps, bc(C_I16), ALU.is_equal))
                    link(dve.tensor_tensor(tmp4, tmp4, keys16(i4[:, :, 1, :]), ALU.mult))
                    link(dve.tensor_reduce(slots[:, 1, :], tmp, AX.X, ALU.add))
                    dve.wait_ge(s["gexp"], s.had("gexp") + tt + 1)
                    link(dve.tensor_reduce(gsum[:, 0, :], selv[:, :, :], AX.X, ALU.add))
                    link(dve.reciprocal(gsum[:, 1, :], gsum[:, 0, :]))
                    dve.tensor_tensor(slots[:, 2, :].rearrange("p (h k) -> p h k", h=PH), selv[:, :, :],
                                      gsum[:, 1, :].unsqueeze(2).to_broadcast([P, PH, 16]),
                                      ALU.mult).then_inc(s["slot"], 1)

                def one_hot(g, i, t0, reuse):
                    if reuse:
                        dve.wait_ge(s["g"], s.had("g") + g - 1)
                    for t in range(4):
                        ins = dve.tensor_scalar(oh1[i][:, t, :], iota, slotT[:, 0, bass.ds(t0 + t, 1)],
                                                slotT[:, 2, bass.ds(t0 + t, 1)], ALU.is_equal, ALU.mult)
                    ins.then_inc(s["oh1"], 1)

                dve.wait_ge(s["slotTc"], s.had("slotTc") + NT)
                one_hot(0, 0, 0, False)
                one_hot(1, 1, 4, False)
                with dve.Fori(1, 32) as n:
                    for i in range(2):
                        one_hot(2 * n + i, i, 8 * n + 4 * i, True)

                def u_split(c, i):
                    dve.wait_ge(s["uhi"], s.had("uhi") + c + 1)
                    dve.tensor_tensor(u_lo[i][:, :], ps_ut, u_hi[i][:, :].bitcast(F32), ALU.subtract)\
                       .then_inc(s["ulo"], 1)

                def cycle(c, i, last=False):
                    if not last:
                        u_split(c + 1, 1 - i)
                    dve.wait_ge(s["vhi"], s.had("vhi") + c + 1)
                    dve.tensor_tensor(v_lo[i][:, :], v_raw[i][:, :], v_hi[i][:, :].bitcast(F32), ALU.subtract)\
                       .then_inc(s["vlo"], 1)
                    dve.wait_ge(s["gelu"], s.had("gelu") + c + 1)
                    w1 = wgt[:, :].unsqueeze(2)
                    dve.tensor_tensor(w1, w1, G[:, :, bass.ds(c, 1)], ALU.mult).then_inc(s["w"], 1)
                    dve.wait_ge(s["wsp"], s.had("wsp") + c + 1)
                    dve.tensor_tensor(w_lo[i][:, :], wgt[:, :], w_hi[i][:, :].bitcast(F32), ALU.subtract)\
                       .then_inc(s["wl"], 1)

                u_split(0, 0)
                cycle(0, 0)
                cycle(1, 1)
                with dve.Fori(1, NK // 2 - 1) as n:
                    for i in range(2):
                        cycle(2 * n + i, i)
                cycle(NK - 2, 0)
                cycle(NK - 1, 1, last=True)
                dve.wait_ge(s["v"], s.had("v") + NK)
                for tt in range(NT):
                    for hf in range(2):
                        xs = x[:, tt, 512 * hf:512 * hf + 512]
                        dve.tensor_tensor(xs, xs, ps[:, 4 + 2 * tt + hf, :], ALU.add).then_inc(s["xnew"], 1)

            dve.wait_ge(s_fss, NT)
            dve.tensor_scalar(msq[:, 0:NT], ssq[:, 0:NT], 1.0 / D, EPS, ALU.mult, ALU.add).then_inc(s_fms, 1)
            dve.wait_ge(s_frt, 1)
            link(dve.reciprocal(rstd[:, 0:NT], rms[:, 0:NT]))
            dve.wait_ge(s_gain, 16)
            for tt in range(NT):
                dve.scalar_tensor_tensor(out=y_out[:, tt, :], in0=x[:, tt, :], scalar=rstd[:, tt:tt + 1],
                                         in1=gain_f[:, :], op0=ALU.mult, op1=ALU.mult).then_inc(s_y, 1)


def constants():
    c = np.zeros((P, C_END + M_END), np.float32)
    c[:, C_ID:C_ID + P] = np.eye(P)
    c[:, C_IOTA:C_IOTA + P] = np.arange(P)
    c[:, C_START:C_START + 16] = STARTS
    c[:, C_DSTART:C_DSTART + 16] = np.diff([0] + STARTS)
    c[:, C_I16:C_I16 + 16] = np.arange(16)
    c[:, C_FREQ:C_END] = np.float32(10000.0) ** (-np.arange(0, MROPE, 2, dtype=np.float32) / np.float32(MROPE))
    q, k = np.arange(P)[:, None], np.arange(P)[None, :]
    m = c[:, C_END:]
    m[:, M_MLA + P:M_MLA + 2 * P] = np.where(k // CHUNK <= q // CHUNK, 0.0, NEG)
    m[:, M_FOX + P:M_FOX + 2 * P] = np.where(k <= q, 0.0, NEG)
    m[:, M_STRICT:M_STRICT + P] = 1.0
    m[:, M_STRICT + P:M_STRICT + 2 * P] = k < q
    m[:, M_TRIU:M_TRIU + P] = q <= k
    m[:, M_TRIU + P:M_TRIU + 2 * P] = 1.0
    return c


_INS = ["x", "positions", "norm1_g", "w_in", "mla_q_norm_g", "w_uq", "mla_kv_norm_g", "w_ukv", "fox_b_f",
        "w_o_mla", "w_o_sb", "w_o_fox", "b_gate", "w_out", "norm2_g", "peer_w_q", "peer_sub_keys",
        "peer_u", "peer_v", "final_norm_g"]


def kernel(**inputs):
    import concourse.bacc as bacc
    from concourse.bass_utils import run_bass_kernel_spmd

    nc = bacc.Bacc("TRN2", target_bir_lowering=False, num_devices=1)
    arrays, t_in = {}, {}
    for name in _INS + ["consts"]:
        a = constants() if name == "consts" else np.ascontiguousarray(inputs[name])
        arrays[f"in_{name}"] = a
        t_in[name] = nc.dram_tensor(f"in_{name}", a.shape, mybir.dt.from_np(a.dtype), kind="ExternalInput").ap()
    out = nc.dram_tensor("out_y", (1, SEQ, D), F32, kind="ExternalOutput").ap()
    build(nc, t_in, out)
    r = run_bass_kernel_spmd(nc, [arrays], core_ids=[0])
    return r.results[0]["out_y"]
```

```python
from contextlib import ExitStack

import numpy as np

import concourse.bass as bass
from concourse import mybir

F32 = mybir.dt.float32
F32R = mybir.dt.float32r
I32 = mybir.dt.int32
U32 = mybir.dt.uint32
ALU = mybir.AluOpType
ACT = mybir.ActivationFunctionType
AX = mybir.AxisListType

P = 128
D = 1024
KD = D // P
SEQ = 256
NT = SEQ // P
DEPTH = 2
CHUNK = 64
HD = 64
EPS = 1e-6
NEG = -1e30
LOWEST = -3.0e38
MH, MNOPE, MROPE, MV = 6, 64, 32, 64
MQK = MNOPE + MROPE
QL, KVL = 256, 128
SH, FH = 5, 5
PH, NK, HALF, TOPK = 8, 128, 128, 16
NEXP = NK * NK
PACK = 2 * NK
W3 = SH * HD
GATES0 = QL + KVL + MROPE + 6 * W3 + FH
NG = 3 * D // P
SCALE_A = float(MQK) ** -0.5
SCALE_H = float(HD) ** -0.5
INV_SQRT2PI = float(1.0 / (2.0 * np.pi))
PI_IN = 3.1415925
TWO_PI = (6.28125, 0.0019350051879882812, 3.019915981956753e-07)

C_ID, C_IOTA, C_START, C_DSTART, C_I16, C_FREQ, C_END = 0, 128, 256, 272, 288, 304, 320
M_MLA, M_FOX, M_STRICT, M_TRIU, M_END = 0, 256, 512, 768, 1024

B_OF = [TOPK // (a + 1) for a in range(TOPK)]
STARTS = [sum(B_OF[:a]) for a in range(TOPK)]
NCAND = sum(B_OF)
SEGMENTS = [(0, 1, 16), (1, 1, 8), (2, 1, 5), (3, 1, 4), (4, 1, 3), (5, 3, 2), (8, 8, 1)]

JOBS = (
    [("cq", "w_in", 0, QL, KD, P, True), ("ckv", "w_in", QL, 256, KD, P, True)]
    + [("qs", "w_in", 416, W3, KD, P, False), ("ks", "w_in", 416 + W3, W3, KD, P, False)]
    + [("uq", "w_uq", 0, MH * MQK, 2, P, True), ("ukv", "w_ukv", 0, MH * (MNOPE + MV), 1, P, True)]
    + [("vs", "w_in", 416 + 2 * W3, W3, KD, P, True)]
    + [("qf", "w_in", 416 + 3 * W3, W3, KD, P, False), ("kf", "w_in", 416 + 4 * W3, W3, KD, P, False)]
    + [("vf", "w_in", 416 + 5 * W3, W3 + FH + 1, KD, P, True)]
    + [("gate", "w_in", GATES0 + 256 * n, 256, KD, P, False) for n in range(12)]
    + [(f"wo{br}", s, 512 * h, 512, 3, r, False) for h in range(2)
       for br, (s, r) in enumerate((("w_o_mla", P), ("w_o_sb", 64), ("w_o_fox", 64)))]
    + [("wout", "w_out", 256 * n, 256, KD, P, True) for n in range(4)]
    + [("wq", "peer_w_q", 256 * n, 256, KD, P, False) for n in range(8)]
)
NJ = len(JOBS)
J_GATE = [j for j, x in enumerate(JOBS) if x[0] == "gate"]
J_WO = J_GATE[-1] + 1
J_WOUT = J_WO + 6
J_WQ = J_WOUT + 4
SLOT = max(x[3] * x[4] for x in JOBS)
NRAW = 3


def groups_of(j):
    name, _, _, w, _, _, tokens = JOBS[j]
    if tokens:
        n = w // 2 if w > 512 or name == "uq" else w
        return [(tt, c, n) for tt in range(NT) for c in range(0, w, n)]
    return [(None, c, min(P, w - c)) for c in range(0, w, P)]


GROUPS = [groups_of(j) for j in range(NJ)]
FIRST = [sum(len(g) for g in GROUPS[:j]) for j in range(NJ + 1)]
NBANK = 3

HEADS = (MH, SH, FH)
UNITS = [(br, qt) for br in range(3) for qt in range(NT)]


def pt_batches(u):
    br, qt = UNITS[u]
    blocks = [(h, kt) for h in range(HEADS[br]) for kt in range(qt + 1)]
    return [blocks[n:n + 4] for n in range(0, len(blocks), 4)]


def pt_bank(u, n):
    return 6 + n % 2


PT0 = [sum(len(pt_batches(v)) for v in range(u)) for u in range(len(UNITS) + 1)]

def g1(l, k): return l * KD + k
def g2(l, k): return (DEPTH + l) * KD + k
def gb(l, n): return 2 * DEPTH * KD + l * NG + n
def gq(l, k): return 2 * DEPTH * KD + DEPTH * NG + 2 * l + k
def gkv(l): return 2 * DEPTH * KD + DEPTH * NG + 2 * DEPTH + l


NVEC = gkv(DEPTH)


NU = len(UNITS)
NGR = P // 4
SOLO = NGR // 2
MIXED = (NGR - SOLO) // 2
EXP_AT = SOLO // 2
PER_LAYER = {
    "masks": 16, "keys": 16,
    "whi": NJ, "wlo": NJ,
    "pj": FIRST[NJ],
    "ss": 2 * NT, "ms": 2, "rt": 2, "xn": 2,
    "xT": KD, "hhi": 2 * KD, "hlo": 2 * KD,
    "cms": 2, "crt": 1, "cn": 1, "cT": 1, "chi": 3, "clo": 3,
    "rope": 1, "mT": 6, "mTc": 6,
    "score": NU, "sfree": NU, "kz": 2,
    "ab": 2, "sb_w": 2, "ex": 2,
    "pmax": 4, "pexp": 4,
    "probs": NU, "pt": PT0[NU], "ptc": PT0[NU], "pv": NU,
    "ohi": NU, "olo": NU,
    "fz": 1, "fe": 2, "lf": 1, "cum": 1, "cumc": 1,
    "sig": 3, "yacc": KD, "yhi": KD, "ylo": KD,
    "keyT": 1, "keyTc": 1, "sc": 8, "scc": NT,
    "ge": NT, "gexp": NT, "slot": NT, "slotT": NT, "slotTc": NT,
    "nw": 1, "k2": NGR, "dist": NGR, "oh1": NGR, "oh2": NGR, "g": NGR, "gc": NGR,
    "oh1b": NGR, "oh2b": NGR, "gb": NGR, "gcb": NGR,
    "ut": NK, "uhi": NK, "ulo": NK, "s": NK, "gelu": NK,
    "w": NK, "wsp": NK, "wl": NK, "vhi": NK, "vlo": NK, "v": NK, "xnew": 4,
}


def build(nc, t_in, out):
    ctx = ExitStack()
    base = -(-nc.sbuf_base // 64) * 64

    def at(name, shape, off, dt=F32):
        return nc.alloc_sbuf_tensor_at(name, shape, dt, offset=base + off)

    def sem(name):
        return ctx.enter_context(nc.semaphore(name))

    with ctx:
        x = at("x", [P, NT, D], 0)
        h_hi = at("h_hi", [P, KD, SEQ], 8192, F32R)
        h_lo = at("h_lo", [P, KD, SEQ], 16384, F32R)
        cst = at("cst", [P, C_END], 24576)
        vecT = at("vecT", [P, 88], 25856)
        trig = at("trig", [P, NT, 2, 16], 26208)
        st = at("st", [P, 104], 26464)
        ident = cst[:, C_ID:C_ID + P]
        iota = cst[:, C_IOTA:C_IOTA + P]
        ssq, msq, rms, rstd = (st[:, 8 * n:8 * n + 4] for n in range(4))
        mx, nmx, esum, rsum, ntot = (st[:, 32 + 6 * n:38 + 6 * n] for n in range(5))
        lf = st[:, 62:72].rearrange("p (t h) -> p t h", t=NT)
        nlf = st[:, 72:82].rearrange("p (t h) -> p t h", t=NT)
        cumq = st[:, 82:92].rearrange("p (t h) -> p t h", t=NT)
        bf = st[:, 92:92 + DEPTH * FH].rearrange("p (l h) -> p l h", l=DEPTH)
        S0 = 26880
        u_raw = [at(f"u_raw{i}", [P, D], S0 + 4096 * i) for i in range(2)]
        v_raw = [at(f"v_raw{i}", [P, D], S0 + 8192 + 4096 * i) for i in range(2)]
        u_hi = [at(f"u_hi{i}", [P, D], S0 + 16384 + 4096 * i, F32R) for i in range(2)]
        u_lo = [at(f"u_lo{i}", [P, D], S0 + 24576 + 4096 * i, F32R) for i in range(2)]
        v_hi = [at(f"v_hi{i}", [P, D], S0 + 32768 + 4096 * i, F32R) for i in range(2)]
        v_lo = [at(f"v_lo{i}", [P, D], S0 + 40960 + 4096 * i, F32R) for i in range(2)]
        wgt = at("wgt", [P, SEQ], S0 + 49152)
        w_hi = [at(f"w_hi{i}", [P, SEQ], S0 + 50176 + 1024 * i, F32R) for i in range(2)]
        w_lo = [at(f"w_lo{i}", [P, SEQ], S0 + 52224 + 1024 * i, F32R) for i in range(2)]
        G = at("G", [P, SEQ, NK], S0 + 54272)
        R0 = S0 + 16384
        sc = at("sc", [P, NT, 16 * NK], R0)
        slotT = at("slotT", [P, 3, SEQ], R0 + 16384)
        oh1 = [at(f"oh1_{i}", [P, 4, NK], R0 + 19456 + 2048 * i) for i in range(2)]
        oh2 = [at(f"oh2_{i}", [P, 4, NK], R0 + 23552 + 2048 * i) for i in range(2)]
        vtop = at("vtop", [P, 16, 16], R0 + 27648)
        itop = at("itop", [P, 16, 16], R0 + 28672, U32)
        itf = at("itf", [P, 16, 16], R0 + 29696)
        cand = at("cand", [P, PH, NCAND], R0 + 30720)
        slots = at("slots", [P, 3, P], R0 + 32320)
        selv = at("selv", [P, PH, 16], R0 + 33856)
        selp = at("selp", [P, PH, 16], R0 + 34368, U32)
        posf = at("posf", [P, P], R0 + 34880)
        sub = at("sub", [P, P], R0 + 35392)
        dtop = at("dtop", [P, PH, 16], R0 + 35904)
        gsum = at("gsum", [P, 2, PH], R0 + 36416)
        key2 = [at(f"key2_{i}", [P, 4], R0 + 36480 + 32 * i) for i in range(2)]
        start_i = at("start_i", [P, P], R0 + 36544, I32)
        startf = at("startf", [P, P], R0 + 37056)
        dist = [at(f"dist{i}", [P, 4, NK], S0 + 12288 + 2048 * i) for i in range(2)]
        nweight = at("nweight", [P, P], S0 + 4096)
        oh1b = [at(f"oh1b_{i}", [P, 4, NK], R0 + 2048 * i) for i in range(2)]
        oh2b = [at(f"oh2b_{i}", [P, 4, NK], R0 + 4096 + 2048 * i) for i in range(2)]
        M0 = S0
        A = at("A", [P, MH, SEQ], M0)
        B = at("B", [P, MH, SEQ], M0 + 6144)
        k_full = at("k_full", [P, NT, MH, MQK], M0 + 6144)
        rope_t = at("rope_t", [P, 4, MH, 16], M0)
        PT = at("PT", [P, 12, P], M0 + 12288)
        raw = [at(f"raw{i}", [P, SLOT], M0 + 18432 + 4 * SLOT * i) for i in range(NRAW)]
        WH0 = M0 + 18432 + 4 * SLOT * NRAW
        wb_hi = [at(f"wb_hi{i}", [P, SLOT], WH0 + 4 * SLOT * i, F32R) for i in range(2)]
        wb_lo = [at(f"wb_lo{i}", [P, SLOT], WH0 + 4 * SLOT * (2 + i), F32R) for i in range(2)]
        Q0 = WH0 + 16 * SLOT
        gates = at("gates", [P, NG, SEQ], Q0)
        xn = at("xn", [P, NT, D], Q0)
        keys = at("keys", [P, 2, P], Q0 + 8192)
        keysT = at("keysT", [P, 2, P], Q0 + 9216)
        C = at("C", [P, MH, SEQ], Q0 + 24576)
        q_tok = at("q_tok", [P, NT, MH * MQK], Q0 + 24576)
        yacc = at("yacc", [P, 4, SEQ], Q0 + 24576)
        ytmp = at("ytmp", [P, 2, SEQ], Q0 + 28672)
        cq = at("cq", [P, NT, QL], Q0 + 30720)
        ckv = at("ckv", [P, NT, KVL + MROPE], Q0 + 32768)
        v_s = at("v_s", [P, NT, W3], Q0 + 34048)
        v_f = at("v_f", [P, NT, W3 + FH + 1], Q0 + 36608)
        X0 = Q0 + 39232
        qT = at("qT", [P, 2, 3, SEQ], X0)
        kT = at("kT", [P, 2, 5, SEQ], X0 + 6144)
        v_m = at("v_m", [P, NT, MH * MV], X0 + 16384)
        mqk = at("mqk", [P, 2, MH, SEQ], X0 + 19456)
        y_hi = at("y_hi", [P, KD, SEQ], X0, F32R)
        y_lo = at("y_lo", [P, KD, SEQ], X0 + 8192, F32R)
        O0 = X0 + 31744
        o_hi = at("o_hi", [P, 3, 3, SEQ], O0, F32R)
        o_lo = at("o_lo", [P, 3, 3, SEQ], O0 + 9216, F32R)
        c_hi = at("c_hi", [P, 3, SEQ], O0, F32R)
        c_lo = at("c_lo", [P, 3, SEQ], O0 + 3072, F32R)
        pq = at("pq", [P, 2 * PH, SEQ], O0)
        masks = at("masks", [P, M_END], O0 + 18432)
        vecs = at("vecs", [P, P], M0)
        pos_i = at("pos_i", [P, NT], M0 + 512, I32)
        pos = at("pos", [P, NT], M0 + 544)
        ang = at("ang", [P, NT, 16], M0 + 576)
        turns_i = at("turns_i", [P, NT, 16], M0 + 704, I32)
        turns = at("turns", [P, NT, 16], M0 + 832)
        half_s = at("half_s", [P, NT, 16], M0 + 960)
        gain_f = at("gain_f", [P, D], M0 + 1088)
        y_out = at("y_out", [P, NT, D], M0 + 8192)

        ps = ctx.enter_context(nc.psum_tensor("ps", [P, 8, 512], F32))
        ps_score = ps[:, 3:6, :].rearrange("p b (h k) -> p (b h) k", k=SEQ)
        ps_norm = ps[:, 3:7, :].rearrange("p b (h k) -> p (b h) k", k=SEQ)
        ps_o = ps[:, 7, :].rearrange("p (h k) -> p h k", k=P)
        ps_ut = ps[:, 0:2, :].rearrange("p b n -> p (b n)")

        s_boot = sem("s_boot")
        s_bootT = sem("s_bootT")
        s_vecT = sem("s_vecT")
        s_ang = sem("s_ang")
        s_sin = sem("s_sin")
        s_trig = sem("s_trig")
        s_dve = sem("s_dve")
        s_act = sem("s_act")
        s_gain = sem("s_gain")
        s_fss = sem("s_fss")
        s_frt = sem("s_frt")
        s_fms = sem("s_fms")
        s_y = sem("s_y")
        s_out = sem("s_out")

        landed, total = [], [0] * NRAW
        for j in range(NJ):
            total[j % NRAW] += 16 * (2 if JOBS[j][5] < P else 1)
            landed.append(total[j % NRAW])
        sems = {n: sem(f"s_{n}") for n in PER_LAYER}
        for n, k in (("land", NRAW), ("free", NBANK), ("landu", 2), ("landv", 2)):
            sems[n] = [sem(f"s_{n}{i}") for i in range(k)]

        class Layer:

            def __init__(self, l):
                self.l = l

            def __getitem__(self, name):
                return sems[name]

            def had(self, name, i=0):
                if name == "land":
                    return self.l * total[i]
                if name == "free":
                    return self.l * ((FIRST[NJ] - i + NBANK - 1) // NBANK)
                return self.l * (16 * NK // 2 if name in ("landu", "landv") else PER_LAYER[name])

        L = [Layer(l) for l in range(DEPTH)]

        def chunk(buf, j):
            return buf[:, 0:JOBS[j][3] * JOBS[j][4]].rearrange("p (k n) -> p k n", k=JOBS[j][4])

        def parts(j):
            k, r = JOBS[j][4], JOBS[j][5]
            return [(P, 0, k)] if r == P else [(P, 0, k - 1), (r, k - 1, k)]

        block = ctx.enter_context(nc.Block())

        @block.sync
        def _(sp):
            sp.dma_start(x[:, :, :], t_in["x"][0].rearrange("(t p) d -> p t d", p=P)).then_inc(s_boot, 16)
            sp.dma_start(cst[:, :], t_in["consts"][:, 0:C_END]).then_inc(s_boot, 16)
            for t, r0, n in (("norm1_g", g1(0, 0), DEPTH * KD), ("norm2_g", g2(0, 0), DEPTH * KD),
                             ("b_gate", gb(0, 0), DEPTH * NG), ("mla_q_norm_g", gq(0, 0), DEPTH * 2),
                             ("mla_kv_norm_g", gkv(0), DEPTH)):
                sp.dma_start(vecs[r0:r0 + n, :], t_in[t].rearrange("l (k p) -> (l k) p", p=P)).then_inc(s_boot, 16)
            sp.dma_start(pos_i[:, :], t_in["positions"][0].rearrange("(t p) -> p t", p=P),
                         allow_slow_non_contiguous=True).then_inc(s_boot, 16)
            sp.dma_start(st[:, 92:92 + DEPTH * FH], t_in["fox_b_f"].rearrange("l h -> (l h)").partition_broadcast(P)).then_inc(s_boot, 16)

            for l in range(DEPTH):
                s = L[l]
                if l:
                    sp.wait_ge(L[l - 1]["xnew"], L[l - 1].had("xnew") + 4)
                sp.dma_start(masks[:, :], t_in["consts"][:, C_END:C_END + M_END]).then_inc(s["masks"], 16)
                for j, (name, src, c0, w, kt, last, _) in enumerate(JOBS):
                    if j >= NRAW:
                        sp.wait_ge(s["wlo"], s.had("wlo") + j - NRAW + 1)
                    if name == "wq" and JOBS[j - 1][0] == "wout":
                        sp.wait_ge(s["ylo"], s.had("ylo") + KD)
                        sp.dma_start(keys[:, :, :], t_in["peer_sub_keys"][l].rearrange("s n c -> n s c")).then_inc(s["keys"], 16)
                    for rows, k0, k1 in parts(j):
                        sp.dma_start(chunk(raw[j % NRAW], j)[0:rows, k0:k1, :],
                                     t_in[src][l, k0 * P:(k1 - 1) * P + rows, c0:c0 + w].rearrange(
                                         "(k p) n -> p k n", p=rows)).then_inc(s["land"][j % NRAW], 16)
                sp.wait_ge(s["ylo"], s.had("ylo") + KD)

                def load_block(b, i):
                    sp.dma_start(u_raw[i][:, :], t_in["peer_u"][l, bass.ds(b * P, P), :]).then_inc(s["landu"][i], 16)

                def load_v(b, i):
                    sp.dma_start(v_raw[i][:, :], t_in["peer_v"][l, bass.ds(b * P, P), :]).then_inc(s["landv"][i], 16)

                load_block(0, 0)
                load_v(0, 0)
                sp.wait_ge(s["oh1"], s.had("oh1") + NGR)
                load_block(1, 1)
                load_v(1, 1)
                with sp.Fori(1, NK // 2) as n:
                    for i in range(2):
                        sp.wait_ge(s["ut"], s.had("ut") + 2 * n + (i - 1))
                        load_block(2 * n + i, i)
                        sp.wait_ge(s["vlo"], s.had("vlo") + 2 * n + (i - 1))
                        load_v(2 * n + i, i)

            sp.wait_ge(L[-1]["v"], L[-1].had("v") + NK)
            sp.dma_start(gain_f[:, :], t_in["final_norm_g"].partition_broadcast(P)).then_inc(s_gain, 16)
            for tt in range(NT):
                sp.wait_ge(s_y, tt + 1)
                sp.dma_start(out[0, tt * P:(tt + 1) * P, :], y_out[:, tt, :]).then_inc(s_out, 16)
            sp.wait_ge(s_out, 16 * NT)

        @block.gpsimd
        def _(pool):
            for l in range(DEPTH):
                s = L[l]
                if l:
                    pool.wait_ge(L[l - 1]["xnew"], L[l - 1].had("xnew") + 4)
                pool.memset(kT[HD:P, :, 0:4:2, :], 0.0).then_inc(s["kz"], 1)
                pool.memset(kT[0:HD, :, 1:4:2, :], 0.0).then_inc(s["kz"], 1)
                pool.wait_ge(s["slotTc"], s.had("slotTc") + 1)

                def take_keys(g, i):
                    pool.tensor_copy(key2[i][:, :], slotT[:, 1, bass.ds(4 * g, 4)]).then_inc(s["k2"], 1)

                def one_hot(g, i, first=False, last=False):
                    if not (first and i == 0):
                        pool.wait_ge(s["oh2"], s.had("oh2") + g)
                    if not first:
                        pool.wait_ge(s["g"], s.had("g") + g - 1)
                    pool.wait_ge(s["k2"], s.had("k2") + g + 1)
                    if not last:
                        take_keys(g + 1, 1 - i)
                    for t in range(4):
                        ins = pool.tensor_scalar(oh2[i][:, t, :], iota, key2[i][:, t:t + 1], None, ALU.is_equal)
                    ins.then_inc(s["oh2"], 1)

                take_keys(0, 0)
                one_hot(0, 0, first=True)
                one_hot(1, 1, first=True)
                with pool.Fori(1, NGR // 2 - 1) as n:
                    for i in range(2):
                        one_hot(2 * n + i, i)
                one_hot(NGR - 2, 0)
                one_hot(NGR - 1, 1, last=True)

        @block.scalar
        def _(act):
            count = [0]

            def link(ins):
                count[0] += 1
                ins.then_inc(s_act, 1)
                act.wait_ge(s_act, count[0])

            act.wait_ge(s_bootT, 1)
            act.activation(vecT[:, 0:NVEC], ps[:, 0, 0:NVEC], ACT.Copy).then_inc(s_vecT, 1)
            act.wait_ge(s_ang, 1)
            act.activation(trig[:, :, 1, :], ang[:, :, :], ACT.Sin).then_inc(s_sin, 1)
            act.activation(half_s[:, :, :], ang[:, :, :], ACT.Sin, scale=0.5).then_inc(s_sin, 1)

            for l in range(DEPTH):
                s = L[l]

                def split_hi(j):
                    act.wait_ge(s["land"][j % NRAW], s.had("land", j % NRAW) + landed[j])
                    if j >= 2:
                        act.wait_ge(s["pj"], s.had("pj") + FIRST[j - 1])
                    ps_ = parts(j)
                    for rows, k0, k1 in ps_:
                        ins = act.activation(chunk(wb_hi[j % 2], j)[0:rows, k0:k1, :],
                                             chunk(raw[j % NRAW], j)[0:rows, k0:k1, :], ACT.Copy)
                    ins.then_inc(s["whi"], 1)

                def evac(j, n):
                    name = JOBS[j][0]
                    g = FIRST[j] + n
                    _, c0, rows = GROUPS[j][n]
                    act.wait_ge(s["pj"], s.had("pj") + g + 1)
                    src = ps[0:rows, g % NBANK, 0:SEQ]
                    if name == "wq":
                        ins = act.activation(pq[:, 2 * (j - J_WQ) + n, :], src, ACT.Copy)
                    elif name in ("qs", "qf"):
                        ins = act.activation(qT[0:rows, int(name == "qf"), n, :], src, ACT.Copy,
                                             scale=SCALE_H if name == "qs" else 1.0)
                    else:
                        for r in range(0, rows, HD):
                            ins = act.activation(kT[r:r + HD, int(name == "kf"), 2 * n + r // HD, :],
                                                 ps[r:r + HD, g % NBANK, 0:SEQ], ACT.Copy)
                    ins.then_inc(s["free"][g % NBANK], 1)

                def evacuated(j):
                    for g in range(FIRST[j + 1] - NBANK, FIRST[j + 1]):
                        act.wait_ge(s["free"][g % NBANK], s.had("free", g % NBANK) + g // NBANK + 1)

                def norm_act(which, gain):
                    if which == 0 and l:
                        act.wait_ge(L[l - 1]["xnew"], L[l - 1].had("xnew") + 4)
                    if which == 0 and l == 0:
                        act.wait_ge(s_boot, 16 * 9)
                    if which == 1:
                        evacuated(J_WQ - 1)
                    for tt in range(NT):
                        act.activation(xn[:, tt, :], x[:, tt, :], ACT.Square,
                                       accum_out=ssq[:, tt:tt + 1]).then_inc(s["ss"], 1)
                    act.wait_ge(s["ms"], s.had("ms") + which + 1)
                    act.activation(rms[:, 0:NT], msq[:, 0:NT], ACT.Sqrt).then_inc(s["rt"], 1)
                    for k in range(KD):
                        if k % 2 == 0:
                            act.wait_ge(s["xT"], s.had("xT") + (which * KD + k) // 2 + 1)
                        act.activation(h_hi[:, k, :], ps_norm[:, k, :], ACT.Copy,
                                       scale=vecT[:, gain(l, k):gain(l, k) + 1]).then_inc(s["hhi"], 1)

                def evac_gates(j):
                    for n in range(2):
                        g = FIRST[j] + n
                        k = 2 * (j - J_GATE[0]) + n
                        c = gb(l, k)
                        act.wait_ge(s["pj"], s.had("pj") + g + 1)
                        act.activation(gates[:, k, :], ps[:, g % NBANK, 0:SEQ], ACT.Identity,
                                       bias=vecT[:, c:c + 1]).then_inc(s["free"][g % NBANK], 1)

                def stick_act(u):
                    br, qt = UNITS[u]
                    H, N = HEADS[br], P * (qt + 1)
                    if br != 1:
                        return
                    act.wait_ge(s["score"], s.had("score") + u + 1)
                    act.wait_ge(s["pt"], s.had("pt") + PT0[u])
                    z = ps_score[:, 0:H, 0:N]
                    link(act.activation(A[:, 0:H, 0:N], z, ACT.Abs))
                    link(act.activation(A[:, 0:H, 0:N], A[:, 0:H, 0:N], ACT.Exp, scale=-1.0))
                    act.activation(A[:, 0:H, 0:N], A[:, 0:H, 0:N], ACT.Ln, bias=1.0).then_inc(s["ab"], 1)

                def exp_act(u):
                    br, qt = UNITS[u]
                    H, N = HEADS[br], P * (qt + 1)
                    if br == 1:
                        act.wait_ge(s["sb_w"], s.had("sb_w") + qt + 1)
                        for h in range(H):
                            ins = act.activation(A[:, h, 0:N], B[:, h, 0:N], ACT.Exp, bias=ntot[:, h:h + 1])
                        ins.then_inc(s["ex"], 1)
                        return
                    act.wait_ge(s["pmax"], s.had("pmax") + (u + 1 if br == 0 else u - 1))
                    for h in range(H):
                        ins = act.activation(A[:, h, 0:N], A[:, h, 0:N], ACT.Exp, bias=nmx[:, h:h + 1],
                                             scale=SCALE_A if br == 0 else SCALE_H,
                                             accum_out=esum[:, h:h + 1])
                    ins.then_inc(s["pexp"], 1)

                def copy_probs(u):
                    if u:
                        act.wait_ge(s["pv"], s.had("pv") + u)
                    at_ = 0
                    for n, batch in enumerate(pt_batches(u)):
                        act.wait_ge(s["pt"], s.had("pt") + PT0[u] + n + 1)
                        m = len(batch)
                        act.activation(PT[:, at_:at_ + m, :],
                                       ps[:, pt_bank(u, n), 0:m * P].rearrange("p (m k) -> p m k", k=P),
                                       ACT.Copy).then_inc(s["ptc"], 1)
                        at_ += m

                def pv_act(u):
                    br, qt = UNITS[u]
                    act.wait_ge(s["pv"], s.had("pv") + u + 1)
                    cols = slice(qt * P, (qt + 1) * P)
                    if HEADS[br] % 2 == 0:
                        ins = act.activation(o_hi[:, br, :, cols], ps_o[:, 0:3, :], ACT.Copy)
                    else:
                        act.activation(o_hi[:, br, 0:2, cols], ps_o[:, 0:2, :], ACT.Copy)
                        ins = act.activation(o_hi[0:64, br, 2, cols], ps_o[0:64, 2, :], ACT.Copy)
                    ins.then_inc(s["ohi"], 1)

                norm_act(0, g1)
                for j in range(3):
                    split_hi(j)
                evacuated(1)
                for tt in range(NT):
                    act.activation(C[:, tt, :], cq[:, tt, :], ACT.Square, accum_out=ssq[:, 2 * tt:2 * tt + 1])
                    ins = act.activation(C[:, 2 + tt, 0:KVL], ckv[:, tt, 0:KVL], ACT.Square,
                                         accum_out=ssq[:, 2 * tt + 1:2 * tt + 2])
                ins.then_inc(s["cms"], 1)
                act.wait_ge(s["cms"], s.had("cms") + 2)
                act.activation(rms[:, 0:4], msq[:, 0:4], ACT.Sqrt).then_inc(s["crt"], 1)
                split_hi(3)
                for n in range(3):
                    evac(2, n)
                act.wait_ge(s["cT"], s.had("cT") + 1)
                for k in range(3):
                    c = gq(l, k) if k < 2 else gkv(l)
                    act.activation(c_hi[:, k, :], ps_norm[:, k, :], ACT.Copy, scale=vecT[:, c:c + 1]).then_inc(s["chi"], 1)
                split_hi(4)
                for n in range(3):
                    evac(3, n)
                split_hi(5)
                split_hi(6)
                split_hi(7)
                for n in range(6):
                    act.wait_ge(s["mT"], s.had("mT") + n + 1)
                    act.activation(mqk[0:MQK, n // 3, 2 * (n % 3):2 * (n % 3) + 2, :],
                                   ps_score[0:MQK, 2 * (n % 3):2 * (n % 3) + 2, :], ACT.Copy).then_inc(s["mTc"], 1)
                split_hi(8)
                for n in range(3):
                    evac(7, n)
                split_hi(9)
                for n in range(3):
                    evac(8, n)
                split_hi(10)
                act.wait_ge(s["fz"], s.had("fz") + 1)
                act.activation(lf[:, :, :], nlf[:, :, :], ACT.Exp, scale=1.0).then_inc(s["fe"], 1)
                act.wait_ge(s["fe"], s.had("fe") + 1)
                act.activation(lf[:, :, :], lf[:, :, :], ACT.Ln, bias=1.0).then_inc(s["fe"], 1)
                for u in range(NU):
                    exp_act(u)
                    split_hi(11 + 2 * u)
                    evac_gates(10 + 2 * u)
                    split_hi(12 + 2 * u)
                    copy_probs(u)
                    if u + 1 < NU:
                        stick_act(u + 1)
                    evac_gates(11 + 2 * u)
                    if u + 1 == NU:
                        evacuated(J_WO - 1)
                        for br in range(3):
                            act.activation(gates[:, 8 * br:8 * br + 8, :], gates[:, 8 * br:8 * br + 8, :],
                                           ACT.Sigmoid).then_inc(s["sig"], 1)
                            if br == 0:
                                pv_act(u)
                    else:
                        pv_act(u)
                for j in range(J_WO + 1, J_WO + 6):
                    split_hi(j)
                    if j == J_WO + 3:
                        for n in range(4):
                            act.wait_ge(s["yacc"], s.had("yacc") + n + 1)
                            act.activation(y_hi[:, n, :], yacc[:, n, :], ACT.Copy).then_inc(s["yhi"], 1)
                split_hi(J_WOUT)
                for n in range(4):
                    act.wait_ge(s["yacc"], s.had("yacc") + 4 + n + 1)
                    act.activation(y_hi[:, 4 + n, :], yacc[:, n, :], ACT.Copy).then_inc(s["yhi"], 1)
                for j in range(J_WOUT + 1, J_WQ + 1):
                    split_hi(j)
                norm_act(1, g2)
                act.wait_ge(s["keyT"], s.had("keyT") + 1)
                act.activation(keysT[:, :, :], ps_o[:, 0:2, :], ACT.Copy).then_inc(s["keyTc"], 1)
                for j in range(J_WQ, NJ):
                    if j + 1 < NJ:
                        split_hi(j + 1)
                    for n in range(2):
                        evac(j, n)
                for tt in range(NT):
                    for b in range(4):
                        act.wait_ge(s["sc"], s.had("sc") + 4 * tt + b + 1)
                        ins = act.activation(sc[:, tt, 512 * b:512 * b + 512], ps[:, 4 * tt + b, :], ACT.Copy)
                    ins.then_inc(s["scc"], 1)
                def selected(tt):
                    act.wait_ge(s["ge"], s.had("ge") + tt + 1)
                    act.activation(selv[:, :, :], selv[:, :, :], ACT.Exp).then_inc(s["gexp"], 1)

                def slots_in(tt):
                    act.wait_ge(s["slotT"], s.had("slotT") + tt + 1)
                    act.activation(slotT[:, :, tt * P:tt * P + P],
                                   ps[:, 2, 0:3 * P].rearrange("p (n t) -> p n t", n=3), ACT.Copy).then_inc(s["slotTc"], 1)

                def distances(g, i):
                    for t in range(4):
                        ins = act.activation(dist[i][:, t, :], iota, ACT.Abs, scale=-1.0,
                                             bias=slotT[:, 0, bass.ds(4 * g + t, 1)])
                    ins.then_inc(s["dist"], 1)

                def copy_a(g, i):
                    act.wait_ge(s["g"], s.had("g") + g + 1)
                    act.activation(G[:, bass.ds(4 * g, 4), :],
                                   ps[:, i, :].rearrange("p (t k) -> p t k", t=4), ACT.Copy).then_inc(s["gc"], 1)

                def copy_b(g, i):
                    act.wait_ge(s["gb"], s.had("gb") + g + 1)
                    act.activation(G[:, bass.ds(4 * g + P, 4), :],
                                   ps[:, 4 + i, :].rearrange("p (t k) -> p t k", t=4), ACT.Copy).then_inc(s["gcb"], 1)

                def first_keys(g, i, first=False, last=False):
                    if not last:
                        if not (first and i == 0):
                            act.wait_ge(s["oh1"], s.had("oh1") + g)
                        distances(g + 1, 1 - i)
                    act.wait_ge(s["dist"], s.had("dist") + g + 1)
                    if not first:
                        act.wait_ge(s["g"], s.had("g") + g - 1)
                    for t in range(4):
                        ins = act.activation(oh1[i][:, t, :], dist[i][:, t, :], ACT.Relu,
                                             scale=nweight[:, bass.ds(4 * g + t, 1)],
                                             bias=slotT[:, 2, bass.ds(4 * g + t, 1)])
                    ins.then_inc(s["oh1"], 1)
                    if not (first and i == 0):
                        copy_a(g - 1, 1 - i)

                selected(0)
                slots_in(0)
                act.wait_ge(s["slotTc"], s.had("slotTc") + 1)
                act.activation(nweight[:, :], slotT[:, 2, 0:P], ACT.Copy, scale=-1.0).then_inc(s["nw"], 1)
                distances(0, 0)
                act.wait_ge(s["nw"], s.had("nw") + 1)
                first_keys(0, 0, first=True)
                first_keys(1, 1, first=True)
                with act.Fori(1, EXP_AT // 2) as n:
                    for i in range(2):
                        first_keys(2 * n + i, i)
                selected(1)
                with act.Fori(EXP_AT // 2, SOLO // 2) as n:
                    for i in range(2):
                        first_keys(2 * n + i, i)
                slots_in(1)
                first_keys(SOLO, 0)
                with act.Fori(0, MIXED - 1) as n:
                    for i in range(2):
                        first_keys(2 * n + (i + SOLO + 1), 1 - i)
                        for h in range(2):
                            copy_b(4 * n + (2 * i + h), 2 * i + h)
                first_keys(NGR - 1, 1, last=True)
                for i in range(4):
                    copy_b(NGR - 4 + i, i)
                copy_a(NGR - 1, 1)

                def u_split(c, i):
                    act.wait_ge(s["ut"], s.had("ut") + c + 1)
                    act.activation(u_hi[i][:, :], ps_ut, ACT.Copy).then_inc(s["uhi"], 1)

                def cycle(c, i, first=False, last=False, n=None):
                    if not last:
                        if not (first and i == 0):
                            act.wait_ge(s["s"], s.had("s") + c)
                        u_split(c + 1, 1 - i)
                    act.wait_ge(s["landv"][i], s.had("landv", i) + 16 * n + 16)
                    if not first:
                        act.wait_ge(s["v"], s.had("v") + c - 1)
                    act.activation(v_hi[i][:, :], v_raw[i][:, :], ACT.Copy).then_inc(s["vhi"], 1)
                    act.wait_ge(s["s"], s.had("s") + c + 1)
                    if not (first and i == 0):
                        act.wait_ge(s["wl"], s.had("wl") + c)
                    act.activation(wgt[:, :], ps[:, 2 + i, 0:SEQ], ACT.Gelu).then_inc(s["gelu"], 1)
                    act.wait_ge(s["w"], s.had("w") + c + 1)
                    act.activation(w_hi[i][:, :], wgt[:, :], ACT.Copy).then_inc(s["wsp"], 1)

                u_split(0, 0)
                cycle(0, 0, first=True, n=0)
                cycle(1, 1, first=True, n=0)
                with act.Fori(1, NK // 2 - 1) as n:
                    for i in range(2):
                        cycle(2 * n + i, i, n=n)
                cycle(NK - 2, 0, n=NK // 2 - 1)
                cycle(NK - 1, 1, last=True, n=NK // 2 - 1)

            act.wait_ge(L[-1]["xnew"], L[-1].had("xnew") + 4)
            for tt in range(NT):
                act.activation(y_out[:, tt, :], x[:, tt, :], ACT.Square, accum_out=ssq[:, tt:tt + 1]).then_inc(s_fss, 1)
            act.wait_ge(s_fms, 1)
            act.activation(rms[:, 0:NT], msq[:, 0:NT], ACT.Sqrt).then_inc(s_frt, 1)

        @block.tensor
        def _(pe):
            pe.wait_ge(s_boot, 16 * 9)
            pe.transpose(ps[:, 0, 0:NVEC], vecs[0:NVEC, :], ident[0:NVEC, 0:NVEC]).then_inc(s_bootT, 1)
            pe.wait_ge(s_vecT, 1)

            def three(out_, a_hi, a_lo, b_hi, b_lo, start, stop):
                pe.matmul(out_, a_hi, b_hi, start=start, stop=False)
                pe.matmul(out_, a_hi, b_lo, start=False, stop=False)
                return pe.matmul(out_, a_lo, b_hi, start=False, stop=stop)

            for l in range(DEPTH):
                s = L[l]
                def project(j, a_hi, a_lo, ready=None):
                    name, _, _, w, kt, last, tokens = JOBS[j]
                    pe.wait_ge(s["wlo"], s.had("wlo") + j + 1)
                    whi, wlo = chunk(wb_hi[j % 2], j), chunk(wb_lo[j % 2], j)
                    for n, (tt, c0, m) in enumerate(GROUPS[j]):
                        g = FIRST[j] + n
                        b = g % NBANK
                        if g >= NBANK:
                            pe.wait_ge(s["free"][b], s.had("free", b) + g // NBANK)
                        if ready is not None and n == 0 and not isinstance(ready, str):
                            pe.wait_ge(*ready)
                        for k in range(kt):
                            if ready == "norm1" and n == 0:
                                pe.wait_ge(s["hlo"], s.had("hlo") + k + 1)
                            if ready == "norm2" and n == 0:
                                pe.wait_ge(s["hlo"], s.had("hlo") + KD + k + 1)
                            r = P if k < kt - 1 else last
                            edge = dict(start=k == 0, stop=k == kt - 1)
                            if tokens:
                                t = slice(tt * P, tt * P + P)
                                mm = three(ps[:, b, 0:m], a_hi[:, k, t], a_lo[:, k, t],
                                           whi[:, k, c0:c0 + m], wlo[:, k, c0:c0 + m], **edge)
                            else:
                                mm = three(ps[0:m, b, 0:SEQ], whi[0:r, k, c0:c0 + m], wlo[0:r, k, c0:c0 + m],
                                           a_hi[0:r, k, :], a_lo[0:r, k, :], **edge)
                        mm.then_inc(s["pj"], 1)

                def norm_pe(which):
                    pe.wait_ge(s["xn"], s.had("xn") + which + 1)
                    for k in range(KD):
                        for tt in range(NT):
                            mm = pe.transpose(ps_norm[:, k, tt * P:tt * P + P], xn[:, tt, k * P:k * P + P], ident)
                        if k % 2:
                            mm.then_inc(s["xT"], 1)

                def scores(u):
                    br, qt = UNITS[u]
                    N = P * (qt + 1)
                    q = slice(qt * P, qt * P + P)
                    if u:
                        pe.wait_ge(s["sfree"], s.had("sfree") + u)
                    if u == 0:
                        pe.wait_ge(s["mTc"], s.had("mTc") + 6)
                    if u == NT:
                        pe.wait_ge(s["kz"], s.had("kz") + 2)
                    for h in range(HEADS[br]):
                        o = ps_score[:, h, 0:N]
                        if br == 0:
                            mm = pe.matmul(o, mqk[0:MQK, 0, h, q], mqk[0:MQK, 1, h, 0:N], start=True, stop=True)
                            continue
                        r = P if h < 4 else HD
                        mm = pe.matmul(o, qT[0:r, br - 1, h // 2, q], kT[0:r, br - 1, h, 0:N], start=True, stop=br == 1)
                        if br == 2:
                            mm = pe.matmul(o, nlf[:, 0, h:h + 1].to_broadcast([P, P]),
                                           masks[:, M_TRIU:M_TRIU + N], start=False, stop=qt == 0)
                            if qt == 1:
                                mm = pe.matmul(ps_score[:, h, P:N], nlf[:, 1, h:h + 1].to_broadcast([P, P]),
                                               masks[:, M_TRIU:M_TRIU + P], start=False, stop=True)
                    mm.then_inc(s["score"], 1)

                def transpose_probs(u):
                    pe.wait_ge(s["probs"], s.had("probs") + u + 1)
                    if u:
                        pe.wait_ge(s["olo"], s.had("olo") + u)
                    else:
                        pe.wait_ge(s["cumc"], s.had("cumc") + 1)
                    for n, batch in enumerate(pt_batches(u)):
                        if PT0[u] + n > 1:
                            pe.wait_ge(s["ptc"], s.had("ptc") + PT0[u] + n - 1)
                        for i, (h, kt) in enumerate(batch):
                            mm = pe.transpose(ps[:, pt_bank(u, n), i * P:i * P + P], A[:, h, kt * P:kt * P + P], ident)
                        mm.then_inc(s["pt"], 1)

                def pv(u):
                    br, qt = UNITS[u]
                    H = HEADS[br]
                    pe.wait_ge(s["ptc"], s.had("ptc") + PT0[u + 1])
                    v = (v_m, v_s, v_f)[br]
                    for h in range(H):
                        r = slice(64 * (h % 2), 64 * (h % 2) + 64)
                        for kt in range(qt + 1):
                            mm = pe.matmul(ps_o[r, h // 2, :], v[:, kt, h * HD:h * HD + HD],
                                           PT[:, h * (qt + 1) + kt, :], start=kt == 0, stop=kt == qt)
                    mm.then_inc(s["pv"], 1)

                norm_pe(0)
                project(0, h_hi, h_lo, "norm1")
                project(1, h_hi, h_lo)
                project(2, h_hi, h_lo)
                pe.wait_ge(s["cn"], s.had("cn") + 1)
                for k in range(3):
                    for tt in range(NT):
                        src = cq[:, tt, k * P:k * P + P] if k < 2 else ckv[:, tt, 0:KVL]
                        mm = pe.transpose(ps_norm[:, k, tt * P:tt * P + P], src, ident)
                mm.then_inc(s["cT"], 1)
                project(3, h_hi, h_lo)
                project(4, c_hi, c_lo, (s["clo"], s.had("clo") + 3))
                project(5, c_hi[:, 2:3, :], c_lo[:, 2:3, :])
                project(6, h_hi, h_lo)
                pe.wait_ge(s["rope"], s.had("rope") + 1)
                for n in range(6):
                    if n >= 3:
                        pe.wait_ge(s["mTc"], s.had("mTc") + n - 2)
                    for h in (2 * (n % 3), 2 * (n % 3) + 1):
                        for tt in range(NT):
                            src = q_tok[:, tt, h * MQK:h * MQK + MQK] if n < 3 else k_full[:, tt, h, :]
                            mm = pe.transpose(ps_score[0:MQK, h, tt * P:tt * P + P], src, ident)
                    mm.then_inc(s["mT"], 1)
                for j in range(7, 10):
                    project(j, h_hi, h_lo)
                pe.wait_ge(s["masks"], s.had("masks") + 16)
                scores(0)
                for u in range(NU):
                    project(10 + 2 * u, h_hi, h_lo)
                    if u == 0:
                        pe.wait_ge(s["lf"], s.had("lf") + 1)
                        pe.matmul(ps[:, 7, 0:FH], masks[:, M_TRIU:M_TRIU + P], lf[:, 0, :], start=True, stop=True)
                        pe.matmul(ps[:, 7, 8:8 + FH], masks[:, M_TRIU + P:M_TRIU + 2 * P], lf[:, 0, :], start=True,
                                  stop=False)
                        pe.matmul(ps[:, 7, 8:8 + FH], masks[:, M_TRIU:M_TRIU + P], lf[:, 1, :], start=False,
                                  stop=True).then_inc(s["cum"], 1)
                    transpose_probs(u)
                    if u + 1 < NU:
                        scores(u + 1)
                    project(11 + 2 * u, h_hi, h_lo)
                    pv(u)
                for j in range(J_WO, J_WO + 6):
                    br = (j - J_WO) % 3
                    project(j, o_hi[:, br], o_lo[:, br], (s["olo"], s.had("olo") + NU))
                for j in range(J_WOUT, J_WOUT + 4):
                    project(j, y_hi, y_lo, (s["ylo"], s.had("ylo") + KD))
                norm_pe(1)
                pe.wait_ge(s["keys"], s.had("keys") + 16)
                for i in range(2):
                    mm = pe.transpose(ps_o[:, i, :], keys[:, i, :], ident)
                mm.then_inc(s["keyT"], 1)
                for j in range(J_WQ, NJ):
                    project(j, h_hi, h_lo, "norm2" if j == J_WQ else None)
                pe.wait_ge(s["keyTc"], s.had("keyTc") + 1)
                for b in range(NBANK):
                    pe.wait_ge(s["free"][b], s.had("free", b) + (FIRST[NJ] - b + NBANK - 1) // NBANK)
                for tt in range(NT):
                    for b in range(4):
                        for i in range(4):
                            n = 4 * b + i
                            mm = pe.matmul(ps[:, 4 * tt + b, i * P:i * P + P], pq[:, n, tt * P:tt * P + P],
                                           keysT[:, n % 2, :], start=True, stop=True)
                        mm.then_inc(s["sc"], 1)
                def slots_out(tt):
                    if tt == 0:
                        pe.wait_ge(s["scc"], s.had("scc") + NT)
                    else:
                        pe.wait_ge(s["slotTc"], s.had("slotTc") + tt)
                    pe.wait_ge(s["slot"], s.had("slot") + tt + 1)
                    for n in range(3):
                        mm = pe.transpose(ps[:, 2, n * P:n * P + P], slots[:, n, :], ident)
                    mm.then_inc(s["slotT"], 1)

                def weights_a(g, i, reuse=True):
                    pe.wait_ge(s["oh1"], s.had("oh1") + g + 1)
                    pe.wait_ge(s["oh2"], s.had("oh2") + g + 1)
                    if reuse:
                        pe.wait_ge(s["gc"], s.had("gc") + g - 1)
                    for t in range(4):
                        mm = pe.matmul(ps[:, i, t * P:t * P + P], oh2[i][:, t, :], oh1[i][:, t, :],
                                       start=True, stop=True)
                    mm.then_inc(s["g"], 1)

                def weights_b(g, i, reuse=True):
                    pe.wait_ge(s["oh1b"], s.had("oh1b") + g + 1)
                    pe.wait_ge(s["oh2b"], s.had("oh2b") + g + 1)
                    if reuse:
                        pe.wait_ge(s["gcb"], s.had("gcb") + g - 3)
                    for t in range(4):
                        mm = pe.matmul(ps[:, 4 + i, t * P:t * P + P], oh2b[i % 2][:, t, :], oh1b[i % 2][:, t, :],
                                       start=True, stop=True)
                    mm.then_inc(s["gb"], 1)

                slots_out(0)
                weights_a(0, 0, reuse=False)
                weights_a(1, 1, reuse=False)
                with pe.Fori(1, SOLO // 2) as n:
                    for i in range(2):
                        weights_a(2 * n + i, i)
                slots_out(1)
                for i in range(2):
                    weights_a(SOLO + i, i)
                    for h in range(2):
                        weights_b(2 * i + h, 2 * i + h, reuse=False)
                with pe.Fori(1, MIXED) as n:
                    for i in range(2):
                        weights_a(2 * n + (i + SOLO), i)
                        for h in range(2):
                            weights_b(4 * n + (2 * i + h), 2 * i + h)

                def transpose_block(c, i, n):
                    pe.wait_ge(s["landu"][i], s.had("landu", i) + 16 * n + 16)
                    for k in range(KD):
                        mm = pe.transpose(ps_ut[:, k * P:k * P + P], u_raw[i][:, k * P:k * P + P], ident)
                    mm.then_inc(s["ut"], 1)

                def activations(c, i, first=False):
                    pe.wait_ge(s["ulo"], s.had("ulo") + c + 1)
                    if not first:
                        pe.wait_ge(s["gelu"], s.had("gelu") + c - 1)
                    for k in range(KD):
                        e = slice(k * P, k * P + P)
                        mm = three(ps[:, 2 + i, 0:SEQ], u_hi[i][:, e], u_lo[i][:, e], h_hi[:, k, :], h_lo[:, k, :],
                                   k == 0, k == KD - 1)
                    mm.then_inc(s["s"], 1)

                def combine(c, i, start=False, stop=False):
                    pe.wait_ge(s["wl"], s.had("wl") + c + 1)
                    for tt in range(NT):
                        t = slice(tt * P, tt * P + P)
                        for hf in range(2):
                            o, d = ps[:, 4 + 2 * tt + hf, :], slice(512 * hf, 512 * hf + 512)
                            pe.matmul(o, w_hi[i][:, t], v_hi[i][:, d], start=start, stop=False)
                            pe.matmul(o, w_hi[i][:, t], v_lo[i][:, d], start=False, stop=False)
                        for hf in range(2):
                            o, d = ps[:, 4 + 2 * tt + hf, :], slice(512 * hf, 512 * hf + 512)
                            mm = pe.matmul(o, w_lo[i][:, t], v_hi[i][:, d], start=False, stop=stop)
                    mm.then_inc(s["v"], 1)

                pe.wait_ge(s["gc"], s.had("gc") + NGR)
                transpose_block(0, 0, 0)
                pe.wait_ge(s["ulo"], s.had("ulo") + 1)
                transpose_block(1, 1, 0)
                activations(0, 0, first=True)
                pe.wait_ge(s["ulo"], s.had("ulo") + 2)
                transpose_block(2, 0, 1)
                activations(1, 1, first=True)
                pe.wait_ge(s["gcb"], s.had("gcb") + NGR)
                combine(0, 0, start=True)
                with pe.Fori(1, NK // 2 - 1) as n:
                    for i in range(2):
                        c = 2 * n + i
                        pe.wait_ge(s["ulo"], s.had("ulo") + c + 1)
                        transpose_block(c + 1, 1 - i, n + i)
                        activations(c, i)
                        combine(c - 1, 1 - i)
                c = NK - 2
                pe.wait_ge(s["ulo"], s.had("ulo") + c + 1)
                transpose_block(c + 1, 1, NK // 2 - 1)
                activations(c, 0)
                combine(c - 1, 1)
                activations(c + 1, 1)
                combine(c, 0)
                combine(c + 1, 1, stop=True)

        @block.vector
        def _(dve):
            count = [0]

            def link(ins):
                count[0] += 1
                ins.then_inc(s_dve, 1)
                dve.wait_ge(s_dve, count[0])

            dve.wait_ge(s_boot, 16 * 9)
            link(dve.tensor_copy(pos[:, :], pos_i[:, :]))
            for tt in range(NT):
                ins = dve.tensor_scalar(ang[:, tt, :], cst[:, C_FREQ:C_END], pos[:, tt:tt + 1], None, ALU.mult)
            link(ins)
            link(dve.tensor_scalar(turns_i[:, :, :], ang[:, :, :], INV_SQRT2PI, None, ALU.mult))
            link(dve.tensor_copy(turns[:, :, :], turns_i[:, :, :]))
            for part in TWO_PI:
                link(dve.scalar_tensor_tensor(out=ang[:, :, :], in0=turns[:, :, :], scalar=-part, in1=ang[:, :, :],
                                              op0=ALU.mult, op1=ALU.add))
            dve.tensor_scalar(ang[:, :, :], ang[:, :, :], PI_IN, -PI_IN, ALU.min, ALU.max).then_inc(s_ang, 1)
            dve.wait_ge(s_sin, 2)
            link(dve.tensor_tensor(half_s[:, :, :], half_s[:, :, :], half_s[:, :, :], ALU.mult))
            link(dve.tensor_scalar(trig[:, :, 0, :], half_s[:, :, :], -2.0, 1.0, ALU.mult, ALU.add))

            for l in range(DEPTH):
                s = L[l]

                def split_lo(j):
                    dve.wait_ge(s["whi"], s.had("whi") + j + 1)
                    for rows, k0, k1 in parts(j):
                        ins = dve.tensor_tensor(chunk(wb_lo[j % 2], j)[0:rows, k0:k1, :],
                                                chunk(raw[j % NRAW], j)[0:rows, k0:k1, :],
                                                chunk(wb_hi[j % 2], j)[0:rows, k0:k1, :].bitcast(F32), ALU.subtract)
                    ins.then_inc(s["wlo"], 1)

                def norm_dve(which, gain):
                    dve.wait_ge(s["ss"], s.had("ss") + NT * (which + 1))
                    dve.tensor_scalar(msq[:, 0:NT], ssq[:, 0:NT], 1.0 / D, EPS, ALU.mult, ALU.add).then_inc(s["ms"], 1)
                    dve.wait_ge(s["rt"], s.had("rt") + which + 1)
                    link(dve.reciprocal(rstd[:, 0:NT], rms[:, 0:NT]))
                    for tt in range(NT):
                        ins = dve.tensor_scalar(xn[:, tt, :], x[:, tt, :], rstd[:, tt:tt + 1], None, ALU.mult)
                    ins.then_inc(s["xn"], 1)
                    for k in range(KD):
                        if k % 2 == 0:
                            dve.wait_ge(s["hhi"], s.had("hhi") + which * KD + k + 2)
                        c = gain(l, k)
                        dve.scalar_tensor_tensor(out=h_lo[:, k, :], in0=ps_norm[:, k, :], scalar=vecT[:, c:c + 1],
                                                 in1=h_hi[:, k, :].bitcast(F32), op0=ALU.mult,
                                                 op1=ALU.subtract).then_inc(s["hlo"], 1)

                def group(j, n):
                    g = FIRST[j] + n
                    dve.wait_ge(s["pj"], s.had("pj") + g + 1)
                    return g % NBANK

                def evac_tokens(j, dst):
                    for n, (tt, c0, m) in enumerate(GROUPS[j]):
                        b = group(j, n)
                        w = min(m, dst.shape[-1])
                        ins = dve.tensor_copy(dst[:, tt, c0:c0 + w], ps[:, b, 0:w])
                        ins.then_inc(s["free"][b], 1)
                    return ins

                def written(j):
                    for g in range(max(FIRST[j], FIRST[j + 1] - NBANK), FIRST[j + 1]):
                        dve.wait_ge(s["free"][g % NBANK], s.had("free", g % NBANK) + g // NBANK + 1)

                def rotate(src, dst, tt, heads):
                    w = MROPE // 2
                    cos = trig[:, tt, 0, :].unsqueeze(1).to_broadcast([P, heads, w])
                    sin = trig[:, tt, 1, :].unsqueeze(1).to_broadcast([P, heads, w])
                    r = [rope_t[:, n, 0:heads, :] for n in range(4)]
                    dve.tensor_tensor(r[0], src[:, :, 0:w], cos, ALU.mult)
                    dve.tensor_tensor(r[1], src[:, :, w:2 * w], sin, ALU.mult)
                    dve.tensor_tensor(r[2], src[:, :, 0:w], sin, ALU.mult)
                    link(dve.tensor_tensor(r[3], src[:, :, w:2 * w], cos, ALU.mult))
                    dve.tensor_tensor(dst[:, :, 0:w], r[0], r[1], ALU.subtract)
                    link(dve.tensor_tensor(dst[:, :, w:2 * w], r[2], r[3], ALU.add))

                def softmax_dve(u, part):
                    br, qt = UNITS[u]
                    H, N = HEADS[br], P * (qt + 1)
                    m0 = P * (1 - qt)
                    Au, Bu, Cu = (t[:, 0:H, 0:N] for t in (A, B, C))
                    zu = ps_score[:, 0:H, 0:N]
                    if br == 1:
                        strict = masks[:, M_STRICT + m0:M_STRICT + 2 * P].unsqueeze(1).to_broadcast([P, H, N])
                        if part == 0:
                            dve.wait_ge(s["ab"], s.had("ab") + qt + 1)
                            link(dve.scalar_tensor_tensor(out=Bu, in0=zu, scalar=0.0, in1=Au, op0=ALU.max, op1=ALU.add))
                            link(dve.tensor_tensor(Cu, Bu, strict, ALU.mult))
                            for h in range(H):
                                dve.tensor_tensor_scan(A[:, h, 0:N], C[:, h, 0:N], C[:, h, 0:N], 0.0, ALU.add, ALU.max)
                            ins = dve.tensor_tensor(Bu, zu, Bu, ALU.subtract)
                            ins.then_inc(s["sfree"], 1)
                            dve.wait_ge(s["sfree"], s.had("sfree") + u + 1)
                            dve.tensor_tensor(Bu, Bu, Au, ALU.add)
                            dve.tensor_scalar(ntot[:, 0:H], A[:, 0:H, N - 1], -1.0, None, ALU.mult).then_inc(s["sb_w"], 1)
                        else:
                            dve.wait_ge(s["ex"], s.had("ex") + qt + 1)
                            dve.tensor_tensor(Au, Au, strict, ALU.mult).then_inc(s["probs"], 1)
                        return
                    base_ = M_MLA if br == 0 else M_FOX
                    allow = masks[:, base_ + m0:base_ + 2 * P]
                    if part == 0:
                        dve.wait_ge(s["score"], s.had("score") + u + 1)
                        if u:
                            dve.wait_ge(s["pt"], s.had("pt") + PT0[u])
                        if br == 0:
                            ins = dve.tensor_tensor(Au, zu, allow.unsqueeze(1).to_broadcast([P, H, N]), ALU.add)
                        else:
                            for h in range(H):
                                ins = dve.scalar_tensor_tensor(out=A[:, h, 0:N], in0=ps_score[:, h, 0:N],
                                                               scalar=cumq[:, qt, h:h + 1], in1=allow,
                                                               op0=ALU.add, op1=ALU.add)
                        ins.then_inc(s["sfree"], 1)
                        dve.wait_ge(s["sfree"], s.had("sfree") + u + 1)
                        link(dve.tensor_reduce(mx[:, 0:H], Au, AX.X, ALU.max))
                        dve.tensor_scalar(nmx[:, 0:H], mx[:, 0:H], -(SCALE_A if br == 0 else SCALE_H), None,
                                          ALU.mult).then_inc(s["pmax"], 1)
                    else:
                        dve.wait_ge(s["pexp"], s.had("pexp") + (u + 1 if br == 0 else u - 1))
                        link(dve.reciprocal(rsum[:, 0:H], esum[:, 0:H]))
                        dve.tensor_tensor(Au, Au, rsum[:, 0:H].unsqueeze(2).to_broadcast([P, H, N]),
                                          ALU.mult).then_inc(s["probs"], 1)

                def pv_dve(u):
                    br, qt = UNITS[u]
                    cols = slice(qt * P, (qt + 1) * P)
                    dve.wait_ge(s["ohi"], s.had("ohi") + u + 1)
                    pieces = [(P, 0, 3)] if HEADS[br] % 2 == 0 else [(P, 0, 2), (64, 2, 3)]
                    for r, a, b in pieces:
                        ins = dve.tensor_tensor(o_lo[0:r, br, a:b, cols], ps_o[0:r, a:b, :],
                                                o_hi[0:r, br, a:b, cols].bitcast(F32), ALU.subtract)
                    ins.then_inc(s["olo"], 1)

                norm_dve(0, g1)
                for j in range(2):
                    split_lo(j)
                evac_tokens(0, cq)
                evac_tokens(1, ckv)
                split_lo(2)
                dve.wait_ge(s["cms"], s.had("cms") + 1)
                dve.tensor_scalar(msq[:, 0:4:2], ssq[:, 0:4:2], 1.0 / QL, EPS, ALU.mult, ALU.add)
                dve.tensor_scalar(msq[:, 1:4:2], ssq[:, 1:4:2], 1.0 / KVL, EPS, ALU.mult, ALU.add).then_inc(s["cms"], 1)
                split_lo(3)
                dve.wait_ge(s["crt"], s.had("crt") + 1)
                link(dve.reciprocal(rstd[:, 0:4], rms[:, 0:4]))
                for tt in range(NT):
                    dve.tensor_scalar(cq[:, tt, :], cq[:, tt, :], rstd[:, 2 * tt:2 * tt + 1], None, ALU.mult)
                    ins = dve.tensor_scalar(ckv[:, tt, 0:KVL], ckv[:, tt, 0:KVL], rstd[:, 2 * tt + 1:2 * tt + 2],
                                            None, ALU.mult)
                ins.then_inc(s["cn"], 1)
                dve.wait_ge(s["chi"], s.had("chi") + 3)
                for k in range(3):
                    c = gq(l, k) if k < 2 else gkv(l)
                    dve.scalar_tensor_tensor(out=c_lo[:, k, :], in0=ps_norm[:, k, :], scalar=vecT[:, c:c + 1],
                                             in1=c_hi[:, k, :].bitcast(F32), op0=ALU.mult,
                                             op1=ALU.subtract).then_inc(s["clo"], 1)
                split_lo(4)
                split_lo(5)
                evac_tokens(4, q_tok)
                for n, (tt, c0, m) in enumerate(GROUPS[5]):
                    b = group(5, n)
                    h0 = c0 // (MNOPE + MV)
                    src = ps[:, b, 0:m].rearrange("p (h e) -> p h e", h=3)
                    dve.tensor_copy(k_full[:, tt, h0:h0 + 3, 0:MNOPE], src[:, :, 0:MNOPE])
                    ins = dve.tensor_copy(v_m[:, tt, h0 * MV:(h0 + 3) * MV].rearrange("p (h e) -> p h e", h=3),
                                          src[:, :, MNOPE:])
                    ins.then_inc(s["free"][b], 1)
                split_lo(6)
                split_lo(7)
                for tt in range(NT):
                    q3 = q_tok[:, tt, :].rearrange("p (h e) -> p h e", h=MH)[:, :, MNOPE:]
                    rotate(q3, q3, tt, MH)
                    kr = ckv[:, tt, KVL:KVL + MROPE].unsqueeze(1)
                    rotate(kr, kr, tt, 1)
                    ins = dve.tensor_copy(k_full[:, tt, :, MNOPE:], kr.to_broadcast([P, MH, MROPE]))
                ins.then_inc(s["rope"], 1)
                evac_tokens(6, v_s)
                split_lo(8)
                split_lo(9)
                evac_tokens(9, v_f)
                written(9)
                f = v_f[:, :, W3:W3 + FH]
                link(dve.tensor_tensor(f, f, bf[:, l, :].unsqueeze(1).to_broadcast([P, NT, FH]), ALU.add))
                link(dve.tensor_scalar(nlf[:, :, :], f, -1.0, None, ALU.mult))
                dve.tensor_tensor(nlf[:, :, :], nlf[:, :, :], f, ALU.min).then_inc(s["fz"], 1)
                split_lo(10)
                dve.wait_ge(s["masks"], s.had("masks") + 16)
                softmax_dve(0, 0)
                dve.wait_ge(s["fe"], s.had("fe") + 2)
                link(dve.scalar_tensor_tensor(out=lf[:, :, :], in0=f, scalar=0.0, in1=lf[:, :, :], op0=ALU.min,
                                              op1=ALU.subtract))
                link(dve.tensor_scalar(nlf[:, :, :], lf[:, :, :], -1.0 / SCALE_H, None, ALU.mult))
                dve.tensor_scalar(lf[:, :, :], lf[:, :, :], 1.0 / SCALE_H, None, ALU.mult).then_inc(s["lf"], 1)
                for u in range(NU):
                    softmax_dve(u, 1)
                    if u == 0:
                        dve.wait_ge(s["cum"], s.had("cum") + 1)
                        dve.tensor_copy(cumq[:, :, :], ps[:, 7, 0:16].rearrange("p (t h) -> p t h", t=NT)[:, :, 0:FH])\
                           .then_inc(s["cumc"], 1)
                        dve.wait_ge(s["cumc"], s.had("cumc") + 1)
                    split_lo(11 + 2 * u)
                    split_lo(12 + 2 * u)
                    if u + 1 < NU:
                        softmax_dve(u + 1, 0)
                    pv_dve(u)
                for hf in range(2):
                    for br in range(3):
                        j = J_WO + 3 * hf + br
                        split_lo(j + 1)
                        dve.wait_ge(s["sig"], s.had("sig") + br + 1)
                        if hf == 1 and br == 0:
                            dve.wait_ge(s["ylo"], s.had("ylo") + 4)
                        for n in range(4):
                            b = group(j, n)
                            gt = gates[:, 8 * br + 4 * hf + n, :]
                            if br == 0:
                                dve.tensor_tensor(yacc[:, n, :], ps[:, b, 0:SEQ], gt, ALU.mult).then_inc(s["free"][b], 1)
                                continue
                            ins = dve.tensor_tensor(ytmp[:, n % 2, :], ps[:, b, 0:SEQ], gt, ALU.mult)
                            ins.then_inc(s["free"][b], 1)
                            g = FIRST[j] + n
                            dve.wait_ge(s["free"][b], s.had("free", b) + g // NBANK + 1)
                            ins = dve.tensor_tensor(yacc[:, n, :], yacc[:, n, :], ytmp[:, n % 2, :], ALU.add)
                            if br == 2:
                                ins.then_inc(s["yacc"], 1)
                    for n in range(4):
                        dve.wait_ge(s["yhi"], s.had("yhi") + 4 * hf + n + 1)
                        dve.tensor_tensor(y_lo[:, 4 * hf + n, :], yacc[:, n, :],
                                          y_hi[:, 4 * hf + n, :].bitcast(F32), ALU.subtract).then_inc(s["ylo"], 1)
                for j in range(J_WOUT, J_WOUT + 4):
                    split_lo(j + 1)
                    c0 = 256 * (j - J_WOUT)
                    for n in range(NT):
                        b = group(j, n)
                        xs = x[:, n, c0:c0 + 256]
                        dve.tensor_tensor(xs, xs, ps[:, b, 0:256], ALU.add).then_inc(s["free"][b], 1)
                norm_dve(1, g2)
                for j in range(J_WQ + 1, NJ):
                    split_lo(j)

                for tt in range(NT):
                    lists = [sc[:, tt, n * NK:n * NK + NK] for n in range(16)]
                    dve.wait_ge(s["scc"], s.had("scc") + tt + 1)

                    def top16(arrays, vals, idx):
                        for n, a in enumerate(arrays):
                            ins = dve.max(vals[:, n, 0:8], a)
                        link(ins)
                        for n, a in enumerate(arrays):
                            dve.max_index(idx[:, n, 0:8], vals[:, n, 0:8], a)
                        for n, a in enumerate(arrays):
                            ins = dve.match_replace(a, vals[:, n, 0:8], a, LOWEST)
                        link(ins)
                        for n, a in enumerate(arrays):
                            ins = dve.max(vals[:, n, 8:16], a)
                        link(ins)
                        for n, a in enumerate(arrays):
                            ins = dve.max_index(idx[:, n, 8:16], vals[:, n, 8:16], a)
                        link(ins)

                    top16(lists, vtop, itop)
                    link(dve.tensor_copy(itf[:, :, :], itop[:, :, :]))
                    v2 = vtop[:, :, :].rearrange("p (h s) a -> p h s a", s=2)
                    for a0, na, nb in SEGMENTS:
                        o = cand[:, :, STARTS[a0]:STARTS[a0] + na * nb]
                        if na == 1:
                            ins = dve.tensor_tensor(o, v2[:, :, 0, a0:a0 + 1].to_broadcast([P, PH, nb]),
                                                    v2[:, :, 1, 0:nb], ALU.add)
                        elif nb == 1:
                            ins = dve.tensor_tensor(o, v2[:, :, 0, a0:a0 + na],
                                                    v2[:, :, 1, 0:1].to_broadcast([P, PH, na]), ALU.add)
                        else:
                            ins = dve.tensor_tensor(
                                o.rearrange("p h (a b) -> p h a b", b=nb),
                                v2[:, :, 0, a0:a0 + na].unsqueeze(3).to_broadcast([P, PH, na, nb]),
                                v2[:, :, 1, 0:nb].unsqueeze(2).to_broadcast([P, PH, na, nb]), ALU.add)
                    link(ins)
                    top16([cand[:, h, :] for h in range(PH)], selv, selp)
                    link(dve.tensor_copy(posf[:, :], selp[:, :, :].rearrange("p h k -> p (h k)")))
                    dve.tensor_copy(gsum[:, 0, :], selv[:, :, 0])
                    link(dve.tensor_copy(gsum[:, 1, :], selv[:, :, 0]))
                    dve.tensor_tensor(selv[:, :, :], selv[:, :, :], gsum[:, 0, :].unsqueeze(2).to_broadcast([P, PH, 16]),
                                      ALU.subtract).then_inc(s["ge"], 1)
                    tmp = sc[:, tt, :].rearrange("p (n a) -> p n a", a=16)
                    tmp4 = sc[:, tt, :].rearrange("p (h n a) -> p h n a", h=PH, a=16)
                    i4 = itf[:, :, :].rearrange("p (h s) a -> p h s a", s=2)

                    def bc(c0):
                        return cst[:, c0:c0 + 16].unsqueeze(1).to_broadcast([P, P, 16])

                    def keys16(t):
                        return t.unsqueeze(2).to_broadcast([P, PH, 16, 16])

                    dve.tensor_copy(dtop[:, :, 0:1], i4[:, :, 0, 0:1])
                    dve.tensor_tensor(dtop[:, :, 1:16], i4[:, :, 0, 1:16], i4[:, :, 0, 0:15], ALU.subtract)
                    steps = posf[:, :].unsqueeze(2).to_broadcast([P, P, 16])
                    link(dve.tensor_tensor(tmp, steps, bc(C_START), ALU.is_ge))
                    link(dve.tensor_tensor(dtop[:, :, :], dtop[:, :, :],
                                           cst[:, C_DSTART:C_DSTART + 16].unsqueeze(1).to_broadcast([P, PH, 16]),
                                           ALU.add))
                    link(dve.tensor_tensor(tmp4, tmp4, keys16(dtop[:, :, :]), ALU.mult))
                    link(dve.tensor_reduce(sub[:, :], tmp, AX.X, ALU.add))
                    link(dve.tensor_scalar(start_i[:, :], sub[:, :], 1.0 / PACK, None, ALU.mult))
                    link(dve.tensor_copy(startf[:, :], start_i[:, :]))
                    if tt:
                        dve.wait_ge(s["slotT"], s.had("slotT") + tt)
                    dve.scalar_tensor_tensor(out=slots[:, 0, :], in0=startf[:, :], scalar=-float(PACK),
                                             in1=sub[:, :], op0=ALU.mult, op1=ALU.add)
                    link(dve.tensor_tensor(posf[:, :], posf[:, :], startf[:, :], ALU.subtract))
                    link(dve.tensor_tensor(tmp, steps, bc(C_I16), ALU.is_equal))
                    link(dve.tensor_tensor(tmp4, tmp4, keys16(i4[:, :, 1, :]), ALU.mult))
                    link(dve.tensor_reduce(slots[:, 1, :], tmp, AX.X, ALU.add))
                    dve.wait_ge(s["gexp"], s.had("gexp") + tt + 1)
                    link(dve.tensor_reduce(gsum[:, 0, :], selv[:, :, :], AX.X, ALU.add))
                    link(dve.reciprocal(gsum[:, 1, :], gsum[:, 0, :]))
                    dve.tensor_tensor(slots[:, 2, :].rearrange("p (h k) -> p h k", h=PH), selv[:, :, :],
                                      gsum[:, 1, :].unsqueeze(2).to_broadcast([P, PH, 16]),
                                      ALU.mult).then_inc(s["slot"], 1)
                def one_hot(g, i, reuse=True):
                    if reuse:
                        dve.wait_ge(s["gb"], s.had("gb") + g - 1)
                    for t in range(4):
                        ins = dve.tensor_scalar(oh1b[i][:, t, :], iota, slotT[:, 0, bass.ds(4 * g + (P + t), 1)],
                                                slotT[:, 2, bass.ds(4 * g + (P + t), 1)], ALU.is_equal, ALU.mult)
                    ins.then_inc(s["oh1b"], 1)
                    dve.tensor_tensor(oh2b[i][:, :, :], iota.unsqueeze(1).to_broadcast([P, 4, NK]),
                                      slotT[:, 1, bass.ds(4 * g + P, 4)].unsqueeze(2).to_broadcast([P, 4, NK]),
                                      ALU.is_equal).then_inc(s["oh2b"], 1)

                dve.wait_ge(s["slotTc"], s.had("slotTc") + NT)
                one_hot(0, 0, reuse=False)
                one_hot(1, 1, reuse=False)
                with dve.Fori(1, NGR // 2) as n:
                    for i in range(2):
                        one_hot(2 * n + i, i)

                def u_split(c, i):
                    dve.wait_ge(s["uhi"], s.had("uhi") + c + 1)
                    dve.tensor_tensor(u_lo[i][:, :], ps_ut, u_hi[i][:, :].bitcast(F32), ALU.subtract)\
                       .then_inc(s["ulo"], 1)

                def cycle(c, i, last=False):
                    if not last:
                        u_split(c + 1, 1 - i)
                    dve.wait_ge(s["vhi"], s.had("vhi") + c + 1)
                    dve.tensor_tensor(v_lo[i][:, :], v_raw[i][:, :], v_hi[i][:, :].bitcast(F32), ALU.subtract)\
                       .then_inc(s["vlo"], 1)
                    dve.wait_ge(s["gelu"], s.had("gelu") + c + 1)
                    w1 = wgt[:, :].unsqueeze(2)
                    dve.tensor_tensor(w1, w1, G[:, :, bass.ds(c, 1)], ALU.mult).then_inc(s["w"], 1)
                    dve.wait_ge(s["wsp"], s.had("wsp") + c + 1)
                    dve.tensor_tensor(w_lo[i][:, :], wgt[:, :], w_hi[i][:, :].bitcast(F32), ALU.subtract)\
                       .then_inc(s["wl"], 1)

                u_split(0, 0)
                cycle(0, 0)
                cycle(1, 1)
                with dve.Fori(1, NK // 2 - 1) as n:
                    for i in range(2):
                        cycle(2 * n + i, i)
                cycle(NK - 2, 0)
                cycle(NK - 1, 1, last=True)
                dve.wait_ge(s["v"], s.had("v") + NK)
                for tt in range(NT):
                    for hf in range(2):
                        xs = x[:, tt, 512 * hf:512 * hf + 512]
                        dve.tensor_tensor(xs, xs, ps[:, 4 + 2 * tt + hf, :], ALU.add).then_inc(s["xnew"], 1)

            dve.wait_ge(s_fss, NT)
            dve.tensor_scalar(msq[:, 0:NT], ssq[:, 0:NT], 1.0 / D, EPS, ALU.mult, ALU.add).then_inc(s_fms, 1)
            dve.wait_ge(s_frt, 1)
            link(dve.reciprocal(rstd[:, 0:NT], rms[:, 0:NT]))
            dve.wait_ge(s_gain, 16)
            for tt in range(NT):
                dve.scalar_tensor_tensor(out=y_out[:, tt, :], in0=x[:, tt, :], scalar=rstd[:, tt:tt + 1],
                                         in1=gain_f[:, :], op0=ALU.mult, op1=ALU.mult).then_inc(s_y, 1)


def constants():
    c = np.zeros((P, C_END + M_END), np.float32)
    c[:, C_ID:C_ID + P] = np.eye(P)
    c[:, C_IOTA:C_IOTA + P] = np.arange(P)
    c[:, C_START:C_START + 16] = STARTS
    c[:, C_DSTART:C_DSTART + 16] = PACK * np.diff([0] + STARTS)
    c[:, C_I16:C_I16 + 16] = np.arange(16)
    c[:, C_FREQ:C_END] = np.float32(10000.0) ** (-np.arange(0, MROPE, 2, dtype=np.float32) / np.float32(MROPE))
    q, k = np.arange(P)[:, None], np.arange(P)[None, :]
    m = c[:, C_END:]
    m[:, M_MLA + P:M_MLA + 2 * P] = np.where(k // CHUNK <= q // CHUNK, 0.0, NEG)
    m[:, M_FOX + P:M_FOX + 2 * P] = np.where(k <= q, 0.0, NEG)
    m[:, M_STRICT:M_STRICT + P] = 1.0
    m[:, M_STRICT + P:M_STRICT + 2 * P] = k < q
    m[:, M_TRIU:M_TRIU + P] = q <= k
    m[:, M_TRIU + P:M_TRIU + 2 * P] = 1.0
    return c


_INS = ["x", "positions", "norm1_g", "w_in", "mla_q_norm_g", "w_uq", "mla_kv_norm_g", "w_ukv", "fox_b_f",
        "w_o_mla", "w_o_sb", "w_o_fox", "b_gate", "w_out", "norm2_g", "peer_w_q", "peer_sub_keys",
        "peer_u", "peer_v", "final_norm_g"]


def kernel(**inputs):
    import concourse.bacc as bacc
    from concourse.bass_utils import run_bass_kernel_spmd

    nc = bacc.Bacc("TRN2", target_bir_lowering=False, num_devices=1)
    arrays, t_in = {}, {}
    for name in _INS + ["consts"]:
        a = constants() if name == "consts" else np.ascontiguousarray(inputs[name])
        arrays[f"in_{name}"] = a
        t_in[name] = nc.dram_tensor(f"in_{name}", a.shape, mybir.dt.from_np(a.dtype), kind="ExternalInput").ap()
    out = nc.dram_tensor("out_y", (1, SEQ, D), F32, kind="ExternalOutput").ap()
    build(nc, t_in, out)
    r = run_bass_kernel_spmd(nc, [arrays], core_ids=[0])
    return r.results[0]["out_y"]
```

```python
from contextlib import ExitStack

import numpy as np

import concourse.bass as bass
from concourse import mybir

F32 = mybir.dt.float32
F32R = mybir.dt.float32r
I32 = mybir.dt.int32
U32 = mybir.dt.uint32
ALU = mybir.AluOpType
ACT = mybir.ActivationFunctionType
AX = mybir.AxisListType

P = 128
D = 1024
KD = D // P
SEQ = 256
NT = SEQ // P
DEPTH = 2
CHUNK = 64
HD = 64
EPS = 1e-6
NEG = -1e30
LOWEST = -3.0e38
MH, MNOPE, MROPE, MV = 6, 64, 32, 64
MQK = MNOPE + MROPE
QL, KVL = 256, 128
SH, FH = 5, 5
PH, NK, HALF, TOPK = 8, 128, 128, 16
NEXP = NK * NK
PACK = 2 * NK
W3 = SH * HD
GATES0 = QL + KVL + MROPE + 6 * W3 + FH
NG = 3 * D // P
SCALE_A = float(MQK) ** -0.5
SCALE_H = float(HD) ** -0.5
INV_SQRT2PI = float(1.0 / (2.0 * np.pi))
PI_IN = 3.1415925
TWO_PI = (6.28125, 0.0019350051879882812, 3.019915981956753e-07)

C_ID, C_IOTA, C_START, C_DSTART, C_I16, C_FREQ, C_EPS, C_END = 0, 128, 256, 272, 288, 304, 320, 328
M_MLA, M_FOX, M_STRICT, M_TRIU, M_END = 0, 256, 512, 768, 1024

B_OF = [TOPK // (a + 1) for a in range(TOPK)]
STARTS = [sum(B_OF[:a]) for a in range(TOPK)]
NCAND = sum(B_OF)
SEGMENTS = [(0, 1, 16), (1, 1, 8), (2, 1, 5), (3, 1, 4), (4, 1, 3), (5, 3, 2), (8, 8, 1)]

JOBS = (
    [("cq", "w_in", 0, QL, KD, P, True), ("ckv", "w_in", QL, 256, KD, P, True)]
    + [("qs", "w_in", 416, W3, KD, P, False), ("ks", "w_in", 416 + W3, W3, KD, P, False)]
    + [("uq", "w_uq", 0, MH * MQK, 2, P, True), ("vs", "w_in", 416 + 2 * W3, W3, KD, P, True)]
    + [("ukv", "w_ukv", 0, MH * (MNOPE + MV), 1, P, True)]
    + [("qf", "w_in", 416 + 3 * W3, W3, KD, P, False), ("kf", "w_in", 416 + 4 * W3, W3, KD, P, False)]
    + [("vf", "w_in", 416 + 5 * W3, W3 + FH + 1, KD, P, True)]
    + [("gate", "w_in", GATES0 + 256 * n, 256, KD, P, False) for n in range(12)]
    + [(f"wo{br}", s, 512 * h, 512, 3, r, False) for h in range(2)
       for br, (s, r) in enumerate((("w_o_mla", P), ("w_o_sb", 64), ("w_o_fox", 64)))]
    + [("wout", "w_out", 256 * n, 256, KD, P, True) for n in range(4)]
    + [("wq", "peer_w_q", 256 * n, 256, KD, P, False) for n in range(8)]
)
NJ = len(JOBS)
J_GATE = [j for j, x in enumerate(JOBS) if x[0] == "gate"]
J_WO = J_GATE[-1] + 1
J_WOUT = J_WO + 6
J_WQ = J_WOUT + 4
SLOT = max(x[3] * x[4] for x in JOBS)
NRAW = 3


def groups_of(j):
    name, _, _, w, _, _, tokens = JOBS[j]
    if tokens:
        n = w // 2 if w > 512 or name == "uq" else w
        return [(tt, c, n) for tt in range(NT) for c in range(0, w, n)]
    return [(None, c, min(P, w - c)) for c in range(0, w, P)]


GROUPS = [groups_of(j) for j in range(NJ)]
FIRST = [sum(len(g) for g in GROUPS[:j]) for j in range(NJ + 1)]
NBANK = 3

HEADS = (MH, SH, FH)
UNITS = [(br, qt) for br in range(3) for qt in range(NT)]


def pt_batches(u):
    br, qt = UNITS[u]
    blocks = [(h, kt) for h in range(HEADS[br]) for kt in range(qt + 1)]
    return [blocks[n:n + 4] for n in range(0, len(blocks), 4)]


N_BEFORE = (1, 1, 1, 1, 1, 1)
N_AFTER = (1, 1, 2, 1, 1, 0)
_at = [J_GATE[0] + sum(N_BEFORE[:_u]) + sum(N_AFTER[:_u]) for _u in range(len(UNITS))]
BEFORE = [list(range(_at[_u], _at[_u] + N_BEFORE[_u])) for _u in range(len(UNITS))]
AFTER = [list(range(_at[_u] + N_BEFORE[_u], _at[_u] + N_BEFORE[_u] + N_AFTER[_u])) for _u in range(len(UNITS))]


def pt_bank(u, n):
    return 6 + n % 2


PT0 = [sum(len(pt_batches(v)) for v in range(u)) for u in range(len(UNITS) + 1)]

def g1(l, k): return l * KD + k
def g2(l, k): return (DEPTH + l) * KD + k
def gb(l, n): return 2 * DEPTH * KD + l * NG + n
def gq(l, k): return 2 * DEPTH * KD + DEPTH * NG + 2 * l + k
def gkv(l): return 2 * DEPTH * KD + DEPTH * NG + 2 * DEPTH + l


NVEC = gkv(DEPTH)


NU = len(UNITS)
NGR = P // 4
SOLO = 8
ACT_SOLO = 6
ROUNDS = (NGR - SOLO) // 6
ROUND = [(0, 0), (1, 0), (1, 1), (0, 1), (1, 2), (0, 2), (1, 3), (1, 4), (0, 3), (1, 5), (0, 4), (1, 6), (0, 5), (1, 7)]
OWN = (0, 1, 3, 4)
NPRE = 8
EXP_AT = 4
PER_LAYER = {
    "masks": 16, "keys": 16,
    "whi": NJ, "wlo": NJ,
    "pj": FIRST[NJ],
    "ss": 2 * NT + 4 * NT, "ms": 2, "rt": 2, "xn": 2,
    "xT": KD, "hhi": 2 * KD, "hlo": 2 * KD,
    "cms": 2, "crt": 1, "cn": 1, "cT": 1, "chi": 3, "clo": 3,
    "rope": 1, "mT": 6, "mTc": 6,
    "kz": 2,
    "score": NU, "sfree": NU,
    "ab": 2, "sb_w": 2, "ex": 2,
    "pmax": 4, "pexp": 4,
    "probs": NU, "pt": PT0[NU], "ptc": PT0[NU],
    "pv": NU, "ohi": NU, "olo": NU,
    "fz": 1, "fe": 2, "lf": 1, "cum": 1, "cumc": 1,
    "sig": 3, "yadd": 2 * KD, "yhi": KD, "ylo": KD,
    "keyT": 1, "keyTc": 1, "sc": 8, "scc": 8,
    "ge": NT, "gexp": NT, "slot": NT, "slotT": NT, "slotTc": NT,
    "nw": 1, "dist": ACT_SOLO + 4 * ROUNDS, "oh1": ACT_SOLO + 4 * ROUNDS, "oh1v": SOLO - ACT_SOLO + 2 * ROUNDS,
    "k2": NGR, "oh2": NGR, "g": NGR, "gc": NGR,
    "oh1b": NGR, "oh2b": NGR, "gb": NGR, "gcb": NGR,
    "hf": 1,
    "ut": NK, "uhi": NK, "ulo": NK - NPRE,
    "s": NK, "gelu": NK,
    "w": NK, "wsp": NK, "wl": NK,
    "vhi": NK, "vlo": NK, "v": NK,
    "xnew": 4,
}


def build(nc, t_in, out):
    ctx = ExitStack()
    base = -(-nc.sbuf_base // 64) * 64

    def at(name, shape, off, dt=F32):
        return nc.alloc_sbuf_tensor_at(name, shape, dt, offset=base + off)

    def sem(name):
        return ctx.enter_context(nc.semaphore(name))

    with ctx:
        x = at("x", [P, NT, D], 0)
        h_hi = at("h_hi", [P, KD, SEQ], 8192, F32R)
        h_lo = at("h_lo", [P, KD, SEQ], 16384, F32R)
        cst = at("cst", [P, C_END], 24576)
        vecT = at("vecT", [P, 88], 25888)
        trig = at("trig", [P, NT, 2, 16], 26240)
        st = at("st", [P, 104], 26496)
        ident = cst[:, C_ID:C_ID + P]
        iota = cst[:, C_IOTA:C_IOTA + P]
        ssq, msq, rms, rstd = (st[:, 8 * n:8 * n + 8] for n in range(4))
        ssq4 = ssq.rearrange("p (t n) -> p t n", t=NT)
        mx, nmx, esum, rsum, ntot = (st[:, 32 + 6 * n:38 + 6 * n] for n in range(5))
        lf = st[:, 62:72].rearrange("p (t h) -> p t h", t=NT)
        nlf = st[:, 72:82].rearrange("p (t h) -> p t h", t=NT)
        cumq = st[:, 82:92].rearrange("p (t h) -> p t h", t=NT)
        bf = st[:, 92:92 + DEPTH * FH].rearrange("p (l h) -> p l h", l=DEPTH)
        S0 = 26944
        u_raw = [at(f"u_raw{i}", [P, D], S0 + 4096 * i) for i in range(2)]
        v_raw = [at(f"v_raw{i}", [P, D], S0 + 8192 + 4096 * i) for i in range(2)]
        u_hi = [at(f"u_hi{i}", [P, D], S0 + 16384 + 4096 * i, F32R) for i in range(2)]
        u_lo = [at(f"u_lo{i}", [P, D], S0 + 24576 + 4096 * i, F32R) for i in range(2)]
        v_hi = [at(f"v_hi{i}", [P, D], S0 + 32768 + 4096 * i, F32R) for i in range(2)]
        v_lo = [at(f"v_lo{i}", [P, D], S0 + 40960 + 4096 * i, F32R) for i in range(2)]
        wgt = at("wgt", [P, SEQ], S0 + 49152)
        w_hi = [at(f"w_hi{i}", [P, SEQ], S0 + 50176 + 1024 * i, F32R) for i in range(2)]
        w_lo = [at(f"w_lo{i}", [P, SEQ], S0 + 52224 + 1024 * i, F32R) for i in range(2)]
        G = at("G", [P, SEQ, NK], S0 + 54272)
        R0 = S0 + 16384
        sc = at("sc", [P, NT, 16 * NK], S0 + 144384)
        slotT = at("slotT", [P, 3, SEQ], R0 + 16384)
        oh1 = [at(f"oh1_{i}", [P, 4, NK], R0 + 19456 + 2048 * i) for i in range(2)]
        oh2 = [at(f"oh2_{i}", [P, 4, NK], R0 + 23552 + 2048 * i) for i in range(2)]
        vtops = [at(f"vtop{t}", [P, 16, 16], S0 + 180864 + 2048 * t) for t in range(NT)]
        itops = [at(f"itop{t}", [P, 16, 16], S0 + 181888 + 2048 * t, U32) for t in range(NT)]
        itf = at("itf", [P, 16, 16], R0 + 29696)
        cand = at("cand", [P, PH, NCAND], R0 + 30720)
        slots = at("slots", [P, 3, P], R0 + 32320)
        selv = at("selv", [P, PH, 16], R0 + 33856)
        selp = at("selp", [P, PH, 16], R0 + 34368, U32)
        posf = at("posf", [P, P], R0 + 34880)
        sub = at("sub", [P, P], R0 + 35392)
        dtop = at("dtop", [P, PH, 16], R0 + 35904)
        gsum = at("gsum", [P, 2, PH], R0 + 36416)
        key2 = [at(f"key2_{i}", [P, 4], R0 + 36480 + 32 * i) for i in range(2)]
        start_i = at("start_i", [P, P], R0 + 36544, I32)
        startf = at("startf", [P, P], R0 + 35904)
        dist = [at(f"dist{i}", [P, 4, NK], S0 + 12288 + 2048 * i) for i in range(2)]
        nweight = at("nweight", [P, P], R0 + 37056)
        oh1b = [at(f"oh1b_{i}", [P, 4, NK], R0 + 2048 * i) for i in range(2)]
        oh2b = [at(f"oh2b_{i}", [P, 4, NK], R0 + 4096 + 2048 * i) for i in range(2)]
        act_pre = at("act_pre", [P, NPRE, SEQ], S0)
        h_full = at("h_full", [P, KD, SEQ], S0 + 119808)
        p_raw = [at(f"p_raw{i}", [P, D], S0 + 128000 + 4096 * i) for i in range(2)]
        p_ut = [at(f"p_ut{i}", [P, D], S0 + 136192 + 4096 * i) for i in range(2)]
        M0 = S0
        A = at("A", [P, MH, SEQ], M0)
        B = at("B", [P, MH, SEQ], M0 + 6144)
        k_full = at("k_full", [P, NT, MH, MQK], M0 + 6144)
        rope_t = at("rope_t", [P, 4, MH, 16], M0)
        PT = at("PT", [P, 12, P], M0 + 12288)
        raw = [at(f"raw{i}", [P, SLOT], M0 + 18432 + 4 * SLOT * i) for i in range(NRAW)]
        WH0 = M0 + 18432 + 4 * SLOT * NRAW
        wb_hi = [at(f"wb_hi{i}", [P, SLOT], WH0 + 4 * SLOT * i, F32R) for i in range(2)]
        wb_lo = [at(f"wb_lo{i}", [P, SLOT], WH0 + 4 * SLOT * (2 + i), F32R) for i in range(2)]
        Q0 = WH0 + 16 * SLOT
        X0 = Q0 + 39232
        O0 = X0 + 31744
        wb_hi.append(at("wb_hi2", [P, 2048], M0, F32R))
        wb_lo.append(at("wb_lo2", [P, 2048], M0 + 8192, F32R))
        wb_hi += [at("uq_hi", [P, 1152], O0 + 12288, F32R), at("ukv_hi", [P, 768], O0 + 6144, F32R)]
        wb_lo += [at("uq_lo", [P, 1152], M0 + 12288, F32R), at("ukv_lo", [P, 768], O0 + 9216, F32R)]
        raw_first = at("raw_first", [P, 2048], M0)
        gates = at("gates", [P, NG, SEQ], Q0)
        xn = at("xn", [P, NT, D], Q0)
        keys = at("keys", [P, 2, P], Q0 + 8192)
        keysT = at("keysT", [P, 2, P], Q0 + 9216)
        C = at("C", [P, MH, SEQ], Q0 + 24576)
        q_tok = at("q_tok", [P, NT, MH * MQK], Q0 + 24576)
        yacc = [at(f"yacc{i}", [P, 4, SEQ], Q0 + 24576 + 8192 * i) for i in range(2)]
        ytmp = at("ytmp", [P, 4, SEQ], Q0 + 28672)
        cq = at("cq", [P, NT, QL], Q0 + 30720)
        ckv = at("ckv", [P, NT, KVL + MROPE], Q0 + 32768)
        v_s = at("v_s", [P, NT, W3], Q0 + 34048)
        v_f = at("v_f", [P, NT, W3 + FH + 1], Q0 + 36608)
        qT = at("qT", [P, 2, 3, SEQ], X0)
        kT = at("kT", [P, 2, 5, SEQ], X0 + 6144)
        v_m = at("v_m", [P, NT, MH * MV], X0 + 16384)
        mqk = at("mqk", [P, 2, MH, SEQ], X0 + 19456)
        y_hi = at("y_hi", [P, KD, SEQ], X0, F32R)
        y_lo = at("y_lo", [P, KD, SEQ], X0 + 8192, F32R)
        o_hi = at("o_hi", [P, 3, 3, SEQ], O0, F32R)
        o_lo = at("o_lo", [P, 3, 3, SEQ], O0 + 9216, F32R)
        c_hi = at("c_hi", [P, 3, SEQ], O0, F32R)
        c_lo = at("c_lo", [P, 3, SEQ], O0 + 3072, F32R)
        pq = at("pq", [P, 2 * PH, SEQ], O0)
        masks = at("masks", [P, M_END], O0 + 18432)
        E0 = M0 + 12288
        vecs = at("vecs", [P, P], E0)
        pos_i = at("pos_i", [P, NT], E0 + 512, I32)
        pos = at("pos", [P, NT], E0 + 544)
        ang = at("ang", [P, NT, 16], E0 + 576)
        turns_i = at("turns_i", [P, NT, 16], E0 + 704, I32)
        turns = at("turns", [P, NT, 16], E0 + 832)
        half_s = at("half_s", [P, NT, 16], E0 + 960)
        gain_f = at("gain_f", [P, D], E0 + 1088)
        y_out = at("y_out", [P, NT, D], M0)

        ps = ctx.enter_context(nc.psum_tensor("ps", [P, 8, 512], F32))
        ps_score = ps[:, 3:6, :].rearrange("p b (h k) -> p (b h) k", k=SEQ)
        ps_norm = ps[:, 3:7, :].rearrange("p b (h k) -> p (b h) k", k=SEQ)
        ps_o = ps[:, 7, :].rearrange("p (h k) -> p h k", k=P)
        ps_ut = ps[:, 0:2, :].rearrange("p b n -> p (b n)")

        def sc_bank(k):
            return 3 + k % 5

        def pre_banks(i):
            return ps[:, 6 - 2 * i:8 - 2 * i, :].rearrange("p b n -> p (b n)")


        s_boot = sem("s_boot")
        s_bootT = sem("s_bootT")
        s_vecT = sem("s_vecT")
        s_ang = sem("s_ang")
        s_sin = sem("s_sin")
        s_trig = sem("s_trig")
        s_dve = sem("s_dve")
        s_act = sem("s_act")
        s_gain = sem("s_gain")
        s_fss = sem("s_fss")
        s_frt = sem("s_frt")
        s_fms = sem("s_fms")
        s_y = sem("s_y")
        s_out = sem("s_out")

        landed, total = [], [0] * NRAW
        for j in range(NJ):
            total[j % NRAW] += 16 * (2 if JOBS[j][5] < P else 1)
            landed.append(total[j % NRAW])
        sems = {n: sem(f"s_{n}") for n in PER_LAYER}
        for n, k in (("land", NRAW), ("free", NBANK), ("landp", 2), ("landu", 2), ("landv", 2)):
            sems[n] = [sem(f"s_{n}{i}") for i in range(k)]

        class Layer:

            def __init__(self, l):
                self.l = l

            def __getitem__(self, name):
                return sems[name]

            def had(self, name, i=0):
                if name == "land":
                    return self.l * total[i]
                if name == "free":
                    return self.l * ((FIRST[NJ] - i + NBANK - 1) // NBANK)
                blocks = {"landp": NPRE, "landu": NK - NPRE, "landv": NK}
                return self.l * (8 * blocks[name] if name in blocks else PER_LAYER[name])

        L = [Layer(l) for l in range(DEPTH)]

        def chunk(buf, j):
            return buf[:, 0:JOBS[j][3] * JOBS[j][4]].rearrange("p (k n) -> p k n", k=JOBS[j][4])

        def raw_of(j):
            return raw[j % NRAW] if j else raw_first

        buf, last_in = [], []
        for j, job in enumerate(JOBS):
            nth = sum(x[0] not in ("uq", "ukv") for x in JOBS[:j])
            buf.append({"uq": 3, "ukv": 4}[job[0]] if job[0] in ("uq", "ukv") else nth % 2 if j < J_WO else (j - J_WO) % 3)
            last_in.append(max((i for i in range(j) if buf[i] == buf[j]), default=None))

        def buf_of(j):
            return buf[j]

        def parts(j):
            k, r = JOBS[j][4], JOBS[j][5]
            return [(P, 0, k)] if r == P else [(P, 0, k - 1), (r, k - 1, k)]

        block = ctx.enter_context(nc.Block())

        @block.sync
        def _(sp):
            sp.dma_start(x[:, :, :], t_in["x"][0].rearrange("(t p) d -> p t d", p=P)).then_inc(s_boot, 16)
            sp.dma_start(cst[:, :], t_in["consts"][:, 0:C_END]).then_inc(s_boot, 16)
            for t, r0, n in (("norm1_g", g1(0, 0), DEPTH * KD), ("norm2_g", g2(0, 0), DEPTH * KD),
                             ("b_gate", gb(0, 0), DEPTH * NG), ("mla_q_norm_g", gq(0, 0), DEPTH * 2),
                             ("mla_kv_norm_g", gkv(0), DEPTH)):
                sp.dma_start(vecs[r0:r0 + n, :], t_in[t].rearrange("l (k p) -> (l k) p", p=P)).then_inc(s_boot, 16)
            sp.dma_start(pos_i[:, :], t_in["positions"][0].rearrange("(t p) -> p t", p=P),
                         allow_slow_non_contiguous=True).then_inc(s_boot, 16)
            sp.dma_start(st[:, 92:92 + DEPTH * FH], t_in["fox_b_f"].rearrange("l h -> (l h)").partition_broadcast(P)).then_inc(s_boot, 16)

            for l in range(DEPTH):
                s = L[l]
                if l:
                    sp.wait_ge(L[l - 1]["ut"], L[l - 1].had("ut") + NK)
                sp.dma_start(chunk(raw_first, 0), t_in["w_in"][l, :, 0:QL].rearrange("(k p) n -> p k n", p=P))\
                  .then_inc(s["land"][0], 16)
                if l:
                    sp.wait_ge(L[l - 1]["xnew"], L[l - 1].had("xnew") + 4)
                sp.dma_start(masks[:, :], t_in["consts"][:, C_END:C_END + M_END]).then_inc(s["masks"], 16)
                for j, (name, src, c0, w, kt, last, _) in enumerate(JOBS):
                    if j >= NRAW:
                        sp.wait_ge(s["wlo"], s.had("wlo") + j - NRAW + 1)
                    if name == "wq" and JOBS[j - 1][0] == "wout":
                        sp.wait_ge(s["ylo"], s.had("ylo") + KD)
                        sp.dma_start(keys[:, :, :], t_in["peer_sub_keys"][l].rearrange("s n c -> n s c")).then_inc(s["keys"], 16)
                    for rows, k0, k1 in parts(j) if j else []:
                        sp.dma_start(chunk(raw_of(j), j)[0:rows, k0:k1, :],
                                     t_in[src][l, k0 * P:(k1 - 1) * P + rows, c0:c0 + w].rearrange(
                                         "(k p) n -> p k n", p=rows)).then_inc(s["land"][j % NRAW], 16)
                sp.wait_ge(s["ylo"], s.had("ylo") + KD)

                def load_block(b, i):
                    sp.dma_start(u_raw[i][:, :], t_in["peer_u"][l, bass.ds(b * P, P), :]).then_inc(s["landu"][i], 16)

                def load_v(b, i):
                    sp.dma_start(v_raw[i][:, :], t_in["peer_v"][l, bass.ds(b * P, P), :]).then_inc(s["landv"][i], 16)

                def load_pre(b, i):
                    sp.dma_start(p_raw[i][:, :], t_in["peer_u"][l, bass.ds(b * P, P), :]).then_inc(s["landp"][i], 16)

                sp.wait_ge(s["pj"], s.had("pj") + FIRST[J_WQ])
                for i in range(2):
                    load_pre(i, i)
                sp.wait_ge(s["pj"], s.had("pj") + FIRST[NJ])
                load_v(0, 0)
                with sp.Fori(1, NPRE // 2) as n:
                    for i in range(2):
                        sp.wait_ge(s["ut"], s.had("ut") + 2 * n + (i - 1))
                        load_pre(2 * n + i, i)
                sp.wait_ge(s["oh1"], s.had("oh1") + ACT_SOLO + 4 * ROUNDS)
                load_v(1, 1)

                for c in range(2, NPRE + 2):
                    if c in (5, NPRE + 1):
                        i = int(c > NPRE)
                        sp.wait_ge(s["w"], s.had("w") + c - 1)
                        load_block(NPRE + i, i)
                    sp.wait_ge(s["vlo"], s.had("vlo") + c - 1)
                    load_v(c, c % 2)
                with sp.Fori(NPRE // 2 + 1, NK // 2) as n:
                    for i in range(2):
                        sp.wait_ge(s["ut"], s.had("ut") + 2 * n + (i - 1))
                        load_block(2 * n + i, i)
                        sp.wait_ge(s["vlo"], s.had("vlo") + 2 * n + (i - 1))
                        load_v(2 * n + i, i)

            sp.wait_ge(L[-1]["v"], L[-1].had("v") + NK)
            sp.dma_start(gain_f[:, :], t_in["final_norm_g"].partition_broadcast(P)).then_inc(s_gain, 16)
            for tt in range(NT):
                sp.wait_ge(s_y, tt + 1)
                sp.dma_start(out[0, tt * P:(tt + 1) * P, :], y_out[:, tt, :]).then_inc(s_out, 16)
            sp.wait_ge(s_out, 16 * NT)

        @block.gpsimd
        def _(pool):
            for l in range(DEPTH):
                s = L[l]
                if l:
                    pool.wait_ge(L[l - 1]["xnew"], L[l - 1].had("xnew") + 4)
                pool.memset(kT[HD:P, :, 0:4:2, :], 0.0).then_inc(s["kz"], 1)
                pool.memset(kT[0:HD, :, 1:4:2, :], 0.0).then_inc(s["kz"], 1)
                for hf in range(2):
                    for br in (1, 2):
                        for n in range(4):
                            g = FIRST[J_WO + 3 * hf + br] + n
                            pool.wait_ge(s["free"][g % NBANK], s.had("free", g % NBANK) + g // NBANK + 1)
                            if br == 2:
                                pool.wait_ge(s["yadd"], s.had("yadd") + 8 * hf + n + 1)
                            pool.tensor_tensor(yacc[hf][:, n, :], yacc[hf][:, n, :], ytmp[:, n, :], ALU.add).then_inc(s["yadd"], 1)
                pool.wait_ge(s["hlo"], s.had("hlo") + 2 * KD)
                pool.wait_ge(s["pj"], s.had("pj") + FIRST[J_WQ])
                pool.tensor_tensor(h_full[:, :, :], h_hi[:, :, :].bitcast(F32), h_lo[:, :, :].bitcast(F32),
                                   ALU.add).then_inc(s["hf"], 1)
                pool.wait_ge(s["slotTc"], s.had("slotTc") + 1)

                def take_keys(g, i):
                    pool.tensor_copy(key2[i][:, :], slotT[:, 1, bass.ds(4 * g, 4)]).then_inc(s["k2"], 1)

                def one_hot(g, i, first=False, last=False):
                    if not (first and i == 0):
                        pool.wait_ge(s["oh2"], s.had("oh2") + g)
                    if not first:
                        pool.wait_ge(s["g"], s.had("g") + g - 1)
                    pool.wait_ge(s["k2"], s.had("k2") + g + 1)
                    if not last:
                        take_keys(g + 1, 1 - i)
                    for t in range(4):
                        ins = pool.tensor_scalar(oh2[i][:, t, :], iota, key2[i][:, t:t + 1], None, ALU.is_equal)
                    ins.then_inc(s["oh2"], 1)

                take_keys(0, 0)
                one_hot(0, 0, first=True)
                one_hot(1, 1, first=True)
                with pool.Fori(1, NGR // 2 - 1) as n:
                    for i in range(2):
                        one_hot(2 * n + i, i)
                one_hot(NGR - 2, 0)
                one_hot(NGR - 1, 1, last=True)

        @block.scalar
        def _(act):
            count = [0]

            def link(ins):
                count[0] += 1
                ins.then_inc(s_act, 1)
                act.wait_ge(s_act, count[0])

            act.wait_ge(s_bootT, 1)
            act.activation(vecT[:, 0:NVEC], ps[:, 0, 0:NVEC], ACT.Copy).then_inc(s_vecT, 1)
            act.wait_ge(s_ang, 1)
            act.activation(trig[:, :, 1, :], ang[:, :, :], ACT.Sin).then_inc(s_sin, 1)
            act.activation(half_s[:, :, :], ang[:, :, :], ACT.Sin, scale=0.5).then_inc(s_sin, 1)

            for l in range(DEPTH):
                s = L[l]

                def split_hi(j):
                    act.wait_ge(s["land"][j % NRAW], s.had("land", j % NRAW) + landed[j])
                    if j == J_WO + 2:
                        act.wait_ge(s["pv"], s.had("pv") + NU)
                    elif last_in[j] is not None:
                        act.wait_ge(s["pj"], s.had("pj") + FIRST[last_in[j] + 1])
                    ps_ = parts(j)
                    for rows, k0, k1 in ps_:
                        ins = act.activation(chunk(wb_hi[buf_of(j)], j)[0:rows, k0:k1, :],
                                             chunk(raw_of(j), j)[0:rows, k0:k1, :], ACT.Copy)
                    ins.then_inc(s["whi"], 1)

                def evac(j, n):
                    name = JOBS[j][0]
                    g = FIRST[j] + n
                    _, c0, rows = GROUPS[j][n]
                    act.wait_ge(s["pj"], s.had("pj") + g + 1)
                    src = ps[0:rows, g % NBANK, 0:SEQ]
                    if name == "wq":
                        ins = act.activation(pq[:, 2 * (j - J_WQ) + n, :], src, ACT.Copy)
                    elif name in ("qs", "qf"):
                        ins = act.activation(qT[0:rows, int(name == "qf"), n, :], src, ACT.Copy,
                                             scale=SCALE_H if name == "qs" else 1.0)
                    else:
                        for r in range(0, rows, HD):
                            ins = act.activation(kT[r:r + HD, int(name == "kf"), 2 * n + r // HD, :],
                                                 ps[r:r + HD, g % NBANK, 0:SEQ], ACT.Copy)
                    ins.then_inc(s["free"][g % NBANK], 1)

                def evacuated(j):
                    for g in range(FIRST[j + 1] - NBANK, FIRST[j + 1]):
                        act.wait_ge(s["free"][g % NBANK], s.had("free", g % NBANK) + g // NBANK + 1)

                def squares(tt, part, width):
                    act.activation(xn[:, tt, part * width:(part + 1) * width], x[:, tt, part * width:(part + 1) * width],
                                   ACT.Square, accum_out=ssq4[:, tt, part:part + 1]).then_inc(s["ss"], 1)

                def squares_wout(n):
                    for tt in range(NT):
                        g = FIRST[J_WOUT + n] + tt
                        act.wait_ge(s["free"][g % NBANK], s.had("free", g % NBANK) + g // NBANK + 1)
                        squares(tt, n, 256)

                def norm_act(which, gain):
                    act.activation(rms[:, 4:6], cst[:, C_EPS:C_EPS + 2], ACT.Sqrt)
                    if which == 0:
                        if l == 0:
                            act.wait_ge(s_boot, 16 * 9)
                        for tt in range(NT):
                            for hf in range(2):
                                if l:
                                    act.wait_ge(L[l - 1]["xnew"], L[l - 1].had("xnew") + 2 * tt + hf + 1)
                                squares(tt, hf, 512)
                    else:
                        squares_wout(3)
                    act.wait_ge(s["ms"], s.had("ms") + which + 1)
                    act.activation(rms[:, 0:NT], msq[:, 0:NT], ACT.Sqrt, scale=1.0 / D,
                                   bias=cst[:, C_EPS:C_EPS + 1]).then_inc(s["rt"], 1)
                    if which == 0:
                        split_hi(0)
                    for k in range(KD):
                        if k % 2 == 0:
                            act.wait_ge(s["xT"], s.had("xT") + (which * KD + k) // 2 + 1)
                        act.activation(h_hi[:, k, :], ps_norm[:, k, :], ACT.Copy,
                                       scale=vecT[:, gain(l, k):gain(l, k) + 1]).then_inc(s["hhi"], 1)

                def evac_gates(j):
                    for n in range(2):
                        g = FIRST[j] + n
                        k = 2 * (j - J_GATE[0]) + n
                        c = gb(l, k)
                        act.wait_ge(s["pj"], s.had("pj") + g + 1)
                        act.activation(gates[:, k, :], ps[:, g % NBANK, 0:SEQ], ACT.Identity,
                                       bias=vecT[:, c:c + 1]).then_inc(s["free"][g % NBANK], 1)

                def stick_act(u):
                    br, qt = UNITS[u]
                    H, N = HEADS[br], P * (qt + 1)
                    if br != 1:
                        return
                    act.wait_ge(s["score"], s.had("score") + u + 1)
                    act.wait_ge(s["pt"], s.had("pt") + PT0[u])
                    z = ps_score[:, 0:H, 0:N]
                    link(act.activation(A[:, 0:H, 0:N], z, ACT.Abs))
                    link(act.activation(A[:, 0:H, 0:N], A[:, 0:H, 0:N], ACT.Exp, scale=-1.0))
                    act.activation(A[:, 0:H, 0:N], A[:, 0:H, 0:N], ACT.Ln, bias=1.0).then_inc(s["ab"], 1)

                def exp_act(u):
                    br, qt = UNITS[u]
                    H, N = HEADS[br], P * (qt + 1)
                    if br == 1:
                        act.wait_ge(s["sb_w"], s.had("sb_w") + qt + 1)
                        for h in range(H):
                            ins = act.activation(A[:, h, 0:N], B[:, h, 0:N], ACT.Exp, bias=ntot[:, h:h + 1])
                        ins.then_inc(s["ex"], 1)
                        return
                    act.wait_ge(s["pmax"], s.had("pmax") + (u + 1 if br == 0 else u - 1))
                    for h in range(H):
                        ins = act.activation(A[:, h, 0:N], A[:, h, 0:N], ACT.Exp, bias=nmx[:, h:h + 1],
                                             scale=SCALE_A if br == 0 else SCALE_H,
                                             accum_out=esum[:, h:h + 1])
                    ins.then_inc(s["pexp"], 1)

                def copy_probs(u):
                    if u:
                        act.wait_ge(s["pv"], s.had("pv") + u)
                    at_ = 0
                    for n, batch in enumerate(pt_batches(u)):
                        act.wait_ge(s["pt"], s.had("pt") + PT0[u] + n + 1)
                        m = len(batch)
                        act.activation(PT[:, at_:at_ + m, :],
                                       ps[:, pt_bank(u, n), 0:m * P].rearrange("p (m k) -> p m k", k=P),
                                       ACT.Copy).then_inc(s["ptc"], 1)
                        at_ += m

                def pv_act(u):
                    br, qt = UNITS[u]
                    act.wait_ge(s["pv"], s.had("pv") + u + 1)
                    cols = slice(qt * P, (qt + 1) * P)
                    if HEADS[br] % 2 == 0:
                        ins = act.activation(o_hi[:, br, :, cols], ps_o[:, 0:3, :], ACT.Copy)
                    else:
                        act.activation(o_hi[:, br, 0:2, cols], ps_o[:, 0:2, :], ACT.Copy)
                        ins = act.activation(o_hi[0:64, br, 2, cols], ps_o[0:64, 2, :], ACT.Copy)
                    ins.then_inc(s["ohi"], 1)

                norm_act(0, g1)
                for j in range(1, 3):
                    split_hi(j)
                evacuated(1)
                for tt in range(NT):
                    act.activation(C[:, tt, :], cq[:, tt, :], ACT.Square, accum_out=ssq[:, 2 * tt:2 * tt + 1])
                    ins = act.activation(C[:, 2 + tt, 0:KVL], ckv[:, tt, 0:KVL], ACT.Square,
                                         accum_out=ssq[:, 2 * tt + 1:2 * tt + 2])
                ins.then_inc(s["cms"], 1)
                act.wait_ge(s["cms"], s.had("cms") + 2)
                act.activation(rms[:, 0:4], msq[:, 0:4], ACT.Sqrt).then_inc(s["crt"], 1)
                split_hi(3)
                for n in range(3):
                    evac(2, n)
                split_hi(4)
                split_hi(5)
                act.wait_ge(s["cT"], s.had("cT") + 1)
                for k in range(3):
                    c = gq(l, k) if k < 2 else gkv(l)
                    act.activation(c_hi[:, k, :], ps_norm[:, k, :], ACT.Copy, scale=vecT[:, c:c + 1]).then_inc(s["chi"], 1)
                for n in range(3):
                    evac(3, n)
                split_hi(6)
                split_hi(7)
                split_hi(8)
                for n in range(3):
                    evac(7, n)
                split_hi(9)
                for n in range(3):
                    evac(8, n)
                for n in range(6):
                    act.wait_ge(s["mT"], s.had("mT") + n + 1)
                    act.activation(mqk[0:MQK, n // 3, 2 * (n % 3):2 * (n % 3) + 2, :],
                                   ps_score[0:MQK, 2 * (n % 3):2 * (n % 3) + 2, :], ACT.Copy).then_inc(s["mTc"], 1)
                split_hi(10)
                act.wait_ge(s["fz"], s.had("fz") + 1)
                act.activation(lf[:, :, :], nlf[:, :, :], ACT.Exp, scale=1.0).then_inc(s["fe"], 1)
                act.wait_ge(s["fe"], s.had("fe") + 1)
                act.activation(lf[:, :, :], lf[:, :, :], ACT.Ln, bias=1.0).then_inc(s["fe"], 1)
                def gates_in(br):
                    act.activation(gates[:, 8 * br:8 * br + 8, :], gates[:, 8 * br:8 * br + 8, :],
                                   ACT.Sigmoid).then_inc(s["sig"], 1)

                for u in range(NU):
                    exp_act(u)
                    for j in BEFORE[u]:
                        split_hi(j + 1)
                        evac_gates(j)
                    copy_probs(u)
                    split_hi(BEFORE[u][-1] + 2)
                    if u + 1 < NU:
                        stick_act(u + 1)
                    for j in AFTER[u]:
                        if j > AFTER[u][0]:
                            split_hi(j + 1)
                        evac_gates(j)
                    if u + 1 < NU:
                        pv_act(u)
                evacuated(J_WO - 1)
                gates_in(0)
                gates_in(1)
                pv_act(NU - 1)
                split_hi(J_WO + 2)
                gates_in(2)
                for j in range(J_WO + 3, J_WO + 6):
                    split_hi(j)
                    if j == J_WO + 4:
                        for n in range(4):
                            act.wait_ge(s["yadd"], s.had("yadd") + 4 + n + 1)
                            act.activation(y_hi[:, n, :], yacc[0][:, n, :], ACT.Copy).then_inc(s["yhi"], 1)
                split_hi(J_WOUT)
                for n in range(4):
                    act.wait_ge(s["yadd"], s.had("yadd") + 12 + n + 1)
                    act.activation(y_hi[:, 4 + n, :], yacc[1][:, n, :], ACT.Copy).then_inc(s["yhi"], 1)
                for j in range(J_WOUT + 1, J_WQ + 1):
                    split_hi(j)
                    if j >= J_WOUT + 2:
                        squares_wout(j - J_WOUT - 2)
                norm_act(1, g2)
                split_hi(J_WQ + 1)
                act.wait_ge(s["keyT"], s.had("keyT") + 1)
                act.activation(keysT[:, :, :], ps_o[:, 0:2, :], ACT.Copy).then_inc(s["keyTc"], 1)
                def scores_in(b):
                    for tt in range(NT):
                        k = NT * b + tt
                        act.wait_ge(s["sc"], s.had("sc") + k + 1)
                        act.activation(sc[:, tt, 512 * b:512 * b + 512], ps[:, sc_bank(k), :],
                                       ACT.Copy).then_inc(s["scc"], 1)

                for j in range(J_WQ, NJ):
                    if j + 2 < NJ:
                        split_hi(j + 2)
                    for n in range(2):
                        evac(j, n)
                    if j > J_WQ and (j - J_WQ) % 2 == 0:
                        scores_in((j - J_WQ) // 2 - 1)
                scores_in(3)
                def selected(tt):
                    act.wait_ge(s["ge"], s.had("ge") + tt + 1)
                    act.activation(selv[:, :, :], selv[:, :, :], ACT.Exp).then_inc(s["gexp"], 1)

                def slots_in(tt):
                    act.wait_ge(s["slotT"], s.had("slotT") + tt + 1)
                    act.activation(slotT[:, :, tt * P:tt * P + P],
                                   ps[:, 2, 0:3 * P].rearrange("p (n t) -> p n t", n=3), ACT.Copy).then_inc(s["slotTc"], 1)

                def distances(g, i):
                    for t in range(4):
                        ins = act.activation(dist[i][:, t, :], iota, ACT.Abs, scale=-1.0,
                                             bias=slotT[:, 0, bass.ds(4 * g + t, 1)])
                    ins.then_inc(s["dist"], 1)

                def copy_a(g, i):
                    act.wait_ge(s["g"], s.had("g") + g + 1)
                    act.activation(G[:, bass.ds(4 * g, 4), :],
                                   ps[:, i, :].rearrange("p (t k) -> p t k", t=4), ACT.Copy).then_inc(s["gc"], 1)

                def copy_b(g, i):
                    act.wait_ge(s["gb"], s.had("gb") + g + 1)
                    act.activation(G[:, bass.ds(4 * g + P, 4), :],
                                   ps[:, 4 + i, :].rearrange("p (t k) -> p t k", t=4), ACT.Copy).then_inc(s["gcb"], 1)

                def first_keys(a, g, d, i, nxt, first=False):
                    if nxt is not None:
                        if not (first and a == 0):
                            act.wait_ge(s["oh1"], s.had("oh1") + a)
                        distances(nxt, 1 - d)
                    act.wait_ge(s["dist"], s.had("dist") + a + 1)
                    if not first:
                        act.wait_ge(s["g"], s.had("g") + g - 1)
                    for t in range(4):
                        ins = act.activation(oh1[i][:, t, :], dist[d][:, t, :], ACT.Relu,
                                             scale=nweight[:, bass.ds(4 * g + t, 1)],
                                             bias=slotT[:, 2, bass.ds(4 * g + t, 1)])
                    ins.then_inc(s["oh1"], 1)

                def pre_transposed(c, i):
                    act.wait_ge(s["ut"], s.had("ut") + c + 1)
                    act.activation(p_ut[i][:, :], pre_banks(i), ACT.Copy).then_inc(s["uhi"], 1)

                def pre_gelu(c, i):
                    act.wait_ge(s["s"], s.had("s") + c + 1)
                    act.activation(act_pre[:, c:c + 1, :], ps[:, i:i + 1, 0:SEQ], ACT.Gelu).then_inc(s["gelu"], 1)

                pre_transposed(0, 0)
                pre_transposed(1, 1)
                for c in range(NPRE - 1):
                    pre_gelu(c, c % 2)
                    if c + 2 < NPRE:
                        pre_transposed(c + 2, c % 2)
                    if c == NPRE - 4:
                        selected(0)
                slots_in(0)
                act.wait_ge(s["slotTc"], s.had("slotTc") + 1)
                act.activation(nweight[:, :], slotT[:, 2, 0:P], ACT.Copy, scale=-1.0).then_inc(s["nw"], 1)
                distances(0, 0)
                pre_gelu(NPRE - 1, 1)
                act.wait_ge(s["nw"], s.had("nw") + 1)
                first_keys(0, 0, 0, 0, 1, first=True)
                first_keys(1, 1, 1, 1, 2, first=True)
                copy_a(0, 0)
                with act.Fori(1, EXP_AT // 2) as n:
                    for i in range(2):
                        first_keys(2 * n + i, 2 * n + i, i, i, 2 * n + (i + 1))
                        copy_a(2 * n + (i - 1), 1 - i)
                selected(1)
                for g in range(EXP_AT, ACT_SOLO):
                    first_keys(g, g, g % 2, g % 2, g + 1 if g + 1 < ACT_SOLO else SOLO)
                    copy_a(g - 1, 1 - g % 2)
                slots_in(1)
                copy_a(ACT_SOLO - 1, 1)
                first_keys(ACT_SOLO, SOLO, 0, 0, SOLO + 1)
                for g in range(ACT_SOLO, SOLO):
                    copy_a(g, g % 2)

                def round_(n, last=False):
                    for tile, k in ROUND:
                        if tile == 0 and k in OWN:
                            own = OWN.index(k) + 1
                            if own < 4:
                                nxt = None if last and own == 3 else \
                                    6 * n + (SOLO + (OWN[own + 1] if own < 3 else 6))
                                first_keys(4 * n + (ACT_SOLO + own), 6 * n + (SOLO + OWN[own]), own % 2, OWN[own] % 2, nxt)
                            elif not last:
                                first_keys(4 * n + (ACT_SOLO + 4), 6 * n + (SOLO + 6), 0, 0, 6 * n + (SOLO + 7))
                        if tile == 0:
                            copy_a(6 * n + (SOLO + k), k % 2)
                        else:
                            copy_b(8 * n + k, k % 4)

                with act.Fori(0, ROUNDS - 1) as n:
                    round_(n)
                round_(ROUNDS - 1, last=True)

                def u_split(c, i):
                    act.wait_ge(s["ut"], s.had("ut") + c + 1)
                    act.activation(u_hi[i][:, :], ps_ut, ACT.Copy).then_inc(s["uhi"], 1)

                def cycle(c, i, n, last=False):
                    if not last:
                        act.wait_ge(s["s"], s.had("s") + c)
                        u_split(c + 1, 1 - i)
                    act.wait_ge(s["landv"][i], s.had("landv", i) + 16 * n + 16)
                    act.wait_ge(s["v"], s.had("v") + c - 1)
                    act.activation(v_hi[i][:, :], v_raw[i][:, :], ACT.Copy).then_inc(s["vhi"], 1)
                    act.wait_ge(s["s"], s.had("s") + c + 1)
                    act.wait_ge(s["wl"], s.had("wl") + c)
                    act.activation(wgt[:, :], ps[:, 2 + i, 0:SEQ], ACT.Gelu).then_inc(s["gelu"], 1)
                    act.wait_ge(s["w"], s.had("w") + c + 1)
                    act.activation(w_hi[i][:, :], wgt[:, :], ACT.Copy).then_inc(s["wsp"], 1)

                def weigh(c, i, n, first=False):
                    act.wait_ge(s["landv"][i], s.had("landv", i) + 16 * n + 16)
                    if not first:
                        act.wait_ge(s["v"], s.had("v") + c - 1)
                    act.activation(v_hi[i][:, :], v_raw[i][:, :], ACT.Copy).then_inc(s["vhi"], 1)
                    act.wait_ge(s["w"], s.had("w") + c + 1)
                    act.activation(w_hi[i][:, :], wgt[:, :], ACT.Copy).then_inc(s["wsp"], 1)

                for c in range(NPRE):
                    if c == NPRE - 3:
                        u_split(NPRE, 0)
                    weigh(c, c % 2, c // 2, first=c < 2)
                for i in range(2):
                    cycle(NPRE + i, i, n=NPRE // 2)
                with act.Fori(NPRE // 2 + 1, NK // 2 - 1) as n:
                    for i in range(2):
                        cycle(2 * n + i, i, n=n)
                cycle(NK - 2, 0, n=NK // 2 - 1)
                cycle(NK - 1, 1, last=True, n=NK // 2 - 1)

            act.wait_ge(L[-1]["xnew"], L[-1].had("xnew") + 4)
            for tt in range(NT):
                act.activation(y_out[:, tt, :], x[:, tt, :], ACT.Square, accum_out=ssq[:, tt:tt + 1]).then_inc(s_fss, 1)
            act.wait_ge(s_fms, 1)
            act.activation(rms[:, 0:NT], msq[:, 0:NT], ACT.Sqrt).then_inc(s_frt, 1)

        @block.tensor
        def _(pe):
            pe.wait_ge(s_boot, 16 * 9)
            pe.transpose(ps[:, 0, 0:NVEC], vecs[0:NVEC, :], ident[0:NVEC, 0:NVEC]).then_inc(s_bootT, 1)
            pe.wait_ge(s_vecT, 1)

            def three(out_, a_hi, a_lo, b_hi, b_lo, start, stop):
                pe.matmul(out_, a_hi, b_hi, start=start, stop=False)
                pe.matmul(out_, a_hi, b_lo, start=False, stop=False)
                return pe.matmul(out_, a_lo, b_hi, start=False, stop=stop)

            for l in range(DEPTH):
                s = L[l]
                def project(j, a_hi, a_lo, ready=None):
                    name, _, _, w, kt, last, tokens = JOBS[j]
                    pe.wait_ge(s["wlo"], s.had("wlo") + j + 1)
                    whi, wlo = chunk(wb_hi[buf_of(j)], j), chunk(wb_lo[buf_of(j)], j)
                    def step(k, g, tt, c0, m):
                        b = g % NBANK
                        r = P if k < kt - 1 else last
                        edge = dict(start=k == 0, stop=k == kt - 1)
                        if tokens:
                            t = slice(tt * P, tt * P + P)
                            return three(ps[:, b, 0:m], a_hi[:, k, t], a_lo[:, k, t],
                                         whi[:, k, c0:c0 + m], wlo[:, k, c0:c0 + m], **edge)
                        return three(ps[0:m, b, 0:SEQ], whi[0:r, k, c0:c0 + m], wlo[0:r, k, c0:c0 + m],
                                     a_hi[0:r, k, :], a_lo[0:r, k, :], **edge)

                    def free_bank(g):
                        if g >= NBANK:
                            pe.wait_ge(s["free"][g % NBANK], s.had("free", g % NBANK) + g // NBANK)

                    if ready in ("norm1", "norm2"):
                        for n in range(len(GROUPS[j])):
                            free_bank(FIRST[j] + n)
                        for k in range(kt):
                            pe.wait_ge(s["hlo"], s.had("hlo") + (KD if ready == "norm2" else 0) + k + 1)
                            for n, group in enumerate(GROUPS[j]):
                                mm = step(k, FIRST[j] + n, *group)
                                if k == kt - 1:
                                    mm.then_inc(s["pj"], 1)
                        return
                    for n, group in enumerate(GROUPS[j]):
                        free_bank(FIRST[j] + n)
                        if ready is not None and ready != "y" and n == 0:
                            pe.wait_ge(*ready)
                        for k in range(kt):
                            if ready == "y" and n == 0:
                                pe.wait_ge(s["ylo"], s.had("ylo") + k + 1)
                            mm = step(k, FIRST[j] + n, *group)
                        mm.then_inc(s["pj"], 1)

                def norm_pe(which):
                    pe.wait_ge(s["xn"], s.had("xn") + which + 1)
                    for k in range(KD):
                        for tt in range(NT):
                            mm = pe.transpose(ps_norm[:, k, tt * P:tt * P + P], xn[:, tt, k * P:k * P + P], ident)
                        if k % 2:
                            mm.then_inc(s["xT"], 1)

                def scores(u):
                    br, qt = UNITS[u]
                    N = P * (qt + 1)
                    q = slice(qt * P, qt * P + P)
                    if u:
                        pe.wait_ge(s["sfree"], s.had("sfree") + u)
                    if u == 0:
                        pe.wait_ge(s["mTc"], s.had("mTc") + 6)
                    if u == NT:
                        pe.wait_ge(s["kz"], s.had("kz") + 2)
                    for h in range(HEADS[br]):
                        o = ps_score[:, h, 0:N]
                        if br == 0:
                            mm = pe.matmul(o, mqk[0:MQK, 0, h, q], mqk[0:MQK, 1, h, 0:N], start=True, stop=True)
                            continue
                        r = P if h < 4 else HD
                        mm = pe.matmul(o, qT[0:r, br - 1, h // 2, q], kT[0:r, br - 1, h, 0:N], start=True, stop=br == 1)
                        if br == 2:
                            mm = pe.matmul(o, nlf[:, 0, h:h + 1].to_broadcast([P, P]),
                                           masks[:, M_TRIU:M_TRIU + N], start=False, stop=qt == 0)
                            if qt == 1:
                                mm = pe.matmul(ps_score[:, h, P:N], nlf[:, 1, h:h + 1].to_broadcast([P, P]),
                                               masks[:, M_TRIU:M_TRIU + P], start=False, stop=True)
                    mm.then_inc(s["score"], 1)

                def transpose_probs(u):
                    pe.wait_ge(s["probs"], s.had("probs") + u + 1)
                    if u:
                        pe.wait_ge(s["olo"], s.had("olo") + u)
                    else:
                        pe.wait_ge(s["cumc"], s.had("cumc") + 1)
                    for n, batch in enumerate(pt_batches(u)):
                        if PT0[u] + n > 1:
                            pe.wait_ge(s["ptc"], s.had("ptc") + PT0[u] + n - 1)
                        for i, (h, kt) in enumerate(batch):
                            mm = pe.transpose(ps[:, pt_bank(u, n), i * P:i * P + P], A[:, h, kt * P:kt * P + P], ident)
                        mm.then_inc(s["pt"], 1)

                def pv(u):
                    br, qt = UNITS[u]
                    H = HEADS[br]
                    pe.wait_ge(s["ptc"], s.had("ptc") + PT0[u + 1])
                    v = (v_m, v_s, v_f)[br]
                    for h in range(H):
                        r = slice(64 * (h % 2), 64 * (h % 2) + 64)
                        for kt in range(qt + 1):
                            mm = pe.matmul(ps_o[r, h // 2, :], v[:, kt, h * HD:h * HD + HD],
                                           PT[:, h * (qt + 1) + kt, :], start=kt == 0, stop=kt == qt)
                    mm.then_inc(s["pv"], 1)

                norm_pe(0)
                project(0, h_hi, h_lo, "norm1")
                project(1, h_hi, h_lo)
                project(2, h_hi, h_lo)
                pe.wait_ge(s["cn"], s.had("cn") + 1)
                for k in range(3):
                    for tt in range(NT):
                        src = cq[:, tt, k * P:k * P + P] if k < 2 else ckv[:, tt, 0:KVL]
                        mm = pe.transpose(ps_norm[:, k, tt * P:tt * P + P], src, ident)
                mm.then_inc(s["cT"], 1)
                project(3, h_hi, h_lo)
                project(4, c_hi, c_lo, (s["clo"], s.had("clo") + 3))
                project(5, h_hi, h_lo)
                project(6, c_hi[:, 2:3, :], c_lo[:, 2:3, :])
                project(7, h_hi, h_lo)
                project(8, h_hi, h_lo)
                pe.wait_ge(s["rope"], s.had("rope") + 1)
                for n in range(6):
                    if n >= 3:
                        pe.wait_ge(s["mTc"], s.had("mTc") + n - 2)
                    for h in (2 * (n % 3), 2 * (n % 3) + 1):
                        for tt in range(NT):
                            src = q_tok[:, tt, h * MQK:h * MQK + MQK] if n < 3 else k_full[:, tt, h, :]
                            mm = pe.transpose(ps_score[0:MQK, h, tt * P:tt * P + P], src, ident)
                    mm.then_inc(s["mT"], 1)
                project(9, h_hi, h_lo)
                pe.wait_ge(s["masks"], s.had("masks") + 16)
                scores(0)
                for u in range(NU):
                    for j in BEFORE[u]:
                        project(j, h_hi, h_lo)
                    if u == 0:
                        pe.wait_ge(s["lf"], s.had("lf") + 1)
                        pe.matmul(ps[:, 7, 0:FH], masks[:, M_TRIU:M_TRIU + P], lf[:, 0, :], start=True, stop=True)
                        pe.matmul(ps[:, 7, 8:8 + FH], masks[:, M_TRIU + P:M_TRIU + 2 * P], lf[:, 0, :], start=True,
                                  stop=False)
                        pe.matmul(ps[:, 7, 8:8 + FH], masks[:, M_TRIU:M_TRIU + P], lf[:, 1, :], start=False,
                                  stop=True).then_inc(s["cum"], 1)
                    transpose_probs(u)
                    if u + 1 < NU:
                        scores(u + 1)
                    for j in AFTER[u]:
                        project(j, h_hi, h_lo)
                    if u + 1 < NU:
                        pv(u)
                for j in range(J_WO, J_WO + 6):
                    br = (j - J_WO) % 3
                    project(j, o_hi[:, br], o_lo[:, br], (s["olo"], s.had("olo") + NT * (br + 1)))
                    if j == J_WO:
                        pv(NU - 1)
                for j in range(J_WOUT, J_WOUT + 4):
                    project(j, y_hi, y_lo, "y" if j == J_WOUT else None)
                norm_pe(1)
                pe.wait_ge(s["keys"], s.had("keys") + 16)
                for i in range(2):
                    mm = pe.transpose(ps_o[:, i, :], keys[:, i, :], ident)
                mm.then_inc(s["keyT"], 1)
                def key_scores(b):
                    for g in range(FIRST[J_WQ + 2 * b], FIRST[J_WQ + 2 * b + 2]):
                        pe.wait_ge(s["free"][g % NBANK], s.had("free", g % NBANK) + g // NBANK + 1)
                    for tt in range(NT):
                        k = NT * b + tt
                        if k >= 5:
                            pe.wait_ge(s["scc"], s.had("scc") + k - 4)
                        for i in range(4):
                            n = 4 * b + i
                            mm = pe.matmul(ps[:, sc_bank(k), i * P:i * P + P], pq[:, n, tt * P:tt * P + P],
                                           keysT[:, n % 2, :], start=True, stop=True)
                        mm.then_inc(s["sc"], 1)

                for j in range(J_WQ, NJ):
                    project(j, h_hi, h_lo, "norm2" if j == J_WQ else None)
                    if j == J_WQ:
                        pe.wait_ge(s["keyTc"], s.had("keyTc") + 1)
                    elif (j - J_WQ) % 2 == 0:
                        key_scores((j - J_WQ) // 2 - 1)
                key_scores(3)
                def pre_transpose(c, i):
                    pe.wait_ge(s["landp"][i], s.had("landp", i) + 16 * (c // 2 + 1))
                    if c >= 2:
                        pe.wait_ge(s["uhi"], s.had("uhi") + c - 1)
                    for k in range(KD):
                        mm = pe.transpose(pre_banks(i)[:, k * P:k * P + P], p_raw[i][:, k * P:k * P + P], ident)
                    mm.then_inc(s["ut"], 1)

                pe.wait_ge(s["scc"], s.had("scc") + 5)
                pre_transpose(0, 0)
                pe.wait_ge(s["scc"], s.had("scc") + 8)
                pre_transpose(1, 1)
                pe.wait_ge(s["hf"], s.had("hf") + 1)

                def pre_activations(c):
                    i = c % 2
                    pe.wait_ge(s["uhi"], s.had("uhi") + c + 1)
                    if c >= 2:
                        pe.wait_ge(s["gelu"], s.had("gelu") + c - 1)
                    for k in range(KD):
                        mm = pe.matmul(ps[:, i, 0:SEQ], p_ut[i][:, k * P:k * P + P], h_full[:, k, :],
                                       start=k == 0, stop=k == KD - 1)
                    mm.then_inc(s["s"], 1)
                    if c + 2 < NPRE:
                        pre_transpose(c + 2, i)

                for c in range(NPRE - 1):
                    pre_activations(c)

                def slots_out(tt):
                    if tt:
                        pe.wait_ge(s["slotTc"], s.had("slotTc") + tt)
                    pe.wait_ge(s["slot"], s.had("slot") + tt + 1)
                    for n in range(3):
                        mm = pe.transpose(ps[:, 2, n * P:n * P + P], slots[:, n, :], ident)
                    mm.then_inc(s["slotT"], 1)

                def weights_a(g, i, ready, count, reuse=True):
                    pe.wait_ge(s[ready], s.had(ready) + count)
                    pe.wait_ge(s["oh2"], s.had("oh2") + g + 1)
                    if reuse:
                        pe.wait_ge(s["gc"], s.had("gc") + g - 1)
                    for t in range(4):
                        mm = pe.matmul(ps[:, i, t * P:t * P + P], oh2[i][:, t, :], oh1[i][:, t, :],
                                       start=True, stop=True)
                    mm.then_inc(s["g"], 1)

                def weights_b(g, i, reuse=True):
                    pe.wait_ge(s["oh1b"], s.had("oh1b") + g + 1)
                    pe.wait_ge(s["oh2b"], s.had("oh2b") + g + 1)
                    if reuse:
                        pe.wait_ge(s["gcb"], s.had("gcb") + g - 3)
                    for t in range(4):
                        mm = pe.matmul(ps[:, 4 + i, t * P:t * P + P], oh2b[i % 2][:, t, :], oh1b[i % 2][:, t, :],
                                       start=True, stop=True)
                    mm.then_inc(s["gb"], 1)

                slots_out(0)
                pre_activations(NPRE - 1)
                pe.wait_ge(s["gelu"], s.had("gelu") + NPRE)
                weights_a(0, 0, "oh1", 1, reuse=False)
                weights_a(1, 1, "oh1", 2, reuse=False)
                with pe.Fori(1, ACT_SOLO // 2) as n:
                    for i in range(2):
                        weights_a(2 * n + i, i, "oh1", 2 * n + (i + 1))
                slots_out(1)
                for g in range(ACT_SOLO, SOLO):
                    weights_a(g, g % 2, "oh1v", g + 1 - ACT_SOLO)

                def round_(n, first=False):
                    for tile, k in ROUND:
                        if tile:
                            weights_b(8 * n + k, k % 4, reuse=not first or k >= 4)
                        elif k in OWN:
                            weights_a(6 * n + (SOLO + k), k % 2, "oh1", 4 * n + (ACT_SOLO + OWN.index(k) + 1))
                        else:
                            weights_a(6 * n + (SOLO + k), k % 2, "oh1v",
                                      2 * n + (SOLO - ACT_SOLO + (k + 1) // 3))

                round_(0, first=True)
                with pe.Fori(1, ROUNDS) as n:
                    round_(n)

                def transpose_block(c, i, n):
                    pe.wait_ge(s["landu"][i], s.had("landu", i) + 16 * n + (16 - 8 * NPRE))
                    for k in range(KD):
                        mm = pe.transpose(ps_ut[:, k * P:k * P + P], u_raw[i][:, k * P:k * P + P], ident)
                    mm.then_inc(s["ut"], 1)

                def activations(c, i):
                    pe.wait_ge(s["ulo"], s.had("ulo") + c + (1 - NPRE))
                    pe.wait_ge(s["gelu"], s.had("gelu") + c - 1)
                    for k in range(KD):
                        e = slice(k * P, k * P + P)
                        mm = three(ps[:, 2 + i, 0:SEQ], u_hi[i][:, e], u_lo[i][:, e], h_hi[:, k, :], h_lo[:, k, :],
                                   k == 0, k == KD - 1)
                    mm.then_inc(s["s"], 1)

                def combine(c, i, start=False, stop=False):
                    pe.wait_ge(s["wl"], s.had("wl") + c + 1)
                    for tt in range(NT):
                        t = slice(tt * P, tt * P + P)
                        for hf in range(2):
                            o, d = ps[:, 4 + 2 * tt + hf, :], slice(512 * hf, 512 * hf + 512)
                            pe.matmul(o, w_hi[i][:, t], v_hi[i][:, d], start=start, stop=False)
                            pe.matmul(o, w_hi[i][:, t], v_lo[i][:, d], start=False, stop=False)
                        for hf in range(2):
                            o, d = ps[:, 4 + 2 * tt + hf, :], slice(512 * hf, 512 * hf + 512)
                            mm = pe.matmul(o, w_lo[i][:, t], v_hi[i][:, d], start=False, stop=stop)
                    mm.then_inc(s["v"], 1)

                pe.wait_ge(s["gcb"], s.had("gcb") + NGR)
                for c in range(NPRE - 1):
                    combine(c, c % 2, start=c == 0)
                    if c == NPRE - 5:
                        pe.wait_ge(s["gc"], s.had("gc") + NGR)
                        transpose_block(NPRE, 0, NPRE // 2)
                with pe.Fori(NPRE // 2, NK // 2 - 1) as n:
                    for i in range(2):
                        c = 2 * n + i
                        pe.wait_ge(s["ulo"], s.had("ulo") + c + (1 - NPRE))
                        transpose_block(c + 1, 1 - i, n + i)
                        activations(c, i)
                        combine(c - 1, 1 - i)
                c = NK - 2
                pe.wait_ge(s["ulo"], s.had("ulo") + c + 1 - NPRE)
                transpose_block(c + 1, 1, NK // 2 - 1)
                activations(c, 0)
                combine(c - 1, 1)
                activations(c + 1, 1)
                combine(c, 0)
                combine(c + 1, 1, stop=True)

        @block.vector
        def _(dve):
            count = [0]

            def link(ins):
                count[0] += 1
                ins.then_inc(s_dve, 1)
                dve.wait_ge(s_dve, count[0])

            dve.wait_ge(s_boot, 16 * 9)
            link(dve.tensor_copy(pos[:, :], pos_i[:, :]))
            for tt in range(NT):
                ins = dve.tensor_scalar(ang[:, tt, :], cst[:, C_FREQ:C_EPS], pos[:, tt:tt + 1], None, ALU.mult)
            link(ins)
            link(dve.tensor_scalar(turns_i[:, :, :], ang[:, :, :], INV_SQRT2PI, None, ALU.mult))
            link(dve.tensor_copy(turns[:, :, :], turns_i[:, :, :]))
            for part in TWO_PI:
                link(dve.scalar_tensor_tensor(out=ang[:, :, :], in0=turns[:, :, :], scalar=-part, in1=ang[:, :, :],
                                              op0=ALU.mult, op1=ALU.add))
            dve.tensor_scalar(ang[:, :, :], ang[:, :, :], PI_IN, -PI_IN, ALU.min, ALU.max).then_inc(s_ang, 1)
            dve.wait_ge(s_sin, 2)
            link(dve.tensor_tensor(half_s[:, :, :], half_s[:, :, :], half_s[:, :, :], ALU.mult))
            link(dve.tensor_scalar(trig[:, :, 0, :], half_s[:, :, :], -2.0, 1.0, ALU.mult, ALU.add))

            for l in range(DEPTH):
                s = L[l]

                def split_lo(j):
                    dve.wait_ge(s["whi"], s.had("whi") + j + 1)
                    for rows, k0, k1 in parts(j):
                        ins = dve.tensor_tensor(chunk(wb_lo[buf_of(j)], j)[0:rows, k0:k1, :],
                                                chunk(raw_of(j), j)[0:rows, k0:k1, :],
                                                chunk(wb_hi[buf_of(j)], j)[0:rows, k0:k1, :].bitcast(F32), ALU.subtract)
                    ins.then_inc(s["wlo"], 1)

                def norm_dve(which, gain):
                    parts_ = (2, 4)[which]
                    dve.wait_ge(s["ss"], s.had("ss") + (2 * NT, 6 * NT)[which])
                    dve.tensor_reduce(msq[:, 0:NT], ssq4[:, :, 0:parts_], AX.X, ALU.add).then_inc(s["ms"], 1)
                    dve.wait_ge(s["rt"], s.had("rt") + which + 1)
                    link(dve.reciprocal(rstd[:, 0:NT], rms[:, 0:NT]))
                    for tt in range(NT):
                        ins = dve.tensor_scalar(xn[:, tt, :], x[:, tt, :], rstd[:, tt:tt + 1], None, ALU.mult)
                    ins.then_inc(s["xn"], 1)
                    if which == 0:
                        split_lo(0)
                    for k in range(KD):
                        if k % 2 == 0:
                            dve.wait_ge(s["hhi"], s.had("hhi") + which * KD + k + 2)
                        c = gain(l, k)
                        dve.scalar_tensor_tensor(out=h_lo[:, k, :], in0=ps_norm[:, k, :], scalar=vecT[:, c:c + 1],
                                                 in1=h_hi[:, k, :].bitcast(F32), op0=ALU.mult,
                                                 op1=ALU.subtract).then_inc(s["hlo"], 1)

                def group(j, n):
                    g = FIRST[j] + n
                    dve.wait_ge(s["pj"], s.had("pj") + g + 1)
                    return g % NBANK

                def evac_tokens(j, dst):
                    for n, (tt, c0, m) in enumerate(GROUPS[j]):
                        b = group(j, n)
                        w = min(m, dst.shape[-1])
                        ins = dve.tensor_copy(dst[:, tt, c0:c0 + w], ps[:, b, 0:w])
                        ins.then_inc(s["free"][b], 1)
                    return ins

                def written(j):
                    for g in range(max(FIRST[j], FIRST[j + 1] - NBANK), FIRST[j + 1]):
                        dve.wait_ge(s["free"][g % NBANK], s.had("free", g % NBANK) + g // NBANK + 1)

                def rotate(src, dst, tt, heads):
                    w = MROPE // 2
                    cos = trig[:, tt, 0, :].unsqueeze(1).to_broadcast([P, heads, w])
                    sin = trig[:, tt, 1, :].unsqueeze(1).to_broadcast([P, heads, w])
                    r = [rope_t[:, n, 0:heads, :] for n in range(4)]
                    dve.tensor_tensor(r[0], src[:, :, 0:w], cos, ALU.mult)
                    dve.tensor_tensor(r[1], src[:, :, w:2 * w], sin, ALU.mult)
                    dve.tensor_tensor(r[2], src[:, :, 0:w], sin, ALU.mult)
                    link(dve.tensor_tensor(r[3], src[:, :, w:2 * w], cos, ALU.mult))
                    dve.tensor_tensor(dst[:, :, 0:w], r[0], r[1], ALU.subtract)
                    link(dve.tensor_tensor(dst[:, :, w:2 * w], r[2], r[3], ALU.add))

                def softmax_dve(u, part, splits=()):
                    br, qt = UNITS[u]
                    H, N = HEADS[br], P * (qt + 1)
                    m0 = P * (1 - qt)
                    Au, Bu, Cu = (t[:, 0:H, 0:N] for t in (A, B, C))
                    zu = ps_score[:, 0:H, 0:N]
                    if br == 1:
                        strict = masks[:, M_STRICT + m0:M_STRICT + 2 * P].unsqueeze(1).to_broadcast([P, H, N])
                        if part == 0:
                            dve.wait_ge(s["ab"], s.had("ab") + qt + 1)
                            link(dve.scalar_tensor_tensor(out=Bu, in0=zu, scalar=0.0, in1=Au, op0=ALU.max, op1=ALU.add))
                            link(dve.tensor_tensor(Cu, Bu, strict, ALU.mult))
                            for h in range(H):
                                dve.tensor_tensor_scan(A[:, h, 0:N], C[:, h, 0:N], C[:, h, 0:N], 0.0, ALU.add, ALU.max)
                            for j in splits:
                                split_lo(j)
                            ins = dve.tensor_tensor(Bu, zu, Bu, ALU.subtract)
                            ins.then_inc(s["sfree"], 1)
                            dve.wait_ge(s["sfree"], s.had("sfree") + u + 1)
                            dve.tensor_tensor(Bu, Bu, Au, ALU.add)
                            dve.tensor_scalar(ntot[:, 0:H], A[:, 0:H, N - 1], -1.0, None, ALU.mult).then_inc(s["sb_w"], 1)
                        else:
                            dve.wait_ge(s["ex"], s.had("ex") + qt + 1)
                            dve.tensor_tensor(Au[:, :, N - P:N], Au[:, :, N - P:N], strict[:, :, N - P:N],
                                              ALU.mult).then_inc(s["probs"], 1)
                        return
                    base_ = M_MLA if br == 0 else M_FOX
                    allow = masks[:, base_ + m0:base_ + 2 * P]
                    if part == 0:
                        dve.wait_ge(s["score"], s.had("score") + u + 1)
                        if u:
                            dve.wait_ge(s["pt"], s.had("pt") + PT0[u])
                        if br == 0:
                            ins = dve.tensor_tensor(Au, zu, allow.unsqueeze(1).to_broadcast([P, H, N]), ALU.add)
                        else:
                            for h in range(H):
                                ins = dve.scalar_tensor_tensor(out=A[:, h, 0:N], in0=ps_score[:, h, 0:N],
                                                               scalar=cumq[:, qt, h:h + 1], in1=allow,
                                                               op0=ALU.add, op1=ALU.add)
                        ins.then_inc(s["sfree"], 1)
                        dve.wait_ge(s["sfree"], s.had("sfree") + u + 1)
                        link(dve.tensor_reduce(mx[:, 0:H], Au, AX.X, ALU.max))
                        dve.tensor_scalar(nmx[:, 0:H], mx[:, 0:H], -(SCALE_A if br == 0 else SCALE_H), None,
                                          ALU.mult).then_inc(s["pmax"], 1)
                    else:
                        dve.wait_ge(s["pexp"], s.had("pexp") + (u + 1 if br == 0 else u - 1))
                        link(dve.reciprocal(rsum[:, 0:H], esum[:, 0:H]))
                        dve.tensor_tensor(Au, Au, rsum[:, 0:H].unsqueeze(2).to_broadcast([P, H, N]),
                                          ALU.mult).then_inc(s["probs"], 1)

                def pv_dve(u):
                    br, qt = UNITS[u]
                    cols = slice(qt * P, (qt + 1) * P)
                    dve.wait_ge(s["ohi"], s.had("ohi") + u + 1)
                    pieces = [(P, 0, 3)] if HEADS[br] % 2 == 0 else [(P, 0, 2), (64, 2, 3)]
                    for r, a, b in pieces:
                        ins = dve.tensor_tensor(o_lo[0:r, br, a:b, cols], ps_o[0:r, a:b, :],
                                                o_hi[0:r, br, a:b, cols].bitcast(F32), ALU.subtract)
                    ins.then_inc(s["olo"], 1)

                norm_dve(0, g1)
                split_lo(1)
                evac_tokens(0, cq)
                split_lo(2)
                evac_tokens(1, ckv)
                dve.wait_ge(s["cms"], s.had("cms") + 1)
                dve.tensor_scalar(msq[:, 0:4:2], ssq[:, 0:4:2], 1.0 / QL, EPS, ALU.mult, ALU.add)
                dve.tensor_scalar(msq[:, 1:4:2], ssq[:, 1:4:2], 1.0 / KVL, EPS, ALU.mult, ALU.add).then_inc(s["cms"], 1)
                split_lo(3)
                dve.wait_ge(s["crt"], s.had("crt") + 1)
                link(dve.reciprocal(rstd[:, 0:4], rms[:, 0:4]))
                for tt in range(NT):
                    dve.tensor_scalar(cq[:, tt, :], cq[:, tt, :], rstd[:, 2 * tt:2 * tt + 1], None, ALU.mult)
                    ins = dve.tensor_scalar(ckv[:, tt, 0:KVL], ckv[:, tt, 0:KVL], rstd[:, 2 * tt + 1:2 * tt + 2],
                                            None, ALU.mult)
                ins.then_inc(s["cn"], 1)
                split_lo(4)
                split_lo(5)
                dve.wait_ge(s["chi"], s.had("chi") + 3)
                for k in range(3):
                    c = gq(l, k) if k < 2 else gkv(l)
                    dve.scalar_tensor_tensor(out=c_lo[:, k, :], in0=ps_norm[:, k, :], scalar=vecT[:, c:c + 1],
                                             in1=c_hi[:, k, :].bitcast(F32), op0=ALU.mult,
                                             op1=ALU.subtract).then_inc(s["clo"], 1)
                evac_tokens(4, q_tok)
                split_lo(6)
                split_lo(7)
                evac_tokens(5, v_s)
                for n, (tt, c0, m) in enumerate(GROUPS[6]):
                    b = group(6, n)
                    h0 = c0 // (MNOPE + MV)
                    src = ps[:, b, 0:m].rearrange("p (h e) -> p h e", h=3)
                    dve.tensor_copy(k_full[:, tt, h0:h0 + 3, 0:MNOPE], src[:, :, 0:MNOPE])
                    ins = dve.tensor_copy(v_m[:, tt, h0 * MV:(h0 + 3) * MV].rearrange("p (h e) -> p h e", h=3),
                                          src[:, :, MNOPE:])
                    ins.then_inc(s["free"][b], 1)
                split_lo(8)
                for tt in range(NT):
                    q3 = q_tok[:, tt, :].rearrange("p (h e) -> p h e", h=MH)[:, :, MNOPE:]
                    rotate(q3, q3, tt, MH)
                    kr = ckv[:, tt, KVL:KVL + MROPE].unsqueeze(1)
                    rotate(kr, kr, tt, 1)
                    ins = dve.tensor_copy(k_full[:, tt, :, MNOPE:], kr.to_broadcast([P, MH, MROPE]))
                ins.then_inc(s["rope"], 1)
                split_lo(9)
                split_lo(10)
                evac_tokens(9, v_f)
                written(9)
                f = v_f[:, :, W3:W3 + FH]
                link(dve.tensor_tensor(f, f, bf[:, l, :].unsqueeze(1).to_broadcast([P, NT, FH]), ALU.add))
                link(dve.tensor_scalar(nlf[:, :, :], f, -1.0, None, ALU.mult))
                dve.tensor_tensor(nlf[:, :, :], nlf[:, :, :], f, ALU.min).then_inc(s["fz"], 1)
                dve.wait_ge(s["masks"], s.had("masks") + 16)
                softmax_dve(0, 0)
                dve.wait_ge(s["fe"], s.had("fe") + 2)
                link(dve.scalar_tensor_tensor(out=lf[:, :, :], in0=f, scalar=0.0, in1=lf[:, :, :], op0=ALU.min,
                                              op1=ALU.subtract))
                link(dve.tensor_scalar(nlf[:, :, :], lf[:, :, :], -1.0 / SCALE_H, None, ALU.mult))
                dve.tensor_scalar(lf[:, :, :], lf[:, :, :], 1.0 / SCALE_H, None, ALU.mult).then_inc(s["lf"], 1)
                for u in range(NU):
                    softmax_dve(u, 1)
                    if u == 0:
                        dve.wait_ge(s["cum"], s.had("cum") + 1)
                        dve.tensor_copy(cumq[:, :, :], ps[:, 7, 0:16].rearrange("p (t h) -> p t h", t=NT)[:, :, 0:FH])\
                           .then_inc(s["cumc"], 1)
                        dve.wait_ge(s["cumc"], s.had("cumc") + 1)
                    for j in BEFORE[u] + AFTER[u][:1]:
                        split_lo(j + 1)
                    if u + 1 < NU:
                        softmax_dve(u + 1, 0, [j + 1 for j in AFTER[u][1:]])
                        pv_dve(u)
                def y_split(hf):
                    for n in range(4):
                        dve.wait_ge(s["yhi"], s.had("yhi") + 4 * hf + n + 1)
                        dve.tensor_tensor(y_lo[:, 4 * hf + n, :], yacc[hf][:, n, :],
                                          y_hi[:, 4 * hf + n, :].bitcast(F32), ALU.subtract).then_inc(s["ylo"], 1)

                for hf in range(2):
                    for br in range(3):
                        j = J_WO + 3 * hf + br
                        split_lo(j + 1)
                        dve.wait_ge(s["sig"], s.had("sig") + br + 1)
                        for n in range(4):
                            b = group(j, n)
                            gt = gates[:, 8 * br + 4 * hf + n, :]
                            if br == 0:
                                dve.tensor_tensor(yacc[hf][:, n, :], ps[:, b, 0:SEQ], gt, ALU.mult).then_inc(s["free"][b], 1)
                                continue
                            if hf or br == 2:
                                dve.wait_ge(s["yadd"], s.had("yadd") + 8 * hf + 4 * (br - 2) + n + 1)
                            dve.tensor_tensor(ytmp[:, n, :], ps[:, b, 0:SEQ], gt, ALU.mult).then_inc(s["free"][b], 1)
                        if j == J_WO:
                            pv_dve(NU - 1)
                        if j == J_WO + 3:
                            y_split(0)
                y_split(1)
                for j in range(J_WOUT, J_WOUT + 4):
                    split_lo(j + 1)
                    c0 = 256 * (j - J_WOUT)
                    for n in range(NT):
                        b = group(j, n)
                        xs = x[:, n, c0:c0 + 256]
                        dve.tensor_tensor(xs, xs, ps[:, b, 0:256], ALU.add).then_inc(s["free"][b], 1)
                norm_dve(1, g2)
                def top16(arrays, vals, idx):
                    for n, a in enumerate(arrays):
                        ins = dve.max(vals[:, n, 0:8], a)
                    link(ins)
                    for n, a in enumerate(arrays):
                        dve.max_index(idx[:, n, 0:8], vals[:, n, 0:8], a)
                    for n, a in enumerate(arrays):
                        ins = dve.match_replace(a, vals[:, n, 0:8], a, LOWEST)
                    link(ins)
                    for n, a in enumerate(arrays):
                        ins = dve.max(vals[:, n, 8:16], a)
                    link(ins)
                    for n, a in enumerate(arrays):
                        ins = dve.max_index(idx[:, n, 8:16], vals[:, n, 8:16], a)
                    link(ins)

                def key_lists(b, tt):
                    dve.wait_ge(s["scc"], s.had("scc") + NT * b + tt + 1)
                    top16([sc[:, tt, n * NK:n * NK + NK] for n in range(4 * b, 4 * b + 4)],
                          vtops[tt][:, 4 * b:4 * b + 4, :], itops[tt][:, 4 * b:4 * b + 4, :])

                split_lo(J_WQ + 1)
                for b in range(3):
                    for j in range(J_WQ + 2 * b + 2, J_WQ + 2 * b + 4):
                        split_lo(j)
                        if j == J_WQ + 2 * b + 2 and b:
                            key_lists(b - 1, 1)
                    key_lists(b, 0)
                key_lists(2, 1)
                for tt in range(NT):
                    vtop, itop = vtops[tt], itops[tt]
                    key_lists(3, tt)
                    link(dve.tensor_copy(itf[:, :, :], itop[:, :, :]))
                    v2 = vtop[:, :, :].rearrange("p (h s) a -> p h s a", s=2)
                    for a0, na, nb in SEGMENTS:
                        o = cand[:, :, STARTS[a0]:STARTS[a0] + na * nb]
                        if na == 1:
                            ins = dve.tensor_tensor(o, v2[:, :, 0, a0:a0 + 1].to_broadcast([P, PH, nb]),
                                                    v2[:, :, 1, 0:nb], ALU.add)
                        elif nb == 1:
                            ins = dve.tensor_tensor(o, v2[:, :, 0, a0:a0 + na],
                                                    v2[:, :, 1, 0:1].to_broadcast([P, PH, na]), ALU.add)
                        else:
                            ins = dve.tensor_tensor(
                                o.rearrange("p h (a b) -> p h a b", b=nb),
                                v2[:, :, 0, a0:a0 + na].unsqueeze(3).to_broadcast([P, PH, na, nb]),
                                v2[:, :, 1, 0:nb].unsqueeze(2).to_broadcast([P, PH, na, nb]), ALU.add)
                    link(ins)
                    top16([cand[:, h, :] for h in range(PH)], selv, selp)
                    link(dve.tensor_copy(posf[:, :], selp[:, :, :].rearrange("p h k -> p (h k)")))
                    dve.tensor_copy(gsum[:, 0, :], selv[:, :, 0])
                    link(dve.tensor_copy(gsum[:, 1, :], selv[:, :, 0]))
                    dve.tensor_tensor(selv[:, :, :], selv[:, :, :], gsum[:, 0, :].unsqueeze(2).to_broadcast([P, PH, 16]),
                                      ALU.subtract).then_inc(s["ge"], 1)
                    tmp = sc[:, tt, :].rearrange("p (n a) -> p n a", a=16)
                    tmp4 = sc[:, tt, :].rearrange("p (h n a) -> p h n a", h=PH, a=16)
                    i4 = itf[:, :, :].rearrange("p (h s) a -> p h s a", s=2)

                    def bc(c0):
                        return cst[:, c0:c0 + 16].unsqueeze(1).to_broadcast([P, P, 16])

                    def keys16(t):
                        return t.unsqueeze(2).to_broadcast([P, PH, 16, 16])

                    dve.tensor_copy(dtop[:, :, 0:1], i4[:, :, 0, 0:1])
                    dve.tensor_tensor(dtop[:, :, 1:16], i4[:, :, 0, 1:16], i4[:, :, 0, 0:15], ALU.subtract)
                    steps = posf[:, :].unsqueeze(2).to_broadcast([P, P, 16])
                    link(dve.tensor_tensor(tmp, steps, bc(C_START), ALU.is_ge))
                    link(dve.tensor_tensor(dtop[:, :, :], dtop[:, :, :],
                                           cst[:, C_DSTART:C_DSTART + 16].unsqueeze(1).to_broadcast([P, PH, 16]),
                                           ALU.add))
                    link(dve.tensor_tensor(tmp4, tmp4, keys16(dtop[:, :, :]), ALU.mult))
                    link(dve.tensor_reduce(sub[:, :], tmp, AX.X, ALU.add))
                    link(dve.tensor_scalar(start_i[:, :], sub[:, :], 1.0 / PACK, None, ALU.mult))
                    link(dve.tensor_copy(startf[:, :], start_i[:, :]))
                    if tt:
                        dve.wait_ge(s["slotT"], s.had("slotT") + tt)
                    dve.scalar_tensor_tensor(out=slots[:, 0, :], in0=startf[:, :], scalar=-float(PACK),
                                             in1=sub[:, :], op0=ALU.mult, op1=ALU.add)
                    link(dve.tensor_tensor(posf[:, :], posf[:, :], startf[:, :], ALU.subtract))
                    link(dve.tensor_tensor(tmp, steps, bc(C_I16), ALU.is_equal))
                    link(dve.tensor_tensor(tmp4, tmp4, keys16(i4[:, :, 1, :]), ALU.mult))
                    link(dve.tensor_reduce(slots[:, 1, :], tmp, AX.X, ALU.add))
                    dve.wait_ge(s["gexp"], s.had("gexp") + tt + 1)
                    link(dve.tensor_reduce(gsum[:, 0, :], selv[:, :, :], AX.X, ALU.add))
                    link(dve.reciprocal(gsum[:, 1, :], gsum[:, 0, :]))
                    dve.tensor_tensor(slots[:, 2, :].rearrange("p (h k) -> p h k", h=PH), selv[:, :, :],
                                      gsum[:, 1, :].unsqueeze(2).to_broadcast([P, PH, 16]),
                                      ALU.mult).then_inc(s["slot"], 1)
                def first_keys(g, i):
                    dve.wait_ge(s["g"], s.had("g") + g - 1)
                    for t in range(4):
                        ins = dve.tensor_scalar(oh1[i][:, t, :], iota, slotT[:, 0, bass.ds(4 * g + t, 1)],
                                                slotT[:, 2, bass.ds(4 * g + t, 1)], ALU.is_equal, ALU.mult)
                    ins.then_inc(s["oh1v"], 1)

                def one_hot(g, i, reuse=True):
                    if reuse:
                        dve.wait_ge(s["gb"], s.had("gb") + g - 1)
                    for t in range(4):
                        ins = dve.tensor_scalar(oh1b[i][:, t, :], iota, slotT[:, 0, bass.ds(4 * g + (P + t), 1)],
                                                slotT[:, 2, bass.ds(4 * g + (P + t), 1)], ALU.is_equal, ALU.mult)
                    ins.then_inc(s["oh1b"], 1)
                    dve.tensor_tensor(oh2b[i][:, :, :], iota.unsqueeze(1).to_broadcast([P, 4, NK]),
                                      slotT[:, 1, bass.ds(4 * g + P, 4)].unsqueeze(2).to_broadcast([P, 4, NK]),
                                      ALU.is_equal).then_inc(s["oh2b"], 1)

                dve.wait_ge(s["slotTc"], s.had("slotTc") + 1)
                for g in range(ACT_SOLO, SOLO):
                    first_keys(g, g % 2)
                dve.wait_ge(s["slotTc"], s.had("slotTc") + NT)

                def round_(n, first=False):
                    for tile, k in ROUND:
                        if tile:
                            one_hot(8 * n + k, k % 2, reuse=not first or k >= 2)
                        elif k not in OWN:
                            first_keys(6 * n + (SOLO + k), k % 2)

                round_(0, first=True)
                with dve.Fori(1, ROUNDS) as n:
                    round_(n)

                def u_split(c, i):
                    dve.wait_ge(s["uhi"], s.had("uhi") + c + 1)
                    dve.tensor_tensor(u_lo[i][:, :], ps_ut, u_hi[i][:, :].bitcast(F32), ALU.subtract)\
                       .then_inc(s["ulo"], 1)

                def cycle(c, i, last=False):
                    if not last:
                        u_split(c + 1, 1 - i)
                    dve.wait_ge(s["vhi"], s.had("vhi") + c + 1)
                    dve.tensor_tensor(v_lo[i][:, :], v_raw[i][:, :], v_hi[i][:, :].bitcast(F32), ALU.subtract)\
                       .then_inc(s["vlo"], 1)
                    dve.wait_ge(s["gelu"], s.had("gelu") + c + 1)
                    w1 = wgt[:, :].unsqueeze(2)
                    dve.tensor_tensor(w1, w1, G[:, :, bass.ds(c, 1)], ALU.mult).then_inc(s["w"], 1)
                    dve.wait_ge(s["wsp"], s.had("wsp") + c + 1)
                    dve.tensor_tensor(w_lo[i][:, :], wgt[:, :], w_hi[i][:, :].bitcast(F32), ALU.subtract)\
                       .then_inc(s["wl"], 1)

                def weigh(c, i):
                    if c:
                        dve.wait_ge(s["wl"], s.had("wl") + c)
                    else:
                        dve.wait_ge(s["gcb"], s.had("gcb") + NGR)
                        dve.wait_ge(s["gc"], s.had("gc") + NGR)
                    dve.tensor_tensor(wgt[:, :].unsqueeze(2), act_pre[:, c, :].unsqueeze(2), G[:, :, c:c + 1],
                                      ALU.mult).then_inc(s["w"], 1)
                    dve.wait_ge(s["vhi"], s.had("vhi") + c + 1)
                    dve.tensor_tensor(v_lo[i][:, :], v_raw[i][:, :], v_hi[i][:, :].bitcast(F32), ALU.subtract)\
                       .then_inc(s["vlo"], 1)
                    dve.wait_ge(s["wsp"], s.had("wsp") + c + 1)
                    dve.tensor_tensor(w_lo[i][:, :], wgt[:, :], w_hi[i][:, :].bitcast(F32), ALU.subtract)\
                       .then_inc(s["wl"], 1)

                for c in range(NPRE):
                    if c == NPRE - 3:
                        u_split(NPRE, 0)
                    weigh(c, c % 2)
                with dve.Fori(NPRE // 2, NK // 2 - 1) as n:
                    for i in range(2):
                        cycle(2 * n + i, i)
                cycle(NK - 2, 0)
                cycle(NK - 1, 1, last=True)
                dve.wait_ge(s["v"], s.had("v") + NK)
                for tt in range(NT):
                    for hf in range(2):
                        xs = x[:, tt, 512 * hf:512 * hf + 512]
                        dve.tensor_tensor(xs, xs, ps[:, 4 + 2 * tt + hf, :], ALU.add).then_inc(s["xnew"], 1)

            dve.wait_ge(s_fss, NT)
            dve.tensor_scalar(msq[:, 0:NT], ssq[:, 0:NT], 1.0 / D, EPS, ALU.mult, ALU.add).then_inc(s_fms, 1)
            dve.wait_ge(s_frt, 1)
            link(dve.reciprocal(rstd[:, 0:NT], rms[:, 0:NT]))
            dve.wait_ge(s_gain, 16)
            for tt in range(NT):
                dve.scalar_tensor_tensor(out=y_out[:, tt, :], in0=x[:, tt, :], scalar=rstd[:, tt:tt + 1],
                                         in1=gain_f[:, :], op0=ALU.mult, op1=ALU.mult).then_inc(s_y, 1)


def constants():
    c = np.zeros((P, C_END + M_END), np.float32)
    c[:, C_ID:C_ID + P] = np.eye(P)
    c[:, C_IOTA:C_IOTA + P] = np.arange(P)
    c[:, C_START:C_START + 16] = STARTS
    c[:, C_DSTART:C_DSTART + 16] = PACK * np.diff([0] + STARTS)
    c[:, C_I16:C_I16 + 16] = np.arange(16)
    c[:, C_EPS:C_END] = EPS
    c[:, C_FREQ:C_EPS] = np.float32(10000.0) ** (-np.arange(0, MROPE, 2, dtype=np.float32) / np.float32(MROPE))
    q, k = np.arange(P)[:, None], np.arange(P)[None, :]
    m = c[:, C_END:]
    m[:, M_MLA + P:M_MLA + 2 * P] = np.where(k // CHUNK <= q // CHUNK, 0.0, NEG)
    m[:, M_FOX + P:M_FOX + 2 * P] = np.where(k <= q, 0.0, NEG)
    m[:, M_STRICT:M_STRICT + P] = 1.0
    m[:, M_STRICT + P:M_STRICT + 2 * P] = k < q
    m[:, M_TRIU:M_TRIU + P] = q <= k
    m[:, M_TRIU + P:M_TRIU + 2 * P] = 1.0
    return c


_INS = ["x", "positions", "norm1_g", "w_in", "mla_q_norm_g", "w_uq", "mla_kv_norm_g", "w_ukv", "fox_b_f",
        "w_o_mla", "w_o_sb", "w_o_fox", "b_gate", "w_out", "norm2_g", "peer_w_q", "peer_sub_keys",
        "peer_u", "peer_v", "final_norm_g"]


def kernel(**inputs):
    import concourse.bacc as bacc
    from concourse.bass_utils import run_bass_kernel_spmd

    nc = bacc.Bacc("TRN2", target_bir_lowering=False, num_devices=1)
    arrays, t_in = {}, {}
    for name in _INS + ["consts"]:
        a = constants() if name == "consts" else np.ascontiguousarray(inputs[name])
        arrays[f"in_{name}"] = a
        t_in[name] = nc.dram_tensor(f"in_{name}", a.shape, mybir.dt.from_np(a.dtype), kind="ExternalInput").ap()
    out = nc.dram_tensor("out_y", (1, SEQ, D), F32, kind="ExternalOutput").ap()
    build(nc, t_in, out)
    r = run_bass_kernel_spmd(nc, [arrays], core_ids=[0])
    return r.results[0]["out_y"]
```
